# Optimizing a Trainium2 kernel written in Bass

```python
import math
import jax, jax.numpy as jnp
from jax import lax
import numpy as np

D_MODEL = 1024
BATCH = 1
SEQ = 512
DEPTH = 1

N_MEM = 256
EPS = 1e-6
ATTN_HEADS = 8
ATTN_KV_HEADS = 2
ATTN_HEAD_DIM = 64
WINDOW = 128
ATTN_BLOCK = 128
REL_BUCKETS = 32
REL_MAX_DIST = 128
DN_HEADS = 8
DN_KEY_DIM = 64
DN_VALUE_DIM = 64
DN_CONV = 5
DN_CHUNK = 64
MEM_HEADS = 4
MEM_HEAD_DIM = 128
D_FF = 2816
FFN_CONV = 3
N_BRANCH = 3

ATTN_Q = ATTN_HEADS * ATTN_HEAD_DIM
ATTN_KV = ATTN_KV_HEADS * ATTN_HEAD_DIM
DN_QK = DN_HEADS * DN_KEY_DIM
DN_V = DN_HEADS * DN_VALUE_DIM
MEM_Q = MEM_HEADS * MEM_HEAD_DIM
IN_SPLITS = (ATTN_Q, ATTN_KV, ATTN_KV, DN_QK, DN_QK, DN_V, DN_V, 2 * DN_HEADS, 2 * DN_HEADS, MEM_Q, N_BRANCH * D_MODEL)
D_IN = sum(IN_SPLITS)

kernel_name = "hybrid_gated_swa_deltanet_memory_encoder"

def _split(t, sizes):
    idx = np.cumsum(sizes)[:-1].tolist()
    return jnp.split(t, idx, axis=-1)

def rmsnorm(x, g):
    x32 = x.astype(jnp.float32)
    y = x32 * lax.rsqrt(jnp.mean(x32 * x32, axis=-1, keepdims=True) + EPS)
    return (y * g.astype(jnp.float32)).astype(x.dtype)

def l2norm(x):
    x32 = x.astype(jnp.float32)
    return (x32 * lax.rsqrt(jnp.sum(x32 * x32, axis=-1, keepdims=True) + EPS)).astype(x.dtype)

def dwconv_centred(x, w):
    K = w.shape[0]
    p = K // 2
    S = x.shape[1]
    xp = jnp.pad(x, ((0, 0), (p, p), (0, 0)))
    y = xp[:, 0:S] * w[0]
    for j in range(1, K):
        y = y + xp[:, j:j + S] * w[j]
    return y

def _t5_buckets(rel):
    nb = REL_BUCKETS // 2
    max_exact = nb // 2
    ret = (rel > 0).astype(np.int32) * nb
    n = np.abs(rel)
    large = max_exact + (np.log(np.maximum(n, 1) / max_exact) / np.log(REL_MAX_DIST / max_exact) * (nb - max_exact)).astype(np.int32)
    large = np.minimum(large, nb - 1)
    return (ret + np.where(n < max_exact, n, large)).astype(np.int32)

def windowed_gqa(q, k, v, sink, rel_table):
    B, S, H, dh = q.shape
    Hkv = k.shape[2]
    G = H // Hkv
    T = ATTN_BLOCK
    nb = S // T
    t_idx = np.arange(T)[:, None]
    j_idx = np.arange(3 * T)[None, :]
    rel = j_idx - T - t_idx
    kpos = np.arange(nb)[:, None, None] * T - T + j_idx[None]
    valid = (np.abs(rel) <= WINDOW)[None] & (kpos >= 0) & (kpos < S)
    bias = jnp.transpose(rel_table[jnp.asarray(_t5_buckets(rel))], (2, 0, 1)).astype(jnp.float32)
    bias = bias.reshape(Hkv, G, T, 3 * T)

    qb = q.reshape(B, nb, T, Hkv, G, dh)

    def band(a):
        ap = jnp.pad(a, ((0, 0), (T, T), (0, 0), (0, 0))).reshape(B, nb + 2, T, Hkv, dh)
        return jnp.concatenate([ap[:, :-2], ap[:, 1:-1], ap[:, 2:]], axis=2)

    kb, vb = band(k), band(v)
    s = jnp.einsum('bnqkgd,bnjkd->bnkgqj', qb, kb).astype(jnp.float32) * (dh ** -0.5) + bias
    s = jnp.where(jnp.asarray(valid)[None, :, None, None], s, -jnp.inf)
    sk = sink.astype(jnp.float32).reshape(1, 1, Hkv, G, 1, 1)
    m = jnp.maximum(s.max(axis=-1, keepdims=True), sk)
    p = jnp.exp(s - m)
    p = p / (p.sum(axis=-1, keepdims=True) + jnp.exp(sk - m))
    o = jnp.einsum('bnkgqj,bnjkd->bnqkgd', p.astype(v.dtype), vb)
    return o.reshape(B, S, H * dh)

def gated_delta_rule(q, k, v, g, beta):
    B, S, H, dk = q.shape
    dv = v.shape[-1]
    C = DN_CHUNK
    n = S // C
    f32 = jnp.float32

    def ch(t):
        return t.astype(f32).reshape(B, n, C, H, -1).transpose(0, 3, 1, 2, 4)

    q, k, v = ch(q), ch(k), ch(v)
    g = g.astype(f32).reshape(B, n, C, H).transpose(0, 3, 1, 2)
    beta = beta.astype(f32).reshape(B, n, C, H).transpose(0, 3, 1, 2)
    gc = jnp.cumsum(g, axis=-1)
    lower = jnp.asarray(np.tril(np.ones((C, C), bool)))
    strict = jnp.asarray(np.tril(np.ones((C, C), bool), -1))
    decay = jnp.exp(jnp.where(lower, gc[..., :, None] - gc[..., None, :], -jnp.inf))
    kb = k * beta[..., None]
    L = jnp.where(strict, jnp.einsum('bhncd,bhnmd->bhncm', kb, k) * decay, 0.0)
    A = L + jnp.eye(C, dtype=f32)
    rhs = jnp.concatenate([v * beta[..., None], kb * jnp.exp(gc)[..., None]], axis=-1)
    sol = lax.linalg.triangular_solve(A, rhs, left_side=True, lower=True, unit_diagonal=True)
    u, w = sol[..., :dv], sol[..., dv:]
    qk = jnp.einsum('bhncd,bhnmd->bhncm', q, k) * decay
    g_last = gc[..., -1]
    q_in = q * jnp.exp(gc)[..., None]
    k_up = k * jnp.exp(g_last[..., None] - gc)[..., None]

    def step(state, inp):
        qi, ki, ui, wi, qki, gl = inp
        v_new = ui - jnp.einsum('bhcd,bhde->bhce', wi, state)
        o = jnp.einsum('bhcd,bhde->bhce', qi, state) + jnp.einsum('bhcm,bhme->bhce', qki, v_new)
        state = state * jnp.exp(gl)[..., None, None] + jnp.einsum('bhcd,bhce->bhde', ki, v_new)
        return state, o

    xs = (jnp.moveaxis(q_in, 2, 0), jnp.moveaxis(k_up, 2, 0), jnp.moveaxis(u, 2, 0),
          jnp.moveaxis(w, 2, 0), jnp.moveaxis(qk, 2, 0), jnp.moveaxis(g_last, 2, 0))
    state0 = jnp.zeros((B, H, dk, dv), f32)
    _, o = lax.scan(step, state0, xs)
    return o.transpose(1, 0, 3, 2, 4).reshape(B, S, H, dv)

def deltanet_branch(dq, dk, dv, dz, db, da, conv_w, a_log, dt_bias, out_g):
    B, S, _ = dq.shape
    f32 = jnp.float32
    qkv = jax.nn.silu(dwconv_centred(jnp.concatenate([dq, dk, dv], axis=-1), conv_w))
    q, k, v = _split(qkv, (DN_QK, DN_QK, DN_V))
    q = l2norm(q.reshape(B, S, DN_HEADS, DN_KEY_DIM)) * (DN_KEY_DIM ** -0.5)
    k = l2norm(k.reshape(B, S, DN_HEADS, DN_KEY_DIM))
    v = v.reshape(B, S, DN_HEADS, DN_VALUE_DIM)
    beta = jax.nn.sigmoid(db.astype(f32)).reshape(B, S, 2, DN_HEADS)
    g = -jnp.exp(a_log.astype(f32)) * jax.nn.softplus(da.astype(f32).reshape(B, S, 2, DN_HEADS) + dt_bias.astype(f32))
    o_fwd = gated_delta_rule(q, k, v, g[:, :, 0], beta[:, :, 0])
    o_bwd = jnp.flip(gated_delta_rule(jnp.flip(q, 1), jnp.flip(k, 1), jnp.flip(v, 1),
                                      jnp.flip(g[:, :, 1], 1), jnp.flip(beta[:, :, 1], 1)), 1)
    z = dz.reshape(B, S, DN_HEADS, DN_VALUE_DIM).astype(f32)
    o = rmsnorm(o_fwd + o_bwd, out_g) * jax.nn.silu(z)
    return o.reshape(B, S, DN_V).astype(dq.dtype)

def memory_cross_attention(mq, mem_n, w_kv, q_g, k_g):
    B, S, _ = mq.shape
    M = mem_n.shape[1]
    k, v = jnp.split(mem_n @ w_kv, 2, axis=-1)
    q = rmsnorm(mq.reshape(B, S, MEM_HEADS, MEM_HEAD_DIM), q_g)
    k = rmsnorm(k.reshape(B, M, MEM_HEADS, MEM_HEAD_DIM), k_g)
    v = v.reshape(B, M, MEM_HEADS, MEM_HEAD_DIM)
    s = jnp.einsum('bshd,bmhd->bhsm', q, k).astype(jnp.float32) * (MEM_HEAD_DIM ** -0.5)
    p = jax.nn.softmax(s, axis=-1).astype(v.dtype)
    return jnp.einsum('bhsm,bmhd->bshd', p, v).reshape(B, S, MEM_Q)

def setup_inputs(seed: int = 0) -> dict:
    key = jax.random.key(seed)
    ks = jax.random.split(key, 26)
    f32 = jnp.float32
    L = DEPTH

    def nrm(k, shape, scale):
        return jax.random.normal(k, shape, f32) * scale

    def gain(k, shape):
        return 1.0 + 0.05 * jax.random.normal(k, shape, f32)

    dt = jnp.exp(jax.random.uniform(ks[9], (L, 2, DN_HEADS), f32, math.log(1e-3), math.log(1e-1)))
    return {
        "x": nrm(ks[0], (BATCH, SEQ, D_MODEL), 1.0),
        "mem": nrm(ks[1], (BATCH, N_MEM, D_MODEL), 1.0),
        "rel_bias_table": nrm(ks[2], (REL_BUCKETS, ATTN_HEADS), 0.5),
        "norm_mix_g": gain(ks[3], (L, D_MODEL)),
        "w_in": nrm(ks[4], (L, D_MODEL, D_IN), D_MODEL ** -0.5),
        "attn_q_norm_g": gain(ks[5], (L, ATTN_HEAD_DIM)),
        "attn_k_norm_g": gain(ks[6], (L, ATTN_HEAD_DIM)),
        "attn_sink": nrm(ks[7], (L, ATTN_HEADS), 1.0),
        "dn_conv_w": nrm(ks[8], (L, DN_CONV, 2 * DN_QK + DN_V), DN_CONV ** -0.5),
        "dn_a_log": jnp.log(jax.random.uniform(ks[10], (L, 2, DN_HEADS), f32, 1.0, 16.0)),
        "dn_dt_bias": dt + jnp.log(-jnp.expm1(-dt)),
        "dn_out_norm_g": gain(ks[11], (L, DN_VALUE_DIM)),
        "mem_norm_g": gain(ks[12], (L, D_MODEL)),
        "mem_w_kv": nrm(ks[13], (L, D_MODEL, 2 * MEM_Q), D_MODEL ** -0.5),
        "mem_q_norm_g": gain(ks[14], (L, MEM_HEAD_DIM)),
        "mem_k_norm_g": gain(ks[15], (L, MEM_HEAD_DIM)),
        "w_br_attn": nrm(ks[16], (L, ATTN_Q, D_MODEL), ATTN_Q ** -0.5),
        "w_br_dn": nrm(ks[17], (L, DN_V, D_MODEL), DN_V ** -0.5),
        "w_br_mem": nrm(ks[18], (L, MEM_Q, D_MODEL), MEM_Q ** -0.5),
        "w_out": nrm(ks[19], (L, D_MODEL, D_MODEL), D_MODEL ** -0.5),
        "norm_ffn_g": gain(ks[20], (L, D_MODEL)),
        "ffn_w_up": nrm(ks[21], (L, D_MODEL, 2 * D_FF), D_MODEL ** -0.5),
        "ffn_conv_w": nrm(ks[22], (L, FFN_CONV, 2 * D_FF), FFN_CONV ** -0.5),
        "ffn_conv_b": nrm(ks[23], (L, 2 * D_FF), 0.01),
        "ffn_w_down": nrm(ks[24], (L, D_FF, D_MODEL), D_FF ** -0.5),
    }

def reference(x, mem, rel_bias_table, norm_mix_g, w_in, attn_q_norm_g, attn_k_norm_g, attn_sink,
              dn_conv_w, dn_a_log, dn_dt_bias, dn_out_norm_g, mem_norm_g, mem_w_kv, mem_q_norm_g,
              mem_k_norm_g, w_br_attn, w_br_dn, w_br_mem, w_out, norm_ffn_g, ffn_w_up, ffn_conv_w,
              ffn_conv_b, ffn_w_down):
    B, S, _ = x.shape
    for l in range(DEPTH):
        h = rmsnorm(x, norm_mix_g[l])
        aq, ak, av, dq, dk, dv, dz, db, da, mq, gates = _split(h @ w_in[l], IN_SPLITS)
        y_attn = windowed_gqa(
            rmsnorm(aq.reshape(B, S, ATTN_HEADS, ATTN_HEAD_DIM), attn_q_norm_g[l]),
            rmsnorm(ak.reshape(B, S, ATTN_KV_HEADS, ATTN_HEAD_DIM), attn_k_norm_g[l]),
            av.reshape(B, S, ATTN_KV_HEADS, ATTN_HEAD_DIM),
            attn_sink[l], rel_bias_table)
        y_dn = deltanet_branch(dq, dk, dv, dz, db, da, dn_conv_w[l], dn_a_log[l], dn_dt_bias[l], dn_out_norm_g[l])
        y_mem = memory_cross_attention(mq, rmsnorm(mem, mem_norm_g[l]), mem_w_kv[l], mem_q_norm_g[l], mem_k_norm_g[l])
        g_attn, g_dn, g_mem = jnp.split(jax.nn.sigmoid(gates), N_BRANCH, axis=-1)
        merged = (g_attn * (y_attn @ w_br_attn[l]) + g_dn * (y_dn @ w_br_dn[l])
                  + g_mem * (y_mem @ w_br_mem[l]))
        x = x + merged @ w_out[l]
        h = rmsnorm(x, norm_ffn_g[l])
        u = dwconv_centred(h @ ffn_w_up[l], ffn_conv_w[l]) + ffn_conv_b[l]
        u_gate, u_val = jnp.split(u, 2, axis=-1)
        x = x + (jax.nn.silu(u_gate) * u_val) @ ffn_w_down[l]
    return x


_drawn_inputs = setup_inputs


def setup_inputs(seed=0):
    import zlib

    import numpy as np

    out = dict(_drawn_inputs(seed))
    spreads = {}
    factors = {'attn_q_norm_g': 8.0,
     'attn_k_norm_g': 8.0,
     'attn_sink': 8.0,
     'dn_out_norm_g': 15.179,
     'mem_norm_g': 8.0,
     'mem_q_norm_g': 8.0,
     'mem_k_norm_g': 8.0,
     'ffn_conv_b': 30.087,
     'rel_bias_table': 8.0,
     'norm_ffn_g': 6.062}
    for name, (base, spread) in spreads.items():
        noise = np.random.default_rng([zlib.crc32(name.encode()), seed]).standard_normal(out[name].shape)
        drawn = base * np.exp(spread * noise) if base else spread * noise
        out[name] = __import__('jax').numpy.asarray(drawn.astype(out[name].dtype))
    for name, factor in factors.items():
        out[name] = (out[name] * factor).astype(out[name].dtype)
    return out
```

```python
import numpy as np
import concourse.bass as bass
from concourse import mybir
from contextlib import ExitStack

D, SEQ, P = 1024, 512, 128
KT = D // P
RT = SEQ // P
N_MEM = 256
MT = N_MEM // P
D_FF = 2816
FT = D_FF // P
EPS = 1e-6
AH, AKV, AD = 8, 2, 64
WINDOW, BUCKETS, MAX_DIST = 128, 32, 128
DH, DK = 8, 64
DN_TAPS, CHUNK = 5, 64
NSLOT = SEQ // CHUNK
HB = 4
MH, MD = 4, 128
FFN_TAPS = 3
ATTN_Q, ATTN_KV, DN_W, MEM_Q = AH * AD, AKV * AD, DH * DK, MH * MD
C_AQ = 0
C_AKV = C_AQ + ATTN_Q
C_DN = C_AKV + 2 * ATTN_KV
C_DZ = C_DN + 3 * DN_W
C_BA = C_DZ + DN_W
C_MQ = C_BA + 4 * DH
C_GATE = C_MQ + MEM_Q
D_IN = C_GATE + 3 * D
LEVELS = 6
NEG = -1e30
BIAS_N = 3 * P + P - 1
RAW_N, HL_N, UNIT = 3, 3, 1024

CONST_COLS = {}


def shape_constants():
    n = np.arange(P)
    same = (n[:, None] // CHUNK) == (n[None, :] // CHUNK)
    half = n // CHUNK
    c64 = np.arange(CHUNK)
    within = n % CHUNK
    parts = {"exchange": np.eye(P)[::-1], "pick": None, "ident": np.eye(P)}
    for p in range(2):
        fwd = (half == p)[:, None]
        parts[f"after{p}"] = same * np.where(fwd, n[:, None] > n[None, :], n[:, None] < n[None, :])
        parts[f"upto{p}"] = same * np.where(fwd, n[:, None] <= n[None, :], n[:, None] >= n[None, :])
    for p in range(2):
        fwd = (half == p)[:, None]
        parts[f"incl{p}"] = np.where(fwd, within[:, None] <= c64[None], within[:, None] >= c64[None])
        parts[f"strict{p}"] = np.where(fwd, within[:, None] < c64[None], within[:, None] > c64[None])
    for l in range(LEVELS):
        parts[f"pair{l}"] = ((within[:, None] >> l) ^ (c64[None] >> l)) == 1
    parts["ident64"] = within[:, None] == c64[None]
    parts["ones64"] = np.ones((P, CHUNK))
    rel = np.arange(BIAS_N) - (2 * P - 1)
    nb = BUCKETS // 2
    exact = nb // 2
    dist = np.abs(rel)
    large = exact + (np.log(np.maximum(dist, 1) / exact) / np.log(MAX_DIST / exact) * (nb - exact)).astype(np.int32)
    bucket = (rel > 0) * nb + np.where(dist < exact, dist, np.minimum(large, nb - 1))
    pick = np.zeros((P, BIAS_N + 1))
    valid = dist <= WINDOW
    pick[bucket[valid], np.arange(BIAS_N)[valid]] = 1.0
    pick[BUCKETS, :BIAS_N] = ~valid
    parts["pick"] = pick
    at = 0
    for k, v in parts.items():
        CONST_COLS[k] = (at, v.shape[1])
        at += v.shape[1]
    return np.concatenate([np.asarray(v, np.float32) for v in parts.values()], axis=1)


CONSTS = shape_constants()
EARLY = ("exchange", "pick")


def walk_order():
    order = [("small",), ("xnorm",)]
    order += [("xT", k) for k in range(KT)]
    order += [("mT", k) for k in range(KT)] + [("bias",)]
    order += [("dnproj", c) for c in range(12)]
    order += [("baproj",), ("zproj",), ("gbeta",), ("aqproj",), ("akvproj",), ("anorm",)]
    order += [("dnnat", rt, j) for rt in range(RT) for j in range(3)] + [("aT",)]
    order += [("attn", n, g) for n in range(RT) for g in range(AKV)]
    order += [("mqproj",), ("mkvproj", 0), ("mkvproj", 1), ("mqnorm",), ("mqT",)]
    order += [("mscore", rt) for rt in range(RT)] + [("mout", h) for h in range(MH)]
    order += [("dnnorm",), ("dnT",)]
    fillers = [("branch", b, c) for b in (0, 1) for c in range(KT)]
    fillers.reverse()
    prep = lambda s, hb: [("decay", s, hb)] + [("level", s, hb, l) for l in range(LEVELS)] + [("uw", s, hb)]
    scan = lambda s, hb: [("scanv", s, hb), ("scans", s, hb)]
    for s in range(NSLOT + 1):
        lanes = []
        if s < NSLOT:
            lanes += [prep(s, 0), prep(s, 1)]
        if s > 0:
            lanes += [scan(s - 1, 0), scan(s - 1, 1)]
        for i in range(max(map(len, lanes))):
            for lane in lanes:
                if i < len(lane):
                    order.append(lane[i])
            if i in (2, 5) and fillers:
                order.append(fillers.pop())
    order += fillers[::-1]
    order += [("osum",), ("oT",)]
    order += [("branch", 2, c) for c in range(KT)]
    order += [("wout", 0), ("wout", 1), ("x2norm",)]
    order += [("h2T", k) for k in range(KT)]
    order += [("up", c) for c in range(FT)]
    order += [("down", 0), ("down", 1)]
    return order


ORDER = walk_order()
G_FILLS = {"dnproj": 1, "baproj": RT, "zproj": RT, "aqproj": RT, "akvproj": RT, "mqproj": RT,
           "mkvproj": MT, "branch": 2, "wout": RT, "up": 2, "down": RT}
D_FILLS = {"small": 3, "bias": 1 + AH, "xT": 1, "mT": 1, "gbeta": 1, "aT": 4 + AKV, "dnnat": 1,
           "mqT": MH + MH // 2, "mscore": 2, "mout": 3, "dnT": 8, "decay": 2, "uw": 1,
           "scanv": 1, "scans": 1, "oT": 4, "h2T": 1}


def d_fills(st):
    if st[0] == "level":
        return 1 if st[1 + 2] == 0 else 2
    if st[0] == "attn":
        return 4 + len(key_blocks(st[1])) + 1
    return D_FILLS.get(st[0], 0)


def key_blocks(n):
    return [kb for kb in range(3) if 0 <= n - 1 + kb < RT]


def stage_units(st):
    kind = st[0]
    if kind == "dnproj":
        return [("w_in", 0, KT, C_DN + st[1] * P, P)]
    if kind == "baproj":
        return [("w_in", 0, KT, C_BA, 4 * DH)]
    if kind in ("zproj", "aqproj", "mqproj"):
        c0 = {"zproj": C_DZ, "aqproj": C_AQ, "mqproj": C_MQ}[kind]
        return [("w_in", 2 * i, 2, c0, 512) for i in range(KT // 2)]
    if kind == "akvproj":
        return [("w_in", 4 * i, 4, C_AKV, 2 * ATTN_KV) for i in range(KT // 4)]
    if kind == "mkvproj":
        return [("mem_w_kv", 2 * i, 2, 512 * st[1], 512) for i in range(KT // 2)]
    if kind == "branch":
        b, c = st[1:]
        name = ("w_br_attn", "w_br_mem", "w_br_dn")[b]
        gate = (0, 2, 1)[b]
        pair = [(name, 0, 4, c * P, 2 * P)] if c % 2 == 0 else []
        return pair + [("w_in", 0, KT, C_GATE + gate * D + c * P, P)]
    if kind == "wout":
        return [("w_out", 2 * i, 2, 512 * st[1], 512) for i in range(KT // 2)]
    if kind == "up":
        return [("ffn_w_up", 0, KT, st[1] * P, P), ("ffn_w_up", 0, KT, D_FF + st[1] * P, P)]
    if kind == "down":
        return [("ffn_w_down", 2 * i, 2, 512 * st[1], 512) for i in range(FT // 2)]
    return []


G_FIRST, D_FIRST, U_FIRST, NTH, UNITS = {}, {}, {}, {}, []
LAST_USE = []
G_AT, D_AT = 0, 0
for PLACE, STAGE in enumerate(ORDER):
    G_FIRST[STAGE], D_FIRST[STAGE], U_FIRST[STAGE] = G_AT, D_AT, len(UNITS)
    NTH[STAGE] = sum(o[0] == STAGE[0] for o in ORDER[:PLACE])
    G_AT += G_FILLS.get(STAGE[0], 0)
    D_AT += d_fills(STAGE)
    for UNIT_OF in stage_units(STAGE):
        UNITS.append(UNIT_OF)
        LAST_USE.append(ORDER.index(STAGE[:2] + (STAGE[2] + 1,)) if UNIT_OF[0].startswith("w_br") else PLACE)

UNIT_DONE, USED_AT = [], 0
for NUMBER, PLACE in enumerate(LAST_USE):
    STAGE = ORDER[PLACE]
    IN_STAGE = len(stage_units(STAGE))
    FIRST = G_FIRST[STAGE]
    if STAGE[0] == "dnproj":
        UNIT_DONE.append(("g_full", FIRST + 1))
    elif STAGE[0] in ("branch", "up"):
        IS_SECOND = NUMBER == U_FIRST[STAGE] + IN_STAGE - 1
        UNIT_DONE.append(("g_full", FIRST + (2 if IS_SECOND else 1)))
    elif NUMBER == U_FIRST[STAGE] + IN_STAGE - 1:
        UNIT_DONE.append(("g_full", FIRST + G_FILLS[STAGE[0]]))
    else:
        USED_AT += 1
        UNIT_DONE.append(("unit_used", USED_AT))

SPLITS_AT = {PLACE: [] for PLACE in range(-1, len(ORDER))}
SPLIT_PLACE = -1
for NUMBER in range(len(UNITS)):
    if NUMBER >= HL_N:
        SPLIT_PLACE = max(SPLIT_PLACE, LAST_USE[NUMBER - HL_N])
    SPLITS_AT[SPLIT_PLACE].append(NUMBER)


def encoder_layer(nc, W, out, stop=None, dump=None):
    F, R = mybir.dt.float32, mybir.dt.float32r
    ALU, ACT, AX = mybir.AluOpType, mybir.ActivationFunctionType, mybir.AxisListType
    X = AX.X
    order = ORDER if stop is None else ORDER[:stop]

    ctx = ExitStack()
    with ctx:
        base = (nc.sbuf_base + 31) // 32 * 32
        end = nc.sbuf_usable_end
        at_end = [0]

        def place(name, shape, offset, dt=F):
            size = int(np.prod(shape[1:])) * 4
            at_end[0] = (offset + size + 31) // 32 * 32
            assert base + offset + size <= end, (name, base + offset + size, end)
            return nc.alloc_sbuf_tensor_at(name, shape, dt, offset=base + offset)

        def after(name, shape, dt=F):
            return place(name, shape, at_end[0], dt)

        def signal(name):
            return ctx.enter_context(nc.semaphore(name))

        kept = [k for k in CONST_COLS if k not in EARLY]
        n_const = sum(CONST_COLS[k][1] for k in kept)
        n_late = sum(CONST_COLS[k][1] for k in EARLY)
        cst = place("cst", [P, n_const], 0)
        raw = after("raw", [P, RAW_N, UNIT])
        w_hi = after("w_hi", [P, HL_N, UNIT], R)
        w_lo = after("w_lo", [P, HL_N, UNIT], R)
        pcol = after("pcol", [P, 96])
        fcol = after("fcol", [P, 4 * 2 * FT])
        rowp = after("rowp", [P, 2 * 16 + AH])
        st_x = after("st_x", [P, RT + MT])
        st_a = after("st_a", [P, RT, 10])
        st_m = after("st_m", [P, 24])
        st_d = after("st_d", [P, 2, RT, DH])
        st_o = after("st_o", [P, RT * DH])
        st_s = after("st_s", [P, 8, 4])
        ba = after("ba", [P, RT, 32])
        sp = after("sp", [P, 2, RT, 16])
        ealog = after("ealog", [P, 16])
        g_slot = after("g_slot", [P, NSLOT, DH])
        b_slot = after("b_slot", [P, NSLOT, DH])
        e_slot = after("e_slot", [P, 192])
        tg = after("tg", [P, SEQ])
        hT_hi = after("hT_hi", [P, KT, SEQ], R)
        hT_lo = after("hT_lo", [P, KT, SEQ], R)
        m0 = at_end[0]
        merged = after("merged", [P, KT, SEQ])
        y0 = at_end[0]
        yA_hi = after("yA_hi", [P, 4, SEQ], R)
        yA_lo = after("yA_lo", [P, 4, SEQ], R)
        yM_hi = after("yM_hi", [P, 4, SEQ], R)
        yM_lo = after("yM_lo", [P, 4, SEQ], R)
        a0 = at_end[0]
        xt = place("xt", [P, RT, D], m0)
        sq = place("sq", [P, RT, D], m0)
        brev = place("brev", [P, AH, 3 * P], y0)
        memT_hi = place("memT_hi", [P, KT, N_MEM], y0 + 16384, R)
        memT_lo = after("memT_lo", [P, KT, N_MEM], R)
        dn_nat = place("dn_nat", [P, 3, RT, DN_W], a0)
        zs = after("zs", [P, RT, DN_W])
        a1 = at_end[0]
        mx = place("mx", [P, MT, D], a1)
        scr = after("scr", [P, D])
        rows = after("rows", [P, 3, P])
        late = after("late", [P, n_late])
        btab = after("btab", [P, AH])
        bT = after("bT", [P, BIAS_N + 1])
        dnc = place("dnc", [P, 12, SEQ], a1)
        bias = after("bias", [P, AH, 3 * P])
        anat = after("anat", [P, RT, ATTN_Q + 2 * ATTN_KV])
        aqT = place("aqT", [P, 4, SEQ], a1)
        akT = after("akT", [P, AKV, SEQ])
        sc = after("sc", [P, 4, 3 * P])
        pT = after("pT", [P, 3, 4, P])
        mqn = place("mqn", [P, RT, MEM_Q], a1)
        mkv = after("mkv", [P, MT, 2 * MEM_Q])
        mqT = after("mqT", [P, MH, SEQ])
        mkT = after("mkT", [P, MH, N_MEM])
        msc = after("msc", [P, RT, MH, N_MEM])
        mpT = place("mpT", [P, MT, SEQ], a1)
        qkT = place("qkT", [P, 8, SEQ], a1)
        o_nat = after("o_nat", [P, RT, DN_W])
        S = after("S", [P, 2, 2, 2, DK])
        dec = after("dec", [P, 2, HB, CHUNK])
        nn = after("nn", [P, 2, HB, CHUNK])
        nm = after("nm", [P, 2, 2, HB, CHUNK])
        yx = after("yx", [P, 2, 2, HB, CHUNK])
        wx = after("wx", [P, 2, HB, CHUNK])
        kk = after("kk", [P, HB, CHUNK])
        vn = after("vn", [P, 2, HB, CHUNK])
        at_ = after("at_", [P, 4, HB, CHUNK])
        uu = place("uu", [P, 2, HB, CHUNK], a0)
        wt = after("wt", [P, 2, 2, 2, CHUNK])
        ku = after("ku", [P, 2, HB, CHUNK])
        o1 = after("o1", [P, 2, HB, CHUNK])
        xr = place("xr", [P, RT, D], a0)
        xn = after("xn", [P, RT, D])
        m_hi = place("m_hi", [P, KT, SEQ], a1, R)
        m_lo = after("m_lo", [P, KT, SEQ], R)
        x2 = place("x2", [P, RT, D], m0)
        scr2 = place("scr2", [P, D], a1)
        act_hi = place("act_hi", [P, FT, SEQ], y0, R)
        act_lo = after("act_lo", [P, FT, SEQ], R)
        u_gv = after("u_gv", [P, 2, 2, SEQ])

        gb = [ctx.enter_context(nc.psum_tensor(f"g_bank{i}", [P, 512], F)) for i in range(4)]
        db = [ctx.enter_context(nc.psum_tensor(f"d_bank{i}", [P, 512], F)) for i in range(4)]
        bias_rows = nc.dram_tensor("bias_rows", (AH, BIAS_N + 1), F)

        def const(name, rows=slice(0, P)):
            if name in EARLY:
                first = CONST_COLS[EARLY[0]][0]
                return late[rows, CONST_COLS[name][0] - first:CONST_COLS[name][0] - first + CONST_COLS[name][1]]
            first = CONST_COLS[kept[0]][0]
            return cst[rows, CONST_COLS[name][0] - first:CONST_COLS[name][0] - first + CONST_COLS[name][1]]

        g_full, d_full = signal("g_full"), signal("d_full")
        g_free = [signal(f"g_free{i}") for i in range(4)]
        d_free = [signal(f"d_free{i}") for i in range(4)]
        raw_loaded = [signal(f"raw_loaded{i}") for i in range(RAW_N)]
        hi_made, lo_made, unit_used = signal("hi_made"), signal("lo_made"), signal("unit_used")
        act_step, dve_step, pool_step, pe_step = (signal(n) for n in ("act_step", "dve_step", "pool_step", "pe_step"))
        consts_in, rows_in, x_in, mem_in = signal("consts_in"), signal("rows_in"), signal("x_in"), signal("mem_in")
        table_in, bias_out, bias_in, xr_in = signal("table_in"), signal("bias_out"), signal("bias_in"), signal("xr_in")
        stored = signal("stored")
        table_ready, ss_made, sqrt_made, var_made = (signal(n) for n in ("table_ready", "ss_made", "sqrt_made", "var_made"))
        x_scaled, part_hi, tap_made = signal("x_scaled"), signal("part_hi"), signal("tap_made")
        dn_silu, sp_made, softplus_made, beta_made = (signal(n) for n in ("dn_silu", "sp_made", "softplus_made", "beta_made"))
        slots_made, decays_made, a_scaled = signal("slots_made"), signal("decays_made"), signal("a_scaled")
        attn_max, attn_exp, attn_p = signal("attn_max"), signal("attn_exp"), signal("attn_p")
        mq_scaled, mmax, mexp, mp = signal("mq_scaled"), signal("mmax"), signal("mexp"), signal("mp")
        dn_scaled, state_zero = signal("dn_scaled"), signal("state_zero")
        b_made, em_made, nm_made, kk_made = signal("b_made"), signal("em_made"), signal("nm_made"), signal("kk_made")
        vn_made, o_added, o_scaled = signal("vn_made"), signal("o_added"), signal("o_scaled")
        gate_used, mhi_made, m_split = (signal(n) for n in ("gate_used", "mhi_made", "m_split"))
        x2_scaled, ua_made, silu_made, glu_made, fhi_made, f_split = (signal(n) for n in ("x2_scaled", "ua_made", "silu_made", "glu_made", "fhi_made", "f_split"))
        SIG = {"g_full": g_full, "unit_used": unit_used}
        PC_MIX, PC_FFN, PC_MEM = DN_TAPS * 12, DN_TAPS * 12 + KT, DN_TAPS * 12 + 2 * KT
        PC_MQ, PC_MK, PC_AQ, PC_AK, PC_DO = (PC_MEM + KT + i for i in range(5))
        N_PC = PC_DO + 1
        FH = 2 * FT
        len_units = sum(len(stage_units(o)) for o in order)

        def level_no(s, hb, l):
            return NTH[("level", s, hb, l)]

        def f_level(s, hb, l):
            return D_FIRST[("level", s, hb, l)] + d_fills(("level", s, hb, l)) - 1

        NORM = {"xnorm": 0, "anorm": 1, "mqnorm": 2, "dnnorm": 3, "osum": 4, "x2norm": 5}
        EARLY_SQUARES = RT + MT

        def heads(ap):
            return ap.rearrange("p (h d) -> p h d", d=64)

        def halves(s):
            return [(hf, 0 if hf == s % 2 else 1, s if hf == s % 2 else NSLOT - 1 - s) for hf in range(2)]

        def decay_of(kind, s, hb, rows=slice(0, P)):
            v = e_slot[rows, 64:192].rearrange("p (k q i h) -> p k q i h", k=2, q=2, i=4)
            return v[:, kind, s % 2, s // 2, HB * hb:HB * hb + HB]

        def unit_view(ring, u):
            _, _, nk, _, nc_ = UNITS[u]
            n = RAW_N if ring is raw else HL_N
            return ring[:, u % n, 0:nk * nc_].rearrange("p (k c) -> p k c", k=nk)

        block = ctx.enter_context(nc.Block())

        @block.sync
        def _(sync):
            sync.dma_start(xt[:], W["x"][0].rearrange("(t p) d -> p t d", p=P)).then_inc(x_in, 16)
            sync.dma_start(late[:], W["consts"][:, 0:n_late]).then_inc(consts_in, 16)
            sync.dma_start(cst[:], W["consts"][:, n_late:]).then_inc(consts_in, 16)
            at = 0
            for src in ("dn_conv_w", "norm_mix_g", "norm_ffn_g", "mem_norm_g", "mem_q_norm_g", "mem_k_norm_g"):
                v = W[src].rearrange("l k (c p) -> (l k c) p", p=P) if src == "dn_conv_w" else W[src].rearrange("l (c p) -> (l c) p", p=P)
                sync.dma_start(rows[at:at + v.shape[0], 0, :], v).then_inc(rows_in, 16)
                at += v.shape[0]
            for src in ("attn_q_norm_g", "attn_k_norm_g", "dn_out_norm_g"):
                for side in range(2):
                    sync.dma_start(rows[at:at + 1, 0, 64 * side:64 * side + 64], W[src]).then_inc(rows_in, 16)
                at += 1
            fw = W["ffn_conv_w"].rearrange("l k (c p) -> (l k c) p", p=P)
            fb = W["ffn_conv_b"].rearrange("l (c p) -> (l c) p", p=P)
            sync.dma_start(rows[0:2 * FH, 1, :], fw[0:2 * FH, :]).then_inc(rows_in, 16)
            sync.dma_start(rows[0:FH, 2, :], fw[2 * FH:3 * FH, :]).then_inc(rows_in, 16)
            sync.dma_start(rows[FH:2 * FH, 2, :], fb).then_inc(rows_in, 16)
            small = (("dn_a_log", 0, 16, "l t h -> l (t h)"), ("dn_dt_bias", 16, 16, "l t h -> l (t h)"), ("attn_sink", 32, AH, None))
            for src, c0, n, how in small:
                v = W[src].rearrange(how) if how else W[src]
                sync.dma_start(rowp[:, c0:c0 + n], v.to_broadcast([P, n])).then_inc(rows_in, 16)
            sync.dma_start(btab[0:BUCKETS, :], W["rel_bias_table"]).then_inc(table_in, 16)
            sync.dma_start(mx[:], W["mem"][0].rearrange("(t p) d -> p t d", p=P)).then_inc(mem_in, 16)

            def load_units(first, last):
                for u in range(first, last):
                    name, k0, nk, c0, n = UNITS[u]
                    if u >= RAW_N:
                        sync.wait_ge(lo_made, u - RAW_N + 1)
                    src = W[name][0, k0 * P:(k0 + nk) * P, c0:c0 + n].rearrange("(k p) c -> p k c", p=P)
                    sync.dma_start(unit_view(raw, u), src).then_inc(raw_loaded[u % RAW_N], 16)

            done = min(RAW_N, len_units)
            load_units(0, done)
            for i, st in enumerate(order):
                if st[0] == "bias":
                    f = D_FIRST[st]
                    sync.wait_ge(d_free[f % 4], f // 4 + 1)
                    sync.dma_start(bias_rows.ap(), bT[0:AH, :]).then_inc(bias_out, 16)
                    sync.wait_ge(bias_out, 16)
                    band = bass.AP(tensor=bias_rows, offset=0, ap=[[1, P], [BIAS_N + 1, AH], [1, 3 * P]])
                    sync.dma_start(brev[:], band).then_inc(bias_in, 16)
                if st == ("wout", 0):
                    f = D_FIRST[("oT",)] + 3
                    sync.wait_ge(d_free[f % 4], f // 4 + 1)
                    sync.dma_start(xr[:], W["x"][0].rearrange("(t p) d -> p t d", p=P)).then_inc(xr_in, 16)
                ahead = min(len_units, U_FIRST[st] + len(stage_units(st)) + RAW_N)
                if ahead > done:
                    load_units(done, ahead)
                    done = ahead
                if st[0] == "down":
                    for rt in range(RT):
                        f = G_FIRST[st] + rt
                        sync.wait_ge(g_free[f % 4], f // 4 + 1)
                        c0 = 512 * st[1]
                        sync.dma_start(out[0, rt * P:(rt + 1) * P, c0:c0 + 512], x2[:, rt, c0:c0 + 512]).then_inc(stored, 16)
                    if st[1] == 1:
                        sync.wait_ge(stored, 16 * 2 * RT)

        @block.tensor
        def _(pe):
            mm = nc.tensor.matmul
            steps = [0]

            def tiles_apart(ins):
                steps[0] += 1
                ins.then_inc(pe_step, 1)
                pe.wait_ge(pe_step, steps[0])

            def d_claim(f):
                if f >= 4:
                    pe.wait_ge(d_free[f % 4], f // 4)
                return db[f % 4]

            def g_claim(f):
                if f >= 4:
                    pe.wait_ge(g_free[f % 4], f // 4)
                return gb[f % 4]

            def evacuated(f):
                pe.wait_ge(d_free[f % 4], f // 4 + 1)

            def arrived(u):
                pe.wait_ge(hi_made, u + 1)
                pe.wait_ge(lo_made, u + 1)

            def transposes(f, sources, width=P):
                bank = d_claim(f)
                for i, src in enumerate(sources):
                    last = nc.tensor.transpose(bank[:, i * width:(i + 1) * width], src, const("ident"))
                last.then_inc(d_full, 1)

            def columns_product(f, u, col, act_hi_, act_lo_, nk, width=SEQ):
                bank = g_claim(f)
                arrived(u)
                hi, lo = unit_view(w_hi, u), unit_view(w_lo, u)
                for k in range(nk):
                    for w, a in ((hi, act_hi_), (hi, act_lo_), (lo, act_hi_)):
                        last = mm(bank[:, 0:width], w[:, k, col:col + P], a[:, k, :], start=(k == 0 and w is hi and a is act_hi_),
                                  stop=(k == nk - 1 and w is lo))
                last.then_inc(g_full, 1)

            def rows_product(f, first, act_hi_, act_lo_, tiles=RT):
                banks = [g_claim(f + t) for t in range(tiles)]
                units = stage_units(st)
                for j, (_, k0, nk, _, n) in enumerate(units):
                    u = first + j
                    arrived(u)
                    hi, lo = unit_view(w_hi, u), unit_view(w_lo, u)
                    final = j == len(units) - 1
                    for t in range(tiles):
                        for k in range(nk):
                            for a, w in ((act_hi_, hi), (act_hi_, lo), (act_lo_, hi)):
                                last = mm(banks[t][:, 0:n], a[:, k0 + k, t * P:(t + 1) * P], w[:, k, :],
                                          start=(k0 + k == 0 and a is act_hi_ and w is hi),
                                          stop=(final and k == nk - 1 and a is act_lo_))
                        if final:
                            last.then_inc(g_full, 1)
                    if not final:
                        last.then_inc(unit_used, 1)

            def small():
                pe.wait_ge(consts_in, 32)
                pe.wait_ge(rows_in, 16 * 18)
                for i, n in enumerate((N_PC, 2 * FH, 2 * FH)):
                    bank = d_claim(D_FIRST[st] + i)
                    nc.tensor.transpose(bank[:, 0:n], rows[0:n, i, :], const("ident", slice(0, n))[:, 0:n]).then_inc(d_full, 1)

            def bias_():
                f = D_FIRST[st]
                bank = d_claim(f)
                pe.wait_ge(table_in, 16)
                pe.wait_ge(table_ready, 1)
                mm(bank[0:AH, 0:BIAS_N + 1], btab[0:BUCKETS + 1, :], const("pick", slice(0, BUCKETS + 1)), start=True, stop=True).then_inc(d_full, 1)
                pe.wait_ge(bias_in, 16)
                for h in range(AH):
                    bank = d_claim(f + 1 + h)
                    mm(bank[:, 0:3 * P], const("exchange"), brev[:, h, :], start=True, stop=True).then_inc(d_full, 1)

            def gbeta():
                bank = d_claim(D_FIRST[st])
                pe.wait_ge(slots_made, 1)
                for hf in range(2):
                    rr = slice(64 * hf, 64 * hf + 64)
                    for p in range(2):
                        d = 0 if hf == p else 1
                        for par in range(2):
                            o = (p * 2 + d) * 16
                            last = mm(bank[64 * par:64 * par + 64, o:o + 16].rearrange("p (i h) -> p i h", i=4), const("ones64", rr),
                                      g_slot[rr, p::2, par::2], start=True, stop=True)
                    tiles_apart(last)
                for kind, mask in enumerate(("upto", "after")):
                    for p in range(2):
                        o = 64 + (kind * 2 + p) * 32
                        last = mm(bank[:, o:o + 32].rearrange("p (i h) -> p i h", i=4), const(f"{mask}{p}"), g_slot[:, p::2, :], start=True, stop=True)
                last.then_inc(d_full, 1)

            def attn(n, g):
                f = D_FIRST[st]
                kbs = key_blocks(n)
                lo, hi = kbs[0], kbs[-1] + 1
                evacuated(D_FIRST[("aT",)] + 5)
                for i in range(4):
                    h = 4 * g + i
                    r = slice(64 * (h % 2), 64 * (h % 2) + 64)
                    bank = d_claim(f + i)
                    mm(bank[:, lo * P:hi * P], aqT[r, h // 2, n * P:(n + 1) * P], akT[r, g, (n - 1 + lo) * P:(n - 1 + hi) * P],
                       start=True, stop=True).then_inc(d_full, 1)
                pe.wait_ge(attn_p, NTH[st] + 1)
                for j, kb in enumerate(kbs):
                    transposes(f + 4 + j, [sc[:, i, kb * P:(kb + 1) * P] for i in range(4)])
                fo = f + 4 + len(kbs)
                bank = d_claim(fo)
                evacuated(fo - 1)
                for par in range(2):
                    for kb in kbs:
                        v = anat[:, n - 1 + kb, ATTN_Q + ATTN_KV + 64 * g:ATTN_Q + ATTN_KV + 64 * g + 64]
                        last = mm(bank[64 * par:64 * par + 64, 0:2 * P].rearrange("p (i q) -> p i q", i=2), v, pT[:, kb, par::2, :],
                                  start=(kb == lo), stop=(kb == hi - 1))
                last.then_inc(d_full, 1)

            def mscore(rt):
                evacuated(D_FIRST[("mqT",)] + 5)
                for j in range(2):
                    bank = d_claim(D_FIRST[st] + j)
                    for i in range(2):
                        h = 2 * j + i
                        last = mm(bank[:, i * N_MEM:(i + 1) * N_MEM], mqT[:, h, rt * P:(rt + 1) * P], mkT[:, h, :], start=True, stop=True)
                    last.then_inc(d_full, 1)

            def mout(h):
                f = D_FIRST[st]
                pe.wait_ge(mp, RT)
                for m in range(MT):
                    transposes(f + m, [msc[:, rt, h, m * P:(m + 1) * P] for rt in range(RT)])
                bank = d_claim(f + 2)
                evacuated(f + 1)
                for m in range(MT):
                    last = mm(bank[:, :], mkv[:, m, MEM_Q + h * P:MEM_Q + (h + 1) * P], mpT[:, m, :], start=(m == 0), stop=(m == MT - 1))
                last.then_inc(d_full, 1)

            def decay(s, hb):
                f, u = D_FIRST[st], 2 * s + hb
                bank = d_claim(f)
                pe.wait_ge(b_made, u + 1)
                mm(bank[:, 0:HB * CHUNK], const(f"after{s % 2}"), dec[:, 0].rearrange("p h c -> p (h c)"), start=True, stop=True).then_inc(d_full, 1)
                bank = d_claim(f + 1)
                evacuated(D_FIRST[("dnT",)] + 7)
                for i in (0, 2, 1, 3):
                    if i == 1:
                        tiles_apart(last)
                    for hf, _, c in halves(s):
                        h = HB * hb + i
                        r = slice(64 * (h % 2), 64 * (h % 2) + 64)
                        both = qkT[r, :, c * CHUNK:(c + 1) * CHUNK].rearrange("p (j t) n -> p t j n", j=2)[:, h // 2]
                        last = mm(bank[64 * hf:64 * hf + 64, i * 128:(i + 1) * 128].rearrange("p (j n) -> p j n", j=2),
                                  qkT[r, 4 + h // 2, c * CHUNK:(c + 1) * CHUNK], both, start=True, stop=True)
                last.then_inc(d_full, 1)

            def level(s, hb, l):
                f, u = D_FIRST[st], 2 * s + hb
                b = u % 2
                bank = d_claim(f)
                pe.wait_ge(nm_made, level_no(s, hb, l) + 1)
                if l > 0:
                    fp = D_FIRST[("level", s, hb, l - 1)]
                    evacuated(fp + d_fills(("level", s, hb, l - 1)) - 1)
                for i in range(HB):
                    for hf in range(2):
                        r = slice(64 * hf, 64 * hf + 64)
                        rhs = const("ident64", r) if l == 0 else yx[r, b, 1, i, :]
                        last = mm(bank[r, i * CHUNK:(i + 1) * CHUNK], nm[r, b, l % 2, i, :], rhs, start=True, stop=True)
                last.then_inc(d_full, 1)
                if l == 0:
                    return
                bank = d_claim(f + 1)
                evacuated(f)
                for i in range(HB):
                    for hf in range(2):
                        r = slice(64 * hf, 64 * hf + 64)
                        last = mm(bank[r, i * CHUNK:(i + 1) * CHUNK], wx[r, b, i, :], yx[r, b, 0, i, :], start=True, stop=True)
                        if l < LEVELS - 1:
                            last = mm(bank[r, 256 + i * CHUNK:256 + (i + 1) * CHUNK], yx[r, b, 0, i, :], wx[r, b, i, :], start=True, stop=True)
                last.then_inc(d_full, 1)

            def uw(s, hb):
                f, u = D_FIRST[st], 2 * s + hb
                b = u % 2
                bank = d_claim(f)
                evacuated(f_level(s, hb, LEVELS - 1))
                pe.wait_ge(kk_made, u + 1)
                for hf, _, c in halves(s):
                    for i in range(HB):
                        h = HB * hb + i
                        r = slice(64 * hf, 64 * hf + 64)
                        q = slice(64 * (h % 2), 64 * (h % 2) + 64)
                        mm(bank[r, i * CHUNK:(i + 1) * CHUNK], yx[r, b, 0, i, :], dn_nat[r, 2, c // 2, h * 64:h * 64 + 64], start=True, stop=True)
                        o = 256 + (hf * 2 + i // 2) * 64
                        last = mm(bank[q, o:o + 64], kk[r, i, :], yx[r, b, 0, i, :], start=True, stop=True)
                    if hf == 0:
                        tiles_apart(last)
                last.then_inc(d_full, 1)

            def scanv(s, hb):
                f, u = D_FIRST[st], 2 * s + hb
                b = u % 2
                bank = d_claim(f)
                evacuated(D_FIRST[("uw", s, hb)])
                if s:
                    evacuated(D_FIRST[("scans", s - 1, hb)])
                else:
                    pe.wait_ge(state_zero, 1)
                for i in (0, 2, 1, 3):
                    if i == 1:
                        tiles_apart(last)
                    for hf, d, c in halves(s):
                        h = HB * hb + i
                        r = slice(64 * hf, 64 * hf + 64)
                        q = slice(64 * (h % 2), 64 * (h % 2) + 64)
                        mm(bank[r, i * 64:i * 64 + 64], wt[q, b, hf, i // 2, :], S[q, hb, d, i // 2, :], start=True, stop=True)
                        last = mm(bank[r, 256 + i * 64:320 + i * 64], qkT[q, h // 2, c * CHUNK:(c + 1) * CHUNK], S[q, hb, d, i // 2, :], start=True, stop=True)
                last.then_inc(d_full, 1)

            def scans(s, hb):
                f, u = D_FIRST[st], 2 * s + hb
                b = u % 2
                bank = d_claim(f)
                pe.wait_ge(vn_made, u + 1)
                for hf, d, c in halves(s):
                    for i in range(HB):
                        h = HB * hb + i
                        r = slice(64 * hf, 64 * hf + 64)
                        q = slice(64 * (h % 2), 64 * (h % 2) + 64)
                        mm(bank[r, i * 64:i * 64 + 64], at_[r, u % 4, i, :], vn[r, b, i, :], start=True, stop=True)
                        o = 256 + (d * 2 + i // 2) * 64
                        last = mm(bank[q, o:o + 64], ku[r, b, i, :], vn[r, b, i, :], start=True, stop=True)
                    if hf == 0:
                        tiles_apart(last)
                last.then_inc(d_full, 1)

            def branch(b, c):
                f = G_FIRST[st]
                units = stage_units(st)
                u = U_FIRST[st]
                uy, ug = (u, u + 1) if len(units) == 2 else (U_FIRST[("branch", b, c - 1)], u)
                y_hi, y_lo = (yM_hi, yM_lo) if b == 1 else (yA_hi, yA_lo)
                if c == 0:
                    evacuated((D_FIRST[("attn", RT - 1, 1)] + d_fills(("attn", RT - 1, 1)) - 1,
                               D_FIRST[("mout", MH - 1)] + 2, D_FIRST[("oT",)] + 3)[b])
                columns_product(f, uy, P * (c % 2), y_hi, y_lo, 4)
                columns_product(f + 1, ug, 0, hT_hi, hT_lo, KT)

            for st in order:
                kind, a = st[0], st[1:]
                f, u = D_FIRST[st], U_FIRST[st]
                if kind == "small":
                    small()
                elif kind == "bias":
                    bias_()
                elif kind == "xT":
                    pe.wait_ge(x_scaled, 1)
                    transposes(f, [xt[:, rt, a[0] * P:(a[0] + 1) * P] for rt in range(RT)])
                elif kind == "mT":
                    pe.wait_ge(x_scaled, 2)
                    transposes(f, [mx[:, m, a[0] * P:(a[0] + 1) * P] for m in range(MT)])
                elif kind == "dnproj":
                    if a[0] == 0:
                        evacuated(D_FIRST[("xT", KT - 1)])
                    columns_product(G_FIRST[st], u, 0, hT_hi, hT_lo, KT)
                elif kind in ("baproj", "zproj", "aqproj", "akvproj", "mqproj"):
                    rows_product(G_FIRST[st], u, hT_hi, hT_lo)
                elif kind == "mkvproj":
                    if a[0] == 0:
                        evacuated(D_FIRST[("mT", KT - 1)])
                    rows_product(G_FIRST[st], u, memT_hi, memT_lo, MT)
                elif kind == "gbeta":
                    gbeta()
                elif kind == "dnnat":
                    rt, j = a
                    pe.wait_ge(dn_silu, 4 * j + 4)
                    transposes(f, [dnc[:, 4 * j + t, rt * P:(rt + 1) * P] for t in range(4)])
                elif kind == "aT":
                    pe.wait_ge(a_scaled, 1)
                    for t in range(4):
                        transposes(f + t, [anat[:, rt, t * P:(t + 1) * P] for rt in range(RT)])
                    for g in range(AKV):
                        bank = d_claim(f + 4 + g)
                        for rt in range(RT):
                            for side in range(2):
                                last = mm(bank[64 * side:64 * side + 64, rt * P:(rt + 1) * P], anat[:, rt, ATTN_Q + 64 * g:ATTN_Q + 64 * g + 64],
                                          const("ident"), start=True, stop=True)
                        last.then_inc(d_full, 1)
                elif kind == "attn":
                    attn(*a)
                elif kind == "mqT":
                    pe.wait_ge(mq_scaled, 1)
                    for h in range(MH):
                        transposes(f + h, [mqn[:, rt, h * P:(h + 1) * P] for rt in range(RT)])
                    for j in range(MH // 2):
                        transposes(f + MH + j, [mkv[:, m, (2 * j + i) * P:(2 * j + i + 1) * P] for i in range(2) for m in range(MT)])
                elif kind == "mscore":
                    mscore(*a)
                elif kind == "mout":
                    mout(*a)
                elif kind == "dnT":
                    pe.wait_ge(dn_scaled, 1)
                    for j in range(2):
                        for t in range(4):
                            transposes(f + 4 * j + t, [dn_nat[:, j, rt, t * P:(t + 1) * P] for rt in range(RT)])
                elif kind == "decay":
                    decay(*a)
                elif kind == "level":
                    level(*a)
                elif kind == "uw":
                    uw(*a)
                elif kind == "scanv":
                    scanv(*a)
                elif kind == "scans":
                    scans(*a)
                elif kind == "branch":
                    branch(*a)
                elif kind == "oT":
                    pe.wait_ge(o_scaled, 1)
                    for t in range(4):
                        transposes(f + t, [o_nat[:, rt, t * P:(t + 1) * P] for rt in range(RT)])
                elif kind == "wout":
                    pe.wait_ge(m_split, KT)
                    rows_product(G_FIRST[st], u, m_hi, m_lo)
                elif kind == "h2T":
                    pe.wait_ge(x2_scaled, 1)
                    transposes(f, [xn[:, rt, a[0] * P:(a[0] + 1) * P] for rt in range(RT)])
                elif kind == "up":
                    if a[0] == 0:
                        evacuated(D_FIRST[("h2T", KT - 1)])
                    columns_product(G_FIRST[st], u, 0, hT_hi, hT_lo, KT)
                    columns_product(G_FIRST[st] + 1, u + 1, 0, hT_hi, hT_lo, KT)
                elif kind == "down":
                    pe.wait_ge(f_split, FT)
                    rows_product(G_FIRST[st], u, act_hi, act_lo)

        @block.scalar
        def _(act):
            steps = [0]

            def link(ins):
                steps[0] += 1
                ins.then_inc(act_step, 1)
                act.wait_ge(act_step, steps[0])

            def splits(place):
                for u in SPLITS_AT[place]:
                    if u >= len_units:
                        continue
                    act.wait_ge(raw_loaded[u % RAW_N], 16 * (u // RAW_N + 1))
                    if u >= HL_N:
                        name, value = UNIT_DONE[u - HL_N]
                        act.wait_ge(SIG[name], value)
                    nc.scalar.copy(unit_view(w_hi, u), unit_view(raw, u)).then_inc(hi_made, 1)

            def filled(f):
                act.wait_ge(d_full, f + 1)
                return db[f % 4]

            def g_filled(f):
                act.wait_ge(g_full, f + 1)
                return gb[f % 4]

            def root():
                act.wait_ge(var_made, NORM[kind] + 1)
                v = {"xnorm": st_x, "anorm": st_a, "mqnorm": st_m, "dnnorm": st_d, "osum": st_o, "x2norm": st_x}[kind]
                v = v[:, 0:RT] if kind == "x2norm" else v[:]
                nc.scalar.activation(v, v, ACT.Sqrt).then_inc(sqrt_made, 1)

            def col(i):
                return pcol[:, i:i + 1]

            def silu_of(c):
                f = G_FIRST[("dnproj", c)]
                act.wait_ge(g_free[f % 4], f // 4 + 1)
                nc.scalar.activation(dnc[:, c, :], dnc[:, c, :], ACT.Silu).then_inc(dn_silu, 1)

            def conv_start(c, half_, b):
                f = G_FIRST[st] + half_
                bank = g_filled(f)
                ct = half_ * FT + c
                if c >= 2:
                    act.wait_ge(f_split, c - 1)
                nc.scalar.activation(u_gv[:, b, half_, :], bank[:, :], ACT.Identity, bias=fcol[:, 3 * 2 * FT + ct:3 * 2 * FT + ct + 1],
                                     scale=fcol[:, 2 * FT + ct:2 * FT + ct + 1]).then_inc(ua_made, 1)

            for place_, st in enumerate(order):
                kind, a = st[0], st[1:]
                f, fg = D_FIRST[st], G_FIRST[st]
                if kind == "bias":
                    splits(-1)
                if kind == "small":
                    nc.scalar.copy(pcol[:, 0:N_PC], filled(f)[:, 0:N_PC]).then_inc(d_free[f % 4], 1)
                    for i in range(2):
                        nc.scalar.copy(fcol[:, i * 2 * FH:(i + 1) * 2 * FH], filled(f + 1 + i)[:, 0:2 * FH]).then_inc(d_free[(f + 1 + i) % 4], 1)
                elif kind == "xnorm":
                    act.wait_ge(x_in, 16)
                    act.wait_ge(mem_in, 16)
                    for t in range(RT + MT):
                        src = xt[:, t, :] if t < RT else mx[:, t - RT, :]
                        ins = nc.scalar.activation(scr[:], src, ACT.Square, accum_out=st_x[:, t:t + 1])
                        if t == RT + MT - 1:
                            ins.then_inc(ss_made, 1)
                        else:
                            link(ins)
                    root()
                elif kind == "xT":
                    act.wait_ge(d_free[D_FIRST[("small",)] % 4], D_FIRST[("small",)] // 4 + 1)
                    nc.scalar.activation(hT_hi[:, a[0], :], filled(f)[:, :], ACT.Identity, scale=col(PC_MIX + a[0])).then_inc(part_hi, 1)
                elif kind == "mT":
                    nc.scalar.activation(memT_hi[:, a[0], :], filled(f)[:, 0:N_MEM], ACT.Identity, scale=col(PC_MEM + a[0])).then_inc(part_hi, 1)
                elif kind == "bias":
                    nc.scalar.copy(bT[0:AH, :], filled(f)[0:AH, 0:BIAS_N + 1]).then_inc(d_free[f % 4], 1)
                    for h in range(AH):
                        nc.scalar.copy(bias[:, h, :], filled(f + 1 + h)[:, 0:3 * P]).then_inc(d_free[(f + 1 + h) % 4], 1)
                elif kind == "dnproj":
                    splits(place_)
                    c = a[0]
                    nc.scalar.activation(dnc[:, c, :], g_filled(fg)[:, :], ACT.Identity, scale=col((DN_TAPS // 2) * 12 + c)).then_inc(tap_made, 1)
                    if c:
                        silu_of(c - 1)
                    if c == 11:
                        silu_of(c)
                elif kind == "baproj":
                    splits(place_)
                    for rt in range(RT):
                        nc.scalar.copy(ba[:, rt, :], g_filled(fg + rt)[:, 0:32]).then_inc(g_free[(fg + rt) % 4], 1)
                elif kind == "zproj":
                    splits(place_)
                    for rt in range(RT):
                        nc.scalar.activation(zs[:, rt, :], g_filled(fg + rt)[:, :], ACT.Silu).then_inc(g_free[(fg + rt) % 4], 1)
                elif kind == "gbeta":
                    act.wait_ge(sp_made, 1)
                    link(nc.scalar.activation(sp[:, 1], sp[:, 0], ACT.Abs))
                    link(nc.scalar.activation(sp[:, 1], sp[:, 1], ACT.Exp, scale=-1.0))
                    link(nc.scalar.activation(ealog[:], rowp[:, 0:16], ACT.Exp))
                    nc.scalar.activation(sp[:, 1], sp[:, 1], ACT.Ln, bias=1.0).then_inc(softplus_made, 1)
                    act.wait_ge(sp_made, 2)
                    nc.scalar.activation(sp[:, 1], ba[:, :, 0:16], ACT.Sigmoid).then_inc(beta_made, 1)
                    nc.scalar.activation(e_slot[:], filled(f)[:, 0:192], ACT.Exp).then_inc(d_free[f % 4], 1)
                elif kind == "aqproj":
                    splits(place_)
                    for rt in range(RT):
                        nc.scalar.copy(anat[:, rt, 0:ATTN_Q], g_filled(fg + rt)[:, :]).then_inc(g_free[(fg + rt) % 4], 1)
                elif kind == "akvproj":
                    splits(place_)
                    for rt in range(RT):
                        nc.scalar.copy(anat[:, rt, ATTN_Q:], g_filled(fg + rt)[:, 0:2 * ATTN_KV]).then_inc(g_free[(fg + rt) % 4], 1)
                elif kind in ("anorm", "mqnorm", "dnnorm", "osum"):
                    root()
                elif kind == "dnnat":
                    nc.scalar.copy(dn_nat[:, a[1], a[0], :], filled(f)[:, :]).then_inc(d_free[f % 4], 1)
                elif kind == "aT":
                    for t in range(4):
                        nc.scalar.activation(aqT[:, t, :], filled(f + t)[:, :], ACT.Identity, scale=col(PC_AQ)).then_inc(d_free[(f + t) % 4], 1)
                    for g in range(AKV):
                        nc.scalar.activation(akT[:, g, :], filled(f + 4 + g)[:, :], ACT.Identity, scale=col(PC_AK)).then_inc(d_free[(f + 4 + g) % 4], 1)
                elif kind == "attn":
                    n, g = a
                    kbs = key_blocks(n)
                    lo, hi = kbs[0] * P, (kbs[-1] + 1) * P
                    act.wait_ge(attn_max, NTH[st] + 1)
                    nc.scalar.activation(st_s[:, 5, :], st_s[:, 3, :], ACT.Exp)
                    for i in range(4):
                        ins = nc.scalar.activation(sc[:, i, lo:hi], sc[:, i, lo:hi], ACT.Exp, bias=st_s[:, 2, i:i + 1], accum_out=st_s[:, 4, i:i + 1])
                    ins.then_inc(attn_exp, 1)
                    for j, kb in enumerate(kbs):
                        fk = f + 4 + j
                        nc.scalar.copy(pT[:, kb].rearrange("p i q -> p (i q)"), filled(fk)[:, :]).then_inc(d_free[fk % 4], 1)
                    fo = f + 4 + len(kbs)
                    nc.scalar.copy(yA_hi[:, 2 * g:2 * g + 2, n * P:(n + 1) * P], filled(fo)[:, 0:2 * P].rearrange("p (i q) -> p i q", i=2)).then_inc(part_hi, 1)
                elif kind == "mqproj":
                    splits(place_)
                    for rt in range(RT):
                        nc.scalar.copy(mqn[:, rt, :], g_filled(fg + rt)[:, :]).then_inc(g_free[(fg + rt) % 4], 1)
                elif kind == "mkvproj":
                    splits(place_)
                    for m in range(MT):
                        nc.scalar.copy(mkv[:, m, a[0] * 512:(a[0] + 1) * 512], g_filled(fg + m)[:, :]).then_inc(g_free[(fg + m) % 4], 1)
                elif kind == "mqT":
                    for h in range(MH):
                        nc.scalar.activation(mqT[:, h, :], filled(f + h)[:, :], ACT.Identity, scale=col(PC_MQ)).then_inc(d_free[(f + h) % 4], 1)
                    for j in range(MH // 2):
                        fk = f + MH + j
                        nc.scalar.activation(mkT[:, 2 * j:2 * j + 2, :], filled(fk)[:, :].rearrange("p (h m) -> p h m", h=2), ACT.Identity, scale=col(PC_MK)).then_inc(d_free[fk % 4], 1)
                elif kind == "mscore":
                    rt = a[0]
                    for j in range(2):
                        act.wait_ge(mmax, 2 * rt + j + 1)
                        bank = filled(f + j)
                        for i in range(2):
                            h = 2 * j + i
                            ins = nc.scalar.activation(msc[:, rt, h, :], bank[:, i * N_MEM:(i + 1) * N_MEM], ACT.Exp, bias=st_s[:, 6, h:h + 1], accum_out=st_s[:, 7, h:h + 1])
                        ins.then_inc(d_free[(f + j) % 4], 1)
                elif kind == "mout":
                    for m in range(MT):
                        nc.scalar.copy(mpT[:, m, :], filled(f + m)[:, :]).then_inc(d_free[(f + m) % 4], 1)
                    nc.scalar.copy(yM_hi[:, a[0], :], filled(f + 2)[:, :]).then_inc(part_hi, 1)
                elif kind == "dnT":
                    for j in range(8):
                        nc.scalar.copy(qkT[:, j, :], filled(f + j)[:, :]).then_inc(d_free[(f + j) % 4], 1)
                elif kind == "decay":
                    u = 2 * a[0] + a[1]
                    if u:
                        fu = D_FIRST[("decay",) + divmod(u - 1, 2)] + 1
                        act.wait_ge(d_free[fu % 4], fu // 4 + 1)
                    nc.scalar.activation(dec[:, 0].rearrange("p h c -> p (h c)"), filled(f)[:, 0:HB * CHUNK], ACT.Exp).then_inc(d_free[f % 4], 1)
                elif kind == "level":
                    if a[2]:
                        nc.scalar.copy(wx[:, (2 * a[0] + a[1]) % 2].rearrange("p h c -> p (h c)"), filled(f)[:, 0:HB * CHUNK]).then_inc(d_free[f % 4], 1)
                elif kind == "branch":
                    splits(place_)
                    b, c = a
                    dst = merged[:, c, :] if b == 0 else tg[:]
                    if b and NTH[st] > KT:
                        act.wait_ge(gate_used, NTH[st] - KT)
                    nc.scalar.activation(dst, g_filled(fg + 1)[:, :], ACT.Tanh, scale=0.5).then_inc(g_free[(fg + 1) % 4], 1)
                    if b == 2:
                        act.wait_ge(gate_used, NTH[st] + 1 - KT)
                        nc.scalar.mul(m_hi[:, c, :], merged[:, c, :], 0.5).then_inc(mhi_made, 1)
                elif kind == "oT":
                    for t in range(4):
                        nc.scalar.activation(yA_hi[:, t, :], filled(f + t)[:, :], ACT.Identity, scale=col(PC_DO)).then_inc(part_hi, 1)
                elif kind == "wout":
                    splits(place_)
                elif kind == "x2norm":
                    fo = G_FIRST[("wout", 1)] + RT - 1
                    for b4 in range(4):
                        act.wait_ge(g_free[b4], (fo + 1 - b4 + 3) // 4)
                    for t in range(RT):
                        ins = nc.scalar.activation(scr2[:], x2[:, t, :], ACT.Square, accum_out=st_x[:, t:t + 1])
                        if t == RT - 1:
                            ins.then_inc(ss_made, 1)
                        else:
                            link(ins)
                    root()
                elif kind == "h2T":
                    nc.scalar.activation(hT_hi[:, a[0], :], filled(f)[:, :], ACT.Identity, scale=col(PC_FFN + a[0])).then_inc(part_hi, 1)
                elif kind == "up":
                    splits(place_)
                    c = a[0]
                    conv_start(c, 0, c % 2)
                    conv_start(c, 1, c % 2)
                    act.wait_ge(g_free[fg % 4], fg // 4 + 1)
                    nc.scalar.activation(u_gv[:, c % 2, 0, :], u_gv[:, c % 2, 0, :], ACT.Silu).then_inc(silu_made, 1)
                    act.wait_ge(glu_made, c + 1)
                    nc.scalar.copy(act_hi[:, c, :], u_gv[:, c % 2, 1, :]).then_inc(fhi_made, 1)
                elif kind == "down":
                    splits(place_)

        @block.vector
        def _(dve):
            v = nc.vector
            steps = [0]

            def link(ins):
                steps[0] += 1
                ins.then_inc(dve_step, 1)
                dve.wait_ge(dve_step, steps[0])

            def splits(place):
                for u in SPLITS_AT[place]:
                    if u >= len_units:
                        continue
                    dve.wait_ge(hi_made, u + 1)
                    v.tensor_tensor(unit_view(w_lo, u), unit_view(raw, u), unit_view(w_hi, u).bitcast(F), ALU.subtract).then_inc(lo_made, 1)

            def filled(f):
                dve.wait_ge(d_full, f + 1)
                return db[f % 4]

            def g_filled(f):
                dve.wait_ge(g_full, f + 1)
                return gb[f % 4]

            def inverse_root(stat, n_mean, after_squares=True):
                v.tensor_scalar(stat, stat, 1.0 / n_mean, EPS, ALU.mult, ALU.add).then_inc(var_made, 1)
                dve.wait_ge(sqrt_made, NORM[kind] + 1)
                link(v.reciprocal(stat, stat))

            def squares(dst, src, width, d=64, room=None):
                room = sq_flat if room is None else room
                link(v.tensor_tensor(room[:, 0:width], src, src, ALU.mult))
                link(v.tensor_reduce(dst, room[:, 0:width].rearrange("p (h d) -> p h d", d=d), X, ALU.add))

            def low_part(dst, bank, hi, scale=None):
                if scale is None:
                    return v.tensor_tensor(dst, bank, hi.bitcast(F), ALU.subtract)
                return v.scalar_tensor_tensor(dst, bank, scale, hi.bitcast(F), ALU.mult, ALU.subtract)

            def col(i):
                return pcol[:, i:i + 1]

            def wide(ap, n=64):
                return ap.unsqueeze(len(ap.shape)).to_broadcast(list(ap.shape) + [n])

            sq_flat = sq[:].rearrange("p t d -> p (t d)")
            his = [0]

            def hi_part():
                his[0] += 1
                dve.wait_ge(part_hi, his[0])

            v.memset(btab[BUCKETS:BUCKETS + 1, :], NEG).then_inc(table_ready, 1)
            for place_, st in enumerate(order):
                kind, a = st[0], st[1:]
                f, fg = D_FIRST[st], G_FIRST[st]
                if kind == "bias":
                    splits(-1)
                if kind == "xnorm":
                    dve.wait_ge(ss_made, 1)
                    inverse_root(st_x[:], D)
                    for t in range(RT + MT):
                        dst = xt[:, t, :] if t < RT else mx[:, t - RT, :]
                        ins = v.tensor_scalar(dst, dst, st_x[:, t:t + 1], None, ALU.mult)
                        if t in (RT - 1, RT + MT - 1):
                            ins.then_inc(x_scaled, 1)
                elif kind == "xT":
                    dve.wait_ge(d_free[D_FIRST[("small",)] % 4], D_FIRST[("small",)] // 4 + 1)
                    hi_part()
                    low_part(hT_lo[:, a[0], :], filled(f)[:, :], hT_hi[:, a[0], :], col(PC_MIX + a[0])).then_inc(d_free[f % 4], 1)
                elif kind == "mT":
                    hi_part()
                    low_part(memT_lo[:, a[0], :], filled(f)[:, 0:N_MEM], memT_hi[:, a[0], :], col(PC_MEM + a[0])).then_inc(d_free[f % 4], 1)
                elif kind == "dnproj":
                    splits(place_)
                    c = a[0]
                    bank = g_filled(fg)
                    dve.wait_ge(tap_made, c + 1)
                    for j in (0, 1, 3, 4):
                        d = j - DN_TAPS // 2
                        lo, hi = max(0, -d), SEQ - max(0, d)
                        y = dnc[:, c, lo:hi]
                        ins = v.scalar_tensor_tensor(y, bank[:, lo + d:hi + d], col(j * 12 + c), y, ALU.mult, ALU.add)
                        if j == 4:
                            ins.then_inc(g_free[fg % 4], 1)
                        else:
                            link(ins)
                elif kind in ("baproj", "zproj", "aqproj", "akvproj", "mqproj", "mkvproj"):
                    splits(place_)
                elif kind == "gbeta":
                    fb = G_FIRST[("baproj",)]
                    for rt in range(RT):
                        dve.wait_ge(g_free[(fb + rt) % 4], (fb + rt) // 4 + 1)
                    dve.wait_ge(rows_in, 16 * 18)
                    dt = rowp[:, 16:32].unsqueeze(1).to_broadcast([P, RT, 16])
                    v.tensor_tensor(sp[:, 0], ba[:, :, 16:32], dt, ALU.add).then_inc(sp_made, 1)
                    dve.wait_ge(softplus_made, 1)
                    link(v.scalar_tensor_tensor(sp[:, 0], sp[:, 0], 0.0, sp[:, 1], ALU.max, ALU.add))
                    v.scalar_tensor_tensor(sp[:, 0], sp[:, 0], -1.0, ealog[:].unsqueeze(1).to_broadcast([P, RT, 16]), ALU.mult, ALU.mult).then_inc(sp_made, 1)
                    dve.wait_ge(sp_made, 2)
                    dve.wait_ge(beta_made, 1)
                    for src, dst in ((sp[:, 1], b_slot), (sp[:, 0], g_slot)):
                        for hf in range(2):
                            r = slice(64 * hf, 64 * hf + 64)
                            v.tensor_copy(dst[r, hf::2, :], src[r, :, 0:8])
                            for i in range(RT):
                                ins = v.tensor_copy(dst[r, 2 * i + 1 - hf, :], src[r, RT - 1 - i, 8:16])
                    ins.then_inc(slots_made, 1)
                elif kind == "anorm":
                    fa = G_FIRST[("akvproj",)]
                    for b4 in range(4):
                        dve.wait_ge(g_free[b4], (fa + RT - b4 + 3) // 4)
                    n = ATTN_Q + ATTN_KV
                    for rt in range(RT):
                        squares(st_a[:, rt, :], anat[:, rt, 0:n], n)
                    inverse_root(st_a[:], AD)
                    link(v.tensor_scalar(st_a[:, :, 0:AH], st_a[:, :, 0:AH], AD ** -0.5, None, ALU.mult))
                    for rt in range(RT):
                        x3 = heads(anat[:, rt, 0:n])
                        ins = v.tensor_tensor(x3, x3, wide(st_a[:, rt, :]), ALU.mult)
                    ins.then_inc(a_scaled, 1)
                elif kind == "attn":
                    n, g = a
                    kbs = key_blocks(n)
                    lo, hi = kbs[0] * P, (kbs[-1] + 1) * P
                    fb = D_FIRST[("bias",)] + AH
                    dve.wait_ge(d_free[fb % 4], fb // 4 + 1)
                    if NTH[st]:
                        prev = ORDER[place_ - 1]
                        dve.wait_ge(d_full, D_FIRST[prev] + d_fills(prev))
                    for i in range(4):
                        bank = filled(f + i)
                        v.tensor_tensor(sc[:, i, lo:hi], bank[:, lo:hi], bias[:, 4 * g + i, lo:hi], ALU.add).then_inc(d_free[(f + i) % 4], 1)
                    for i in range(4):
                        dve.wait_ge(d_free[(f + i) % 4], (f + i) // 4 + 1)
                    sink = rowp[:, 32 + 4 * g:36 + 4 * g]
                    link(v.tensor_reduce(st_s[:, 0, :], sc[:, :, lo:hi], X, ALU.max))
                    link(v.tensor_tensor(st_s[:, 1, :], st_s[:, 0, :], sink, ALU.max))
                    link(v.tensor_scalar(st_s[:, 2, :], st_s[:, 1, :], -1.0, None, ALU.mult))
                    v.tensor_tensor(st_s[:, 3, :], sink, st_s[:, 2, :], ALU.add).then_inc(attn_max, 1)
                    dve.wait_ge(attn_exp, NTH[st] + 1)
                    link(v.tensor_tensor(st_s[:, 4, :], st_s[:, 4, :], st_s[:, 5, :], ALU.add))
                    link(v.reciprocal(st_s[:, 4, :], st_s[:, 4, :]))
                    for i in range(4):
                        ins = v.tensor_scalar(sc[:, i, lo:hi], sc[:, i, lo:hi], st_s[:, 4, i:i + 1], None, ALU.mult)
                    ins.then_inc(attn_p, 1)
                    fo = f + 4 + len(kbs)
                    hi_part()
                    dst = slice(n * P, (n + 1) * P)
                    low_part(yA_lo[:, 2 * g:2 * g + 2, dst], filled(fo)[:, 0:2 * P].rearrange("p (i q) -> p i q", i=2),
                             yA_hi[:, 2 * g:2 * g + 2, dst]).then_inc(d_free[fo % 4], 1)
                elif kind == "mqnorm":
                    fm = G_FIRST[("mkvproj", 1)] + MT
                    for b4 in range(4):
                        dve.wait_ge(g_free[b4], (fm - b4 + 3) // 4)
                    for rt in range(RT):
                        squares(st_m[:, 4 * rt:4 * rt + 4], mqn[:, rt, :], 512, MD)
                    for m in range(MT):
                        squares(st_m[:, 16 + 4 * m:20 + 4 * m], mkv[:, m, 0:512], 512, MD)
                    inverse_root(st_m[:], MD)
                    link(v.tensor_scalar(st_m[:, 0:16], st_m[:, 0:16], MD ** -0.5, None, ALU.mult))
                    for rt in range(RT):
                        x3 = mqn[:, rt, :].rearrange("p (h d) -> p h d", d=MD)
                        v.tensor_tensor(x3, x3, wide(st_m[:, 4 * rt:4 * rt + 4], MD), ALU.mult)
                    for m in range(MT):
                        x3 = mkv[:, m, 0:512].rearrange("p (h d) -> p h d", d=MD)
                        ins = v.tensor_tensor(x3, x3, wide(st_m[:, 16 + 4 * m:20 + 4 * m], MD), ALU.mult)
                    ins.then_inc(mq_scaled, 1)
                elif kind == "mscore":
                    rt = a[0]
                    for j in range(2):
                        h2 = slice(2 * j, 2 * j + 2)
                        link(v.tensor_reduce(st_s[:, 0, h2], filled(f + j)[:, :].rearrange("p (h m) -> p h m", h=2), X, ALU.max))
                        v.tensor_scalar(st_s[:, 6, h2], st_s[:, 0, h2], -1.0, None, ALU.mult).then_inc(mmax, 1)
                    dve.wait_ge(d_free[(f + 1) % 4], (f + 1) // 4 + 1)
                    link(v.reciprocal(st_s[:, 7, :], st_s[:, 7, :]))
                    for h in range(MH):
                        ins = v.tensor_scalar(msc[:, rt, h, :], msc[:, rt, h, :], st_s[:, 7, h:h + 1], None, ALU.mult)
                    ins.then_inc(mp, 1)
                elif kind == "mout":
                    hi_part()
                    low_part(yM_lo[:, a[0], :], filled(f + 2)[:, :], yM_hi[:, a[0], :]).then_inc(d_free[(f + 2) % 4], 1)
                elif kind == "dnnorm":
                    fn = D_FIRST[("dnnat", RT - 1, 2)]
                    dve.wait_ge(d_free[fn % 4], fn // 4 + 1)
                    for j in range(2):
                        for rt in range(RT):
                            squares(st_d[:, j, rt, :], dn_nat[:, j, rt, :], DN_W)
                    inverse_root(st_d[:], 1)
                    link(v.tensor_scalar(st_d[:, 0], st_d[:, 0], DK ** -0.5, None, ALU.mult))
                    for j in range(2):
                        for rt in range(RT):
                            x3 = heads(dn_nat[:, j, rt, :])
                            ins = v.tensor_tensor(x3, x3, wide(st_d[:, j, rt, :]), ALU.mult)
                    ins.then_inc(dn_scaled, 1)
                elif kind == "dnT":
                    dve.wait_ge(d_full, f)
                    v.memset(S[:].rearrange("p a b c d -> p (a b c d)"), 0.0).then_inc(state_zero, 1)
                elif kind == "decay":
                    s, hb = a
                    u = 2 * s + hb
                    bank = filled(f + 1)[:, :].rearrange("p (h j n) -> p h j n", h=HB, j=2)
                    dve.wait_ge(em_made, u + 1)
                    v.tensor_tensor(at_[:, u % 4], bank[:, :, 0, :], dec[:, 0], ALU.mult)
                    v.tensor_tensor(nn[:, u % 2], bank[:, :, 1, :], dec[:, 1], ALU.mult).then_inc(d_free[(f + 1) % 4], 1)
                elif kind == "level":
                    s, hb, l = a
                    b = (2 * s + hb) % 2
                    if l == 0:
                        eye = const("ident64").unsqueeze(1).to_broadcast([P, HB, CHUNK])
                        dve.wait_ge(nm_made, level_no(s, hb, 0) + 1)
                        v.tensor_tensor(yx[:, b, 0], eye, nm[:, b, 0], ALU.subtract)
                        v.tensor_tensor(yx[:, b, 1], eye, heads(filled(f)[:, 0:HB * CHUNK]), ALU.subtract).then_inc(d_free[f % 4], 1)
                    else:
                        n = 2 if l < LEVELS - 1 else 1
                        y = yx[:, b].rearrange("p a h c -> p (a h c)")[:, 0:n * HB * CHUNK]
                        fl = f_level(s, hb, l - 1)
                        dve.wait_ge(d_free[fl % 4], fl // 4 + 1)
                        v.tensor_tensor(y, y, filled(f + 1)[:, 0:n * HB * CHUNK], ALU.subtract).then_inc(d_free[(f + 1) % 4], 1)
                elif kind == "uw":
                    s, hb = a
                    b = (2 * s + hb) % 2
                    bank = filled(f)
                    v.tensor_tensor(uu[:, b], heads(bank[:, 0:256]), wide(b_slot[:, s, HB * hb:HB * hb + HB]), ALU.mult)
                    v.tensor_copy(wt[:, b].rearrange("p a i c -> p (a i c)"), bank[:, 256:512]).then_inc(d_free[f % 4], 1)
                elif kind == "scanv":
                    s, hb = a
                    b = (2 * s + hb) % 2
                    bank = filled(f)
                    fu = D_FIRST[("uw", s, hb)]
                    dve.wait_ge(d_free[fu % 4], fu // 4 + 1)
                    link(v.tensor_tensor(vn[:, b], heads(bank[:, 0:256]), wide(b_slot[:, s, HB * hb:HB * hb + HB]), ALU.mult))
                    v.tensor_tensor(vn[:, b], uu[:, b], vn[:, b], ALU.subtract).then_inc(vn_made, 1)
                    if s:
                        dve.wait_ge(o_added, 2 * (s - 1) + hb + 1)
                    v.tensor_tensor(o1[:, b], heads(bank[:, 256:512]), wide(decay_of(0, s, hb)), ALU.mult).then_inc(d_free[f % 4], 1)
                elif kind == "scans":
                    s, hb = a
                    b = (2 * s + hb) % 2
                    fv = D_FIRST[("scanv", s, hb)]
                    dve.wait_ge(d_free[fv % 4], fv // 4 + 1)
                    egl = e_slot[:, 0:64].rearrange("p (q d i h) -> p q d i h", q=2, d=2, i=4)[:, s % 2, :, s // 2, 2 * hb:2 * hb + 2]
                    link(v.tensor_tensor(S[:, hb], S[:, hb], wide(egl), ALU.mult))
                    bank = filled(f)
                    link(v.tensor_tensor(o1[:, b], o1[:, b], heads(bank[:, 0:256]), ALU.add))
                    s_flat = S[:, hb].rearrange("p d i n -> p (d i n)")
                    v.tensor_tensor(s_flat, s_flat, bank[:, 256:512], ALU.add).then_inc(d_free[f % 4], 1)
                elif kind == "branch":
                    splits(place_)
                    b, c = a
                    yb = g_filled(fg)
                    dve.wait_ge(g_free[(fg + 1) % 4], (fg + 1) // 4 + 1)
                    if b == 0:
                        v.scalar_tensor_tensor(merged[:, c, :], merged[:, c, :], 1.0, yb[:, :], ALU.add, ALU.mult).then_inc(g_free[fg % 4], 1)
                    else:
                        v.scalar_tensor_tensor(tg[:], tg[:], 1.0, yb[:, :], ALU.add, ALU.mult).then_inc(g_free[fg % 4], 1)
                        dve.wait_ge(g_free[fg % 4], fg // 4 + 1)
                        v.tensor_tensor(merged[:, c, :], merged[:, c, :], tg[:], ALU.add).then_inc(gate_used, 1)
                        if b == 2:
                            dve.wait_ge(mhi_made, c + 1)
                            v.scalar_tensor_tensor(m_lo[:, c, :], merged[:, c, :], 0.5, m_hi[:, c, :].bitcast(F), ALU.mult, ALU.subtract).then_inc(m_split, 1)
                elif kind == "osum":
                    dve.wait_ge(o_added, 2 * NSLOT)
                    for rt in range(RT):
                        squares(st_o[:, DH * rt:DH * rt + DH], o_nat[:, rt, :], DN_W, room=at_[:].rearrange("p a h c -> p (a h c)"))
                    inverse_root(st_o[:], DK)
                    for rt in range(RT):
                        x3 = heads(o_nat[:, rt, :])
                        link(v.tensor_tensor(x3, x3, wide(st_o[:, DH * rt:DH * rt + DH]), ALU.mult))
                        ins = v.tensor_tensor(o_nat[:, rt, :], o_nat[:, rt, :], zs[:, rt, :], ALU.mult)
                    ins.then_inc(o_scaled, 1)
                elif kind == "oT":
                    for t in range(4):
                        hi_part()
                        low_part(yA_lo[:, t, :], filled(f + t)[:, :], yA_hi[:, t, :], col(PC_DO)).then_inc(d_free[(f + t) % 4], 1)
                elif kind == "wout":
                    splits(place_)
                    dve.wait_ge(xr_in, 16)
                    cc = slice(512 * a[0], 512 * a[0] + 512)
                    for rt in range(RT):
                        v.tensor_tensor(x2[:, rt, cc], g_filled(fg + rt)[:, :], xr[:, rt, cc], ALU.add).then_inc(g_free[(fg + rt) % 4], 1)
                elif kind == "x2norm":
                    dve.wait_ge(ss_made, 2)
                    inverse_root(st_x[:, 0:RT], D)
                    for t in range(RT):
                        ins = v.tensor_scalar(xn[:, t, :], x2[:, t, :], st_x[:, t:t + 1], None, ALU.mult)
                    ins.then_inc(x2_scaled, 1)
                elif kind == "h2T":
                    hi_part()
                    low_part(hT_lo[:, a[0], :], filled(f)[:, :], hT_hi[:, a[0], :], col(PC_FFN + a[0])).then_inc(d_free[f % 4], 1)
                elif kind == "up":
                    splits(place_)
                    c = a[0]
                    for half_ in range(2):
                        ct = half_ * FT + c
                        bank = g_filled(fg + half_)
                        dve.wait_ge(ua_made, 2 * c + half_ + 1)
                        y = u_gv[:, c % 2, half_, :]
                        link(v.scalar_tensor_tensor(y[:, 1:SEQ], bank[:, 0:SEQ - 1], fcol[:, ct:ct + 1], y[:, 1:SEQ], ALU.mult, ALU.add))
                        v.scalar_tensor_tensor(y[:, 0:SEQ - 1], bank[:, 1:SEQ], fcol[:, 4 * FT + ct:4 * FT + ct + 1], y[:, 0:SEQ - 1], ALU.mult, ALU.add).then_inc(g_free[(fg + half_) % 4], 1)
                    dve.wait_ge(silu_made, c + 1)
                    dve.wait_ge(g_free[(fg + 1) % 4], (fg + 1) // 4 + 1)
                    uv = u_gv[:, c % 2, 1, :]
                    v.tensor_tensor(uv, uv, u_gv[:, c % 2, 0, :], ALU.mult).then_inc(glu_made, 1)
                    dve.wait_ge(fhi_made, c + 1)
                    v.tensor_tensor(act_lo[:, c, :], uv, act_hi[:, c, :].bitcast(F), ALU.subtract).then_inc(f_split, 1)
                elif kind == "down":
                    splits(place_)
                    cc = slice(512 * a[0], 512 * a[0] + 512)
                    for rt in range(RT):
                        v.tensor_tensor(x2[:, rt, cc], x2[:, rt, cc], g_filled(fg + rt)[:, :], ALU.add).then_inc(g_free[(fg + rt) % 4], 1)

        @block.gpsimd
        def _(pool):
            g_ = nc.gpsimd
            steps = [0]
            before = {}

            def link(ins):
                steps[0] += 1
                ins.then_inc(pool_step, 1)
                pool.wait_ge(pool_step, steps[0])

            def say(ins, made):
                before[made.name] = before.get(made.name, 0) + 1
                ins.then_inc(made, 1)
                pool.wait_ge(made, before[made.name])

            def wide(ap, n=64):
                return ap.unsqueeze(len(ap.shape)).to_broadcast(list(ap.shape) + [n])

            def four(ap):
                return ap.unsqueeze(1).to_broadcast([ap.shape[0], HB, CHUNK])

            for st in order:
                kind, a = st[0], st[1:]
                f = D_FIRST[st]
                if kind == "decay":
                    s, hb = a
                    u = 2 * s + hb
                    mine = slice(HB * hb, HB * hb + HB)
                    if u == 0:
                        fq = D_FIRST[("dnT",)] + 7
                        pool.wait_ge(d_free[fq % 4], fq // 4 + 1)
                        pool.wait_ge(slots_made, 1)
                    else:
                        fu = D_FIRST[("decay",) + divmod(u - 1, 2)] + 1
                        pool.wait_ge(d_free[fu % 4], fu // 4 + 1)
                    say(g_.tensor_tensor(dec[:, 0], wide(g_slot[:, s, mine]), four(const(f"incl{s % 2}")), ALU.mult), b_made)
                    link(g_.tensor_tensor(dec[:, 1], wide(b_slot[:, s, mine]), four(const(f"strict{s % 2}")), ALU.mult))
                    pool.wait_ge(d_free[f % 4], f // 4 + 1)
                    link(g_.tensor_tensor(dec[:, 0], dec[:, 0], four(const(f"incl{s % 2}")), ALU.mult))
                    say(g_.tensor_tensor(dec[:, 1], dec[:, 1], dec[:, 0], ALU.mult), em_made)
                elif kind == "level":
                    s, hb, l = a
                    b = (2 * s + hb) % 2
                    fk = D_FIRST[("decay", s, hb)] + 1
                    pool.wait_ge(d_free[fk % 4], fk // 4 + 1)
                    if l == 2:
                        fl = f_level(s, hb, 0)
                        pool.wait_ge(d_free[fl % 4], fl // 4 + 1)
                    if l >= 2:
                        pool.wait_ge(d_full, D_FIRST[("level", s, hb, l - 2)] + 1)
                    elif s:
                        pool.wait_ge(d_full, D_FIRST[("level", s - 1, hb, LEVELS - 2 + l)] + 1)
                    say(g_.tensor_tensor(nm[:, b, l % 2], nn[:, b], four(const(f"pair{l}")), ALU.mult), nm_made)
                elif kind == "uw":
                    s, hb = a
                    u = 2 * s + hb
                    b = u % 2
                    if u:
                        pool.wait_ge(d_full, D_FIRST[("uw",) + divmod(u - 1, 2)] + 1)
                    if s:
                        pool.wait_ge(d_full, D_FIRST[("scans", s - 1, hb)] + 1)
                    for hf, _, c in halves(s):
                        r = slice(64 * hf, 64 * hf + 64)
                        k3 = heads(dn_nat[r, 1, c // 2, 256 * hb:256 * hb + 256])
                        link(g_.tensor_tensor(kk[r], k3, wide(decay_of(0, s, hb, r)), ALU.mult))
                        ins = g_.tensor_tensor(ku[r, b], k3, wide(decay_of(1, s, hb, r)), ALU.mult)
                        if hf == 0:
                            link(ins)
                    say(ins, kk_made)
                elif kind == "scans":
                    s, hb = a
                    b = (2 * s + hb) % 2
                    pool.wait_ge(d_free[f % 4], f // 4 + 1)
                    for hf, _, c in halves(s):
                        r = slice(64 * hf, 64 * hf + 64)
                        dst = heads(o_nat[r, c // 2, 256 * hb:256 * hb + 256])
                        if s < NSLOT // 2:
                            ins = g_.tensor_copy(dst, o1[r, b])
                        else:
                            ins = g_.tensor_tensor(dst, dst, o1[r, b], ALU.add)
                        if hf == 0:
                            link(ins)
                    say(ins, o_added)


_INS = ["x", "mem", "rel_bias_table", "norm_mix_g", "w_in", "attn_q_norm_g", "attn_k_norm_g", "attn_sink",
        "dn_conv_w", "dn_a_log", "dn_dt_bias", "dn_out_norm_g", "mem_norm_g", "mem_w_kv", "mem_q_norm_g",
        "mem_k_norm_g", "w_br_attn", "w_br_dn", "w_br_mem", "w_out", "norm_ffn_g", "ffn_w_up", "ffn_conv_w",
        "ffn_conv_b", "ffn_w_down"]


def kernel(**inputs):
    import concourse.bacc as _bacc
    from concourse.bass_utils import run_bass_kernel_spmd as _run

    nc = _bacc.Bacc("TRN2", target_bir_lowering=False, num_devices=1)
    arrays, args = {}, {}
    for name in _INS + ["consts"]:
        a = CONSTS if name == "consts" else np.ascontiguousarray(inputs[name])
        arrays[f"in_{name}"] = a
        args[name] = nc.dram_tensor(f"in_{name}", a.shape, mybir.dt.from_np(a.dtype), kind="ExternalInput").ap()
    out = nc.dram_tensor("out_x", (1, SEQ, D), mybir.dt.float32, kind="ExternalOutput").ap()
    encoder_layer(nc, args, out)
    r = _run(nc, [arrays], core_ids=[0])
    return r.results[0]["out_x"]
```

```python
import numpy as np
import concourse.bass as bass
from concourse import mybir
from contextlib import ExitStack

D, SEQ, P = 1024, 512, 128
KT = D // P
RT = SEQ // P
N_MEM = 256
MT = N_MEM // P
D_FF = 2816
FT = D_FF // P
EPS = 1e-6
AH, AKV, AD = 8, 2, 64
WINDOW, BUCKETS, MAX_DIST = 128, 32, 128
DH, DK = 8, 64
DN_TAPS, CHUNK = 5, 64
NSLOT = SEQ // CHUNK
HB = 4
MH, MD = 4, 128
FFN_TAPS = 3
ATTN_Q, ATTN_KV, DN_W, MEM_Q = AH * AD, AKV * AD, DH * DK, MH * MD
C_AQ = 0
C_AKV = C_AQ + ATTN_Q
C_DN = C_AKV + 2 * ATTN_KV
C_DZ = C_DN + 3 * DN_W
C_BA = C_DZ + DN_W
C_MQ = C_BA + 4 * DH
C_GATE = C_MQ + MEM_Q
D_IN = C_GATE + 3 * D
LEVELS = 6
NEG = -1e30
BIAS_N = 3 * P + P - 1
RAW_N, HL_N, UNIT = 2, 3, 1024

CONST_COLS = {}


def shape_constants():
    n = np.arange(P)
    same = (n[:, None] // CHUNK) == (n[None, :] // CHUNK)
    half = n // CHUNK
    c64 = np.arange(CHUNK)
    within = n % CHUNK
    parts = {"exchange": np.eye(P)[::-1], "pick": None, "ident": np.eye(P)}
    for p in range(2):
        fwd = (half == p)[:, None]
        parts[f"after{p}"] = same * np.where(fwd, n[:, None] > n[None, :], n[:, None] < n[None, :])
        parts[f"upto{p}"] = same * np.where(fwd, n[:, None] <= n[None, :], n[:, None] >= n[None, :])
    for p in range(2):
        fwd = (half == p)[:, None]
        parts[f"incl{p}"] = np.where(fwd, within[:, None] <= c64[None], within[:, None] >= c64[None])
        parts[f"strict{p}"] = np.where(fwd, within[:, None] < c64[None], within[:, None] > c64[None])
    for l in range(LEVELS):
        parts[f"pair{l}"] = ((within[:, None] >> l) ^ (c64[None] >> l)) == 1
    parts["ident64"] = within[:, None] == c64[None]
    parts["ones64"] = np.ones((P, CHUNK))
    rel = np.arange(BIAS_N) - (2 * P - 1)
    nb = BUCKETS // 2
    exact = nb // 2
    dist = np.abs(rel)
    large = exact + (np.log(np.maximum(dist, 1) / exact) / np.log(MAX_DIST / exact) * (nb - exact)).astype(np.int32)
    bucket = (rel > 0) * nb + np.where(dist < exact, dist, np.minimum(large, nb - 1))
    pick = np.zeros((P, BIAS_N + 1))
    valid = dist <= WINDOW
    pick[bucket[valid], np.arange(BIAS_N)[valid]] = 1.0
    pick[BUCKETS, :BIAS_N] = ~valid
    parts["pick"] = pick
    at = 0
    for k, v in parts.items():
        CONST_COLS[k] = (at, v.shape[1])
        at += v.shape[1]
    return np.concatenate([np.asarray(v, np.float32) for v in parts.values()], axis=1)


CONSTS = shape_constants()
EARLY = ("exchange", "pick")


PARTS = {"by": 2, "bg": 4, "mqproj": 16, "zproj": 16}
FILLER_COST = {"attn_s": 3.4, "attn_e": 0.5, "attn_t": 0.5, "attn_p": 1.8, "attn_o": 1.6, "mqT": 3, "mkT": 1.4, "mscore": 2,
               "mtrans": 1.5, "mout": 2.6, "part": 1.3, "by": 1.3, "bg": 1.3, "mqproj": 1.3}


def with_parts(st):
    return [("part", st, i) for i in range(PARTS[st[0]] - 1)] + [st]


def walk_order():
    order = [("xnorm",), ("small",)] + [("xT", k) for k in range(KT)]
    order += [("dnproj", 0), ("bias_a",), ("dnproj", 1), ("small_b",), ("mnorm",), ("dnproj", 2)]
    for c in range(3, 12):
        order += [("dnproj", c)]
        order += [("bias_b", c - 3), ("mT", c - 3)] if c - 3 < KT else []
        order += {6: [("baproj",)], 7: [("gates_a",)], 9: [("gates_b",)]}.get(c, [])
    order += [("mkvproj", 1)] + [("dnnat", rt, j) for j in range(3) for rt in range(RT)]
    order += [("dnnorm", 0), ("aqproj",), ("dnnorm", 1), ("akvproj",), ("anorm", 0), ("mkvproj", 0), ("anorm", 1), ("dnT",), ("aT",)]

    fillers = [("mknorm",), ("mkT",)]
    q_parts = with_parts(("mqproj",))
    for n in range(RT):
        for g in range(AKV):
            fillers += [("attn_s", n, g), q_parts.pop(0), ("attn_e", n, g)]
            fillers += ([q_parts.pop(0)] if len(q_parts) > 1 else []) + [(k, n, g) for k in ("attn_t", "attn_p", "attn_o")]
    fillers += q_parts + [("mqnorm",), ("mqT",)]
    for rt in range(RT):
        fillers += [("mscore", rt), ("mexp", rt), ("mscale", rt)]
    for h in range(MH):
        fillers += [("mtrans", h), ("mout", h)]
    branches = [with_parts((k, b, c)) for b in range(2) for c in range(KT) for k in ("by", "bg")]
    held_back = sum(branches[-4:], [])
    fillers += sum(branches[:-4], [])

    lane = []
    for s in range(NSLOT + 1):
        here = []
        if s < NSLOT:
            here += [("decay", s, 0), ("decay", s, 1)]
        if s > 0:
            here += [("scanv", s - 1, 0), ("scanv", s - 1, 1)]
        if s < NSLOT:
            here += [("levw", s, 0, 0), ("levw", s, 1, 0)]
        if s > 0:
            here += [("scans", s - 1, 0), ("scans", s - 1, 1)]
        if s < NSLOT:
            for l in range(1, LEVELS):
                here += [("levw", s, 0, l), ("levw", s, 1, l), ("levy", s, 0, l), ("levy", s, 1, l)]
            here += [("uw", s, 0), ("uw", s, 1)]
        lane += here
    cost = [FILLER_COST.get(st[0], 0.5) for st in fillers]
    per_stage = sum(cost) / (len(lane) - 4)
    z_parts = with_parts(("zproj",))
    spent = 0.0
    for i, st in enumerate(lane[:-2]):
        order.append(st)
        while fillers and spent < (i + 1) * per_stage:
            spent += FILLER_COST.get(fillers[0][0], 0.5)
            order.append(fillers.pop(0))
    order += fillers + z_parts[:2] + lane[-2:-1] + z_parts[2:3] + lane[-1:] + z_parts[3:]
    order += [("osum",)] + held_back + [("oT",)]
    for c in range(KT):
        order += with_parts(("by", 2, c)) + with_parts(("bg", 2, c))
    order += [("wout", 0), ("wout", 1), ("x2norm",)]
    order += [("h2T", k) for k in range(KT)]
    order += [("up", c) for c in range(FT)]
    order += [("down", 0), ("down", 1)]
    return order


ORDER = walk_order()
G_FILLS = {"dnproj": 1, "baproj": 1, "zproj": RT, "aqproj": RT, "akvproj": RT, "mqproj": RT,
           "mkvproj": MT, "by": 1, "bg": 1, "wout": RT, "up": 2, "down": RT}
D_FILLS = {"small": 1, "small_b": 2, "bias_a": 1, "bias_b": 1, "xT": 1, "mT": 1, "gates_b": 1, "aT": 4 + AKV, "dnnat": 1,
           "attn_s": 4, "attn_o": 1, "mqT": MH, "mkT": MH // 2, "mscore": 2, "mtrans": MT, "mout": 1, "dnT": 8,
           "decay": 2, "levw": 1, "levy": 1, "uw": 1, "scanv": 1, "scans": 1, "oT": 4, "h2T": 1}


def d_fills(st):
    return len(key_blocks(st[1])) if st[0] == "attn_p" else D_FILLS.get(st[0], 0)


def key_blocks(n):
    return [kb for kb in range(3) if 0 <= n - 1 + kb < RT]


def stage_units(st):
    kind = st[0]
    if kind == "dnproj":
        return [("w_in", 0, KT, C_DN + st[1] * P, P)]
    if kind in ("zproj", "aqproj", "mqproj"):
        c0 = {"zproj": C_DZ, "aqproj": C_AQ, "mqproj": C_MQ}[kind]
        return [("w_in", 2 * i, 2, c0, 512) for i in range(KT // 2)]
    if kind == "akvproj":
        return [("w_in", 4 * i, 4, C_AKV, 2 * ATTN_KV) for i in range(KT // 4)]
    if kind == "mkvproj":
        return [("mem_w_kv", 2 * i, 2, 512 * st[1], 512) for i in range(KT // 2)]
    if kind == "by":
        name = ("w_br_attn", "w_br_mem", "w_br_dn")[st[1]]
        return [(name, 0, 4, st[2] * P, 2 * P)] if st[2] % 2 == 0 else []
    if kind == "bg":
        gate = (0, 2, 1)[st[1]]
        return [("w_in", 0, KT, C_GATE + gate * D + st[2] * P, P)]
    if kind == "wout":
        return [("w_out", 2 * i, 2, 512 * st[1], 512) for i in range(KT // 2)]
    if kind == "up":
        return [("ffn_w_up", 0, KT, st[1] * P, P), ("ffn_w_up", 0, KT, D_FF + st[1] * P, P)]
    if kind == "down":
        return [("ffn_w_down", 2 * i, 2, 512 * st[1], 512) for i in range(FT // 2)]
    return []


G_FIRST, D_FIRST, U_FIRST, NTH, UNITS = {}, {}, {}, {}, []
LAST_USE = []
G_AT, D_AT = 0, 0
for PLACE, STAGE in enumerate(ORDER):
    G_FIRST[STAGE], D_FIRST[STAGE], U_FIRST[STAGE] = G_AT, D_AT, len(UNITS)
    NTH[STAGE] = sum(o[0] == STAGE[0] for o in ORDER[:PLACE])
    G_AT += G_FILLS.get(STAGE[0], 0)
    D_AT += d_fills(STAGE)
    for UNIT_OF in stage_units(STAGE):
        UNITS.append(UNIT_OF)
        NUMBER = len(UNITS) - U_FIRST[STAGE]
        if UNIT_OF[0].startswith("w_br"):
            LAST_USE.append(ORDER.index(STAGE[:2] + (STAGE[2] + 1,)))
        elif STAGE[0] in ("mqproj", "zproj") and NUMBER < KT // 2:
            LAST_USE.append(ORDER.index(("part", STAGE, RT * NUMBER - 1)))
        else:
            LAST_USE.append(PLACE)

UNIT_DONE, USED_AT = [], 0
for NUMBER, PLACE in enumerate(LAST_USE):
    STAGE = ORDER[PLACE][1] if ORDER[PLACE][0] == "part" else ORDER[PLACE]
    IN_STAGE = len(stage_units(STAGE))
    FIRST = G_FIRST[STAGE]
    if STAGE[0] in ("dnproj", "by", "bg"):
        UNIT_DONE.append(("g_full", FIRST + 1))
    elif STAGE[0] == "up":
        UNIT_DONE.append(("g_full", FIRST + NUMBER - U_FIRST[STAGE] + 1))
    elif NUMBER == U_FIRST[STAGE] + IN_STAGE - 1:
        UNIT_DONE.append(("g_full", FIRST + G_FILLS[STAGE[0]]))
    else:
        USED_AT += 1
        UNIT_DONE.append(("unit_used", USED_AT))

SPLITS_AT = {PLACE: [] for PLACE in range(-1, len(ORDER))}
SPLIT_PLACE = -1
for NUMBER in range(len(UNITS)):
    if NUMBER == RAW_N:
        SPLIT_PLACE = ORDER.index(("dnproj", 0))
    if NUMBER >= HL_N:
        SPLIT_PLACE = max(SPLIT_PLACE, LAST_USE[NUMBER - HL_N])
    SPLITS_AT[SPLIT_PLACE].append(NUMBER)


def encoder_layer(nc, W, out, stop=None, dump=None):
    F, R = mybir.dt.float32, mybir.dt.float32r
    ALU, ACT, AX = mybir.AluOpType, mybir.ActivationFunctionType, mybir.AxisListType
    X = AX.X
    order = ORDER if stop is None else ORDER[:stop]

    ctx = ExitStack()
    with ctx:
        base = (nc.sbuf_base + 31) // 32 * 32
        end = nc.sbuf_usable_end
        at_end = [0]

        def place(name, shape, offset, dt=F):
            size = int(np.prod(shape[1:])) * 4
            at_end[0] = (offset + size + 31) // 32 * 32
            assert base + offset + size <= end, (name, base + offset + size, end)
            return nc.alloc_sbuf_tensor_at(name, shape, dt, offset=base + offset)

        def after(name, shape, dt=F):
            return place(name, shape, at_end[0], dt)

        def signal(name):
            return ctx.enter_context(nc.semaphore(name))

        kept = [k for k in CONST_COLS if k not in EARLY]
        n_const = sum(CONST_COLS[k][1] for k in kept)
        n_late = sum(CONST_COLS[k][1] for k in EARLY)
        cst = place("cst", [P, n_const], 0)
        raw = after("raw", [P, RAW_N, UNIT])
        w_hi = after("w_hi", [P, HL_N, UNIT], R)
        w_lo = after("w_lo", [P, HL_N, UNIT], R)
        pcol = after("pcol", [P, 96])
        fcol = after("fcol", [P, 4 * 2 * FT])
        rowp = after("rowp", [P, 2 * 16 + AH])
        st_x = after("st_x", [P, RT + MT])
        st_a = after("st_a", [P, RT, 10])
        st_m = after("st_m", [P, 24])
        st_d = after("st_d", [P, 2, RT, DH])
        st_o = after("st_o", [P, RT * DH])
        st_s = after("st_s", [P, 8, 4])
        ba = after("ba", [P, RT, 32])
        sp = after("sp", [P, 2, RT, 16])
        ealog = after("ealog", [P, 16])
        g_slot = after("g_slot", [P, NSLOT, DH])
        b_slot = after("b_slot", [P, NSLOT, DH])
        e_slot = after("e_slot", [P, 192])
        tg = after("tg", [P, SEQ])
        hT_hi = after("hT_hi", [P, KT, SEQ], R)
        hT_lo = after("hT_lo", [P, KT, SEQ], R)
        m0 = at_end[0]
        merged = after("merged", [P, KT, SEQ])
        y0 = at_end[0]
        yA_hi = after("yA_hi", [P, 4, SEQ], R)
        yA_lo = after("yA_lo", [P, 4, SEQ], R)
        yM_hi = after("yM_hi", [P, 4, SEQ], R)
        yM_lo = after("yM_lo", [P, 4, SEQ], R)
        a0 = at_end[0]
        xt = place("xt", [P, RT, D], m0)
        dnc = place("dnc", [P, 12, SEQ], m0)
        mkn = place("mkn", [P, MT, MEM_Q], m0 + 28672)
        aqT = place("aqT", [P, 4, SEQ], m0)
        sc = after("sc", [P, 4, 3 * P])
        pT1 = after("pT1", [P, 4, P])
        anat = place("anat", [P, RT, ATTN_Q + ATTN_KV], y0)
        bias = place("bias", [P, AH, 3 * P], y0 + 16384)
        akT = after("akT", [P, AKV, SEQ])
        msc = place("msc", [P, RT, MH, N_MEM], m0)
        mqn = place("mqn", [P, RT, MEM_Q], y0 + 16384)
        mqT = after("mqT", [P, MH, SEQ])
        mx = place("mx", [P, MT, D], a0)
        scr = after("scr", [P, D])
        rows = after("rows", [P, 3, P])
        late = after("late", [P, n_late])
        btab = after("btab", [P, AH])
        bT = after("bT", [P, BIAS_N + 1])
        brev = after("brev", [P, AH, 3 * P])
        w_ba = after("w_ba", [P, KT, 4 * DH])
        dn_nat = place("dn_nat", [P, 3, RT, DN_W], a0)
        qkT = after("qkT", [P, 8, SEQ])
        o_nat = after("o_nat", [P, RT, DN_W])
        S = after("S", [P, 2, 2, 2, DK])
        dec = after("dec", [P, 2, HB, CHUNK])
        nn = after("nn", [P, 2, HB, CHUNK])
        nm = after("nm", [P, 2, 2, HB, CHUNK])
        yx = after("yx", [P, 2, 2, HB, CHUNK])
        wx = after("wx", [P, 2, HB, CHUNK])
        kk = after("kk", [P, 2, HB, CHUNK])
        vn = after("vn", [P, 2, HB, CHUNK])
        at_ = after("at_", [P, 4, HB, CHUNK])
        mkT = after("mkT", [P, MH, N_MEM])
        mv = after("mv", [P, MT, MEM_Q])
        av = after("av", [P, RT, ATTN_KV])
        pT2 = after("pT2", [P, 4, P])
        memT_hi = place("memT_hi", [P, KT, N_MEM], a0 + 49152, R)
        memT_lo = after("memT_lo", [P, KT, N_MEM], R)
        uu = place("uu", [P, 2, HB, CHUNK], a0)
        wt = after("wt", [P, 2, 2, 2, CHUNK])
        ku = after("ku", [P, 2, HB, CHUNK])
        o1 = after("o1", [P, 2, HB, CHUNK])
        zs = place("zs", [P, RT, DN_W], a0 + 24576 + 8192)
        xr = place("xr", [P, RT, D], a0)
        xn = after("xn", [P, RT, D])
        m_hi = after("m_hi", [P, KT, SEQ], R)
        m_lo = after("m_lo", [P, KT, SEQ], R)
        x2 = place("x2", [P, RT, D], m0)
        scr2 = place("scr2", [P, D], a0 + 32768)
        act_hi = place("act_hi", [P, FT, SEQ], y0, R)
        act_lo = after("act_lo", [P, FT, SEQ], R)
        u_gv = after("u_gv", [P, 2, 2, SEQ])
        pTs = [tg[:].rearrange("p (i q) -> p i q", i=4), pT1, pT2]
        mpTs = [tg[:], pT2[:].rearrange("p i q -> p (i q)")]

        gb = [ctx.enter_context(nc.psum_tensor(f"g_bank{i}", [P, 512], F)) for i in range(4)]
        db = [ctx.enter_context(nc.psum_tensor(f"d_bank{i}", [P, 512], F)) for i in range(4)]
        bias_rows = nc.dram_tensor("bias_rows", (AH, BIAS_N + 1), F)

        def const(name, rows=slice(0, P)):
            if name in EARLY:
                first = CONST_COLS[EARLY[0]][0]
                return late[rows, CONST_COLS[name][0] - first:CONST_COLS[name][0] - first + CONST_COLS[name][1]]
            first = CONST_COLS[kept[0]][0]
            return cst[rows, CONST_COLS[name][0] - first:CONST_COLS[name][0] - first + CONST_COLS[name][1]]

        g_full, d_full = signal("g_full"), signal("d_full")
        g_free = [signal(f"g_free{i}") for i in range(4)]
        d_free = [signal(f"d_free{i}") for i in range(4)]
        raw_loaded = [signal(f"raw_loaded{i}") for i in range(RAW_N)]
        hi_made, lo_made, unit_used = signal("hi_made"), signal("lo_made"), signal("unit_used")
        act_step, dve_step, pool_step, pe_step = (signal(n) for n in ("act_step", "dve_step", "pool_step", "pe_step"))
        consts_in, late_in, cols_in, fcols_in, rows_in, ba_in, mem_in = (signal(n) for n in (
            "consts_in", "late_in", "cols_in", "fcols_in", "rows_in", "ba_in", "mem_in"))
        x_in = [signal(f"x_in{t}") for t in range(RT)]
        table_in, bias_out, bias_in, xr_in = signal("table_in"), signal("bias_out"), signal("bias_in"), signal("xr_in")
        stored = signal("stored")
        table_ready, ss_made, sqrt_made, var_made = (signal(n) for n in ("table_ready", "ss_made", "sqrt_made", "var_made"))
        x_scaled, part_hi, tap_made = signal("x_scaled"), signal("part_hi"), signal("tap_made")
        dn_silu, sp_made, softplus_made, beta_made = (signal(n) for n in ("dn_silu", "sp_made", "softplus_made", "beta_made"))
        slots_made, decays_made, a_scaled = signal("slots_made"), signal("decays_made"), signal("a_scaled")
        attn_max, attn_exp, attn_scaled = signal("attn_max"), signal("attn_exp"), signal("attn_scaled")
        mq_scaled, mk_scaled, mem_max, mem_scaled = signal("mq_scaled"), signal("mk_scaled"), signal("mem_max"), signal("mem_scaled")
        dn_scaled, state_zero = signal("dn_scaled"), signal("state_zero")
        b_made, em_made, nm_made, kk_made = signal("b_made"), signal("em_made"), signal("nm_made"), signal("kk_made")
        vn_made, o_added, o_scaled = signal("vn_made"), signal("o_added"), signal("o_scaled")
        gate_used, mhi_made, m_split = (signal(n) for n in ("gate_used", "mhi_made", "m_split"))
        x2_scaled, ua_made, silu_made, glu_made, fhi_made, f_split = (signal(n) for n in ("x2_scaled", "ua_made", "silu_made", "glu_made", "fhi_made", "f_split"))
        SIG = {"g_full": g_full, "unit_used": unit_used}
        PC_MIX, PC_FFN, PC_MEM = DN_TAPS * 12, DN_TAPS * 12 + KT, DN_TAPS * 12 + 2 * KT
        PC_MQ, PC_MK, PC_AQ, PC_AK, PC_DO = (PC_MEM + KT + i for i in range(5))
        N_PC = PC_DO + 1
        FH = 2 * FT
        len_units = sum(len(stage_units(o)) for o in order)

        def level_no(s, hb, l):
            return NTH[("levw", s, hb, l)]

        def f_level(s, hb, l):
            return D_FIRST[("levy" if l else "levw", s, hb, l)]

        NORM = {st: i for i, st in enumerate(st for st in ORDER if st[0] in (
            "xnorm", "mnorm", "dnnorm", "anorm", "mknorm", "mqnorm", "osum", "x2norm"))}

        def heads(ap):
            return ap.rearrange("p (h d) -> p h d", d=64)

        def halves(s):
            return [(hf, 0 if hf == s % 2 else 1, s if hf == s % 2 else NSLOT - 1 - s) for hf in range(2)]

        def decay_of(kind, s, hb, rows=slice(0, P)):
            v = e_slot[rows, 64:192].rearrange("p (k q i h) -> p k q i h", k=2, q=2, i=4)
            return v[:, kind, s % 2, s // 2, HB * hb:HB * hb + HB]

        def unit_view(ring, u):
            _, _, nk, _, nc_ = UNITS[u]
            n = RAW_N if ring is raw else HL_N
            return ring[:, u % n, 0:nk * nc_].rearrange("p (k c) -> p k c", k=nk)

        block = ctx.enter_context(nc.Block())

        @block.sync
        def _(sync):
            for t in range(RT):
                sync.dma_start(xt[:, t, :], W["x"][0, t * P:(t + 1) * P, :]).then_inc(x_in[t], 16)
            sync.dma_start(cst[:], W["consts"][:, n_late:]).then_inc(consts_in, 16)
            at = 0
            for src in ("dn_conv_w", "norm_mix_g", "norm_ffn_g", "mem_norm_g", "mem_q_norm_g", "mem_k_norm_g"):
                v = W[src].rearrange("l k (c p) -> (l k c) p", p=P) if src == "dn_conv_w" else W[src].rearrange("l (c p) -> (l c) p", p=P)
                sync.dma_start(rows[at:at + v.shape[0], 0, :], v).then_inc(cols_in, 16)
                at += v.shape[0]
            for src in ("attn_q_norm_g", "attn_k_norm_g", "dn_out_norm_g"):
                for side in range(2):
                    sync.dma_start(rows[at:at + 1, 0, 64 * side:64 * side + 64], W[src]).then_inc(cols_in, 16)
                at += 1
            def load_units(first, last):
                for u in range(first, last):
                    name, k0, nk, c0, n = UNITS[u]
                    if u >= RAW_N:
                        sync.wait_ge(lo_made, u - RAW_N + 1)
                    src = W[name][0, k0 * P:(k0 + nk) * P, c0:c0 + n].rearrange("(k p) c -> p k c", p=P)
                    sync.dma_start(unit_view(raw, u), src).then_inc(raw_loaded[u % RAW_N], 16)

            done = min(RAW_N, len_units)
            load_units(0, done)
            sync.dma_start(btab[0:BUCKETS, :], W["rel_bias_table"]).then_inc(table_in, 16)
            sync.dma_start(late[:], W["consts"][:, 0:n_late]).then_inc(late_in, 16)
            fw = W["ffn_conv_w"].rearrange("l k (c p) -> (l k c) p", p=P)
            fb = W["ffn_conv_b"].rearrange("l (c p) -> (l c) p", p=P)
            sync.dma_start(rows[0:2 * FH, 1, :], fw[0:2 * FH, :]).then_inc(fcols_in, 16)
            sync.dma_start(rows[0:FH, 2, :], fw[2 * FH:3 * FH, :]).then_inc(fcols_in, 16)
            sync.dma_start(rows[FH:2 * FH, 2, :], fb).then_inc(fcols_in, 16)
            small = (("dn_a_log", 0, 16, "l t h -> l (t h)"), ("dn_dt_bias", 16, 16, "l t h -> l (t h)"), ("attn_sink", 32, AH, None))
            for src, c0, n, how in small:
                v = W[src].rearrange(how) if how else W[src]
                sync.dma_start(rowp[:, c0:c0 + n], v.to_broadcast([P, n])).then_inc(rows_in, 16)
            sync.dma_start(w_ba[:], W["w_in"][0, :, C_BA:C_BA + 4 * DH].rearrange("(k p) c -> p k c", p=P)).then_inc(ba_in, 16)
            sync.dma_start(mx[:], W["mem"][0].rearrange("(t p) d -> p t d", p=P)).then_inc(mem_in, 16)

            for i, st in enumerate(order):
                if st == ("wout", 0):
                    f = D_FIRST[("oT",)] + 3
                    sync.wait_ge(d_free[f % 4], f // 4 + 1)
                    sync.dma_start(xr[:], W["x"][0].rearrange("(t p) d -> p t d", p=P)).then_inc(xr_in, 16)
                ahead = min(len_units, U_FIRST[st] + len(stage_units(st)) + HL_N)
                if ahead > done:
                    load_units(done, ahead)
                    done = ahead
                if st[0] == "bias_a":
                    f = D_FIRST[st]
                    sync.wait_ge(d_free[f % 4], f // 4 + 1)
                    sync.dma_start(bias_rows.ap(), bT[0:AH, :]).then_inc(bias_out, 16)
                    sync.wait_ge(bias_out, 16)
                    band = bass.AP(tensor=bias_rows, offset=0, ap=[[1, P], [BIAS_N + 1, AH], [1, 3 * P]])
                    sync.dma_start(brev[:], band).then_inc(bias_in, 16)
                if st[0] == "down":
                    for rt in range(RT):
                        f = G_FIRST[st] + rt
                        sync.wait_ge(g_free[f % 4], f // 4 + 1)
                        c0 = 512 * st[1]
                        sync.dma_start(out[0, rt * P:(rt + 1) * P, c0:c0 + 512], x2[:, rt, c0:c0 + 512]).then_inc(stored, 16)
                    if st[1] == 1:
                        sync.wait_ge(stored, 16 * 2 * RT)

        @block.tensor
        def _(pe):
            mm = nc.tensor.matmul
            steps = [0]

            def tiles_apart(ins):
                steps[0] += 1
                ins.then_inc(pe_step, 1)
                pe.wait_ge(pe_step, steps[0])

            def d_claim(f):
                if f >= 4:
                    pe.wait_ge(d_free[f % 4], f // 4)
                return db[f % 4]

            def g_claim(f):
                if f >= 4:
                    pe.wait_ge(g_free[f % 4], f // 4)
                return gb[f % 4]

            def evacuated(f):
                pe.wait_ge(d_free[f % 4], f // 4 + 1)

            def arrived(u):
                pe.wait_ge(hi_made, u + 1)
                pe.wait_ge(lo_made, u + 1)

            def transposes(f, sources, width=P):
                bank = d_claim(f)
                for i, src in enumerate(sources):
                    last = nc.tensor.transpose(bank[:, i * width:(i + 1) * width], src, const("ident"))
                last.then_inc(d_full, 1)

            def columns_product(f, u, col, act_hi_, act_lo_, nk, part=0, parts=1):
                bank = g_claim(f) if part == 0 else gb[f % 4]
                if part == 0:
                    arrived(u)
                hi, lo = unit_view(w_hi, u), unit_view(w_lo, u)
                for k in range(nk * part // parts, nk * (part + 1) // parts):
                    for w, a in ((hi, act_hi_), (hi, act_lo_), (lo, act_hi_)):
                        last = mm(bank[:, :], w[:, k, col:col + P], a[:, k, :], start=(k == 0 and w is hi and a is act_hi_),
                                  stop=(k == nk - 1 and w is lo))
                if part == parts - 1:
                    last.then_inc(g_full, 1)

            def rows_product(f, first, act_hi_, act_lo_, tiles=RT, units=None, pieces=None, made=None):
                units = stage_units(st) if units is None else units
                for piece in range(len(units) * tiles) if pieces is None else pieces:
                    j, t = divmod(piece, tiles)
                    _, k0, nk, _, n = units[j]
                    u = first + j
                    bank = g_claim(f + t) if j == 0 else gb[(f + t) % 4]
                    if t == 0:
                        arrived(u)
                        if made is not None:
                            pe.wait_ge(made, k0 + nk)
                    hi, lo = unit_view(w_hi, u), unit_view(w_lo, u)
                    final = j == len(units) - 1
                    for k in range(nk):
                        for a, w in ((act_hi_, hi), (act_hi_, lo), (act_lo_, hi)):
                            last = mm(bank[:, 0:n], a[:, k0 + k, t * P:(t + 1) * P], w[:, k, :],
                                      start=(k0 + k == 0 and a is act_hi_ and w is hi),
                                      stop=(final and k == nk - 1 and a is act_lo_))
                    if final:
                        last.then_inc(g_full, 1)
                    elif t == tiles - 1:
                        last.then_inc(unit_used, 1)

            def small():
                pe.wait_ge(consts_in, 16)
                pe.wait_ge(cols_in, 16 * 12)
                bank = d_claim(D_FIRST[st])
                nc.tensor.transpose(bank[:, 0:N_PC], rows[0:N_PC, 0, :], const("ident", slice(0, N_PC))[:, 0:N_PC]).then_inc(d_full, 1)

            def small_b():
                pe.wait_ge(fcols_in, 16 * 3)
                for i in range(2):
                    bank = d_claim(D_FIRST[st] + i)
                    nc.tensor.transpose(bank[:, 0:2 * FH], rows[0:2 * FH, 1 + i, :], const("ident", slice(0, 2 * FH))[:, 0:2 * FH]).then_inc(d_full, 1)

            def bias_a():
                bank = d_claim(D_FIRST[st])
                pe.wait_ge(table_in, 16)
                pe.wait_ge(late_in, 16)
                pe.wait_ge(table_ready, 1)
                mm(bank[0:AH, 0:BIAS_N + 1], btab[0:BUCKETS + 1, :], const("pick", slice(0, BUCKETS + 1)), start=True, stop=True).then_inc(d_full, 1)

            def bias_b(h):
                pe.wait_ge(bias_in, 16)
                bank = d_claim(D_FIRST[st])
                mm(bank[:, 0:3 * P], const("exchange"), brev[:, h, :], start=True, stop=True).then_inc(d_full, 1)

            def baproj():
                pe.wait_ge(ba_in, 16)
                bank = g_claim(G_FIRST[st])
                for t in range(RT):
                    for k in range(KT):
                        for a in (hT_hi, hT_lo):
                            last = mm(bank[:, 32 * t:32 * t + 32], a[:, k, t * P:(t + 1) * P].bitcast(F), w_ba[:, k, :],
                                      start=(k == 0 and a is hT_hi), stop=(k == KT - 1 and a is hT_lo))
                last.then_inc(g_full, 1)

            def gates_b():
                bank = d_claim(D_FIRST[st])
                pe.wait_ge(slots_made, 1)
                for hf in range(2):
                    rr = slice(64 * hf, 64 * hf + 64)
                    for p in range(2):
                        d = 0 if hf == p else 1
                        for par in range(2):
                            o = (p * 2 + d) * 16
                            last = mm(bank[64 * par:64 * par + 64, o:o + 16].rearrange("p (i h) -> p i h", i=4), const("ones64", rr),
                                      g_slot[rr, p::2, par::2], start=True, stop=True)
                    tiles_apart(last)
                for kind, mask in enumerate(("upto", "after")):
                    for p in range(2):
                        o = 64 + (kind * 2 + p) * 32
                        last = mm(bank[:, o:o + 32].rearrange("p (i h) -> p i h", i=4), const(f"{mask}{p}"), g_slot[:, p::2, :], start=True, stop=True)
                last.then_inc(d_full, 1)

            def attn_s(n, g):
                f, kbs = D_FIRST[st], key_blocks(n)
                lo, hi = kbs[0], kbs[-1] + 1
                evacuated(D_FIRST[("aT",)] + 5)
                for i in range(4):
                    h = 4 * g + i
                    r = slice(64 * (h % 2), 64 * (h % 2) + 64)
                    bank = d_claim(f + i)
                    mm(bank[:, lo * P:hi * P], aqT[r, h // 2, n * P:(n + 1) * P], akT[r, g, (n - 1 + lo) * P:(n - 1 + hi) * P],
                       start=True, stop=True).then_inc(d_full, 1)

            def attn_p(n, g):
                pe.wait_ge(attn_scaled, NTH[st] + 1)
                for j, kb in enumerate(key_blocks(n)):
                    transposes(D_FIRST[st] + j, [sc[:, i, kb * P:(kb + 1) * P] for i in range(4)])

            def attn_o(n, g):
                fo, kbs = D_FIRST[st], key_blocks(n)
                bank = d_claim(fo)
                evacuated(D_FIRST[("attn_p", n, g)] + len(kbs) - 1)
                for par in range(2):
                    for kb in kbs:
                        last = mm(bank[64 * par:64 * par + 64, 0:2 * P].rearrange("p (i q) -> p i q", i=2), av[:, n - 1 + kb, 64 * g:64 * g + 64],
                                  pTs[kb][:, par::2, :], start=(kb == kbs[0]), stop=(kb == kbs[-1]))
                last.then_inc(d_full, 1)

            def mscore(rt):
                evacuated(D_FIRST[("mqT",)] + MH - 1)
                evacuated(D_FIRST[("mkT",)] + 1)
                for j in range(2):
                    bank = d_claim(D_FIRST[st] + j)
                    for i in range(2):
                        h = 2 * j + i
                        last = mm(bank[:, i * N_MEM:(i + 1) * N_MEM], mqT[:, h, rt * P:(rt + 1) * P], mkT[:, h, :], start=True, stop=True)
                    last.then_inc(d_full, 1)

            def mtrans(h):
                pe.wait_ge(mem_scaled, RT)
                for m in range(MT):
                    transposes(D_FIRST[st] + m, [msc[:, rt, h, m * P:(m + 1) * P] for rt in range(RT)])

            def mout(h):
                bank = d_claim(D_FIRST[st])
                evacuated(D_FIRST[("mtrans", h)] + MT - 1)
                for m in range(MT):
                    last = mm(bank[:, :], mv[:, m, h * P:(h + 1) * P], mpTs[m], start=(m == 0), stop=(m == MT - 1))
                last.then_inc(d_full, 1)

            def decay(s, hb):
                f, u = D_FIRST[st], 2 * s + hb
                bank = d_claim(f)
                pe.wait_ge(b_made, u + 1)
                mm(bank[:, 0:HB * CHUNK], const(f"after{s % 2}"), dec[:, 0].rearrange("p h c -> p (h c)"), start=True, stop=True).then_inc(d_full, 1)
                bank = d_claim(f + 1)
                evacuated(D_FIRST[("dnT",)] + 7)
                for i in (0, 2, 1, 3):
                    if i == 1:
                        tiles_apart(last)
                    for hf, _, c in halves(s):
                        h = HB * hb + i
                        r = slice(64 * (h % 2), 64 * (h % 2) + 64)
                        both = qkT[r, :, c * CHUNK:(c + 1) * CHUNK].rearrange("p (j t) n -> p t j n", j=2)[:, h // 2]
                        last = mm(bank[64 * hf:64 * hf + 64, i * 128:(i + 1) * 128].rearrange("p (j n) -> p j n", j=2),
                                  qkT[r, 4 + h // 2, c * CHUNK:(c + 1) * CHUNK], both, start=True, stop=True)
                last.then_inc(d_full, 1)

            def levw(s, hb, l):
                f, b = D_FIRST[st], (2 * s + hb) % 2
                bank = d_claim(f)
                pe.wait_ge(nm_made, level_no(s, hb, l) + 1)
                if l > 0:
                    evacuated(f_level(s, hb, l - 1))
                for i in range(HB):
                    for hf in range(2):
                        r = slice(64 * hf, 64 * hf + 64)
                        rhs = const("ident64", r) if l == 0 else yx[r, b, 1, i, :]
                        last = mm(bank[r, i * CHUNK:(i + 1) * CHUNK], nm[r, b, l % 2, i, :], rhs, start=True, stop=True)
                last.then_inc(d_full, 1)

            def levy(s, hb, l):
                f, b = D_FIRST[st], (2 * s + hb) % 2
                bank = d_claim(f)
                evacuated(D_FIRST[("levw", s, hb, l)])
                for i in range(HB):
                    for hf in range(2):
                        r = slice(64 * hf, 64 * hf + 64)
                        last = mm(bank[r, i * CHUNK:(i + 1) * CHUNK], wx[r, b, i, :], yx[r, b, 0, i, :], start=True, stop=True)
                        if l < LEVELS - 1:
                            last = mm(bank[r, 256 + i * CHUNK:256 + (i + 1) * CHUNK], yx[r, b, 0, i, :], wx[r, b, i, :], start=True, stop=True)
                last.then_inc(d_full, 1)

            def uw(s, hb):
                f, u = D_FIRST[st], 2 * s + hb
                b = u % 2
                bank = d_claim(f)
                evacuated(f_level(s, hb, LEVELS - 1))
                pe.wait_ge(kk_made, u + 1)
                for hf, _, c in halves(s):
                    for i in range(HB):
                        h = HB * hb + i
                        r = slice(64 * hf, 64 * hf + 64)
                        q = slice(64 * (h % 2), 64 * (h % 2) + 64)
                        mm(bank[r, i * CHUNK:(i + 1) * CHUNK], yx[r, b, 0, i, :], dn_nat[r, 2, c // 2, h * 64:h * 64 + 64], start=True, stop=True)
                        o = 256 + (hf * 2 + i // 2) * 64
                        last = mm(bank[q, o:o + 64], kk[r, b, i, :], yx[r, b, 0, i, :], start=True, stop=True)
                    if hf == 0:
                        tiles_apart(last)
                last.then_inc(d_full, 1)

            def scanv(s, hb):
                f, u = D_FIRST[st], 2 * s + hb
                b = u % 2
                bank = d_claim(f)
                evacuated(D_FIRST[("uw", s, hb)])
                if s:
                    evacuated(D_FIRST[("scans", s - 1, hb)])
                else:
                    pe.wait_ge(state_zero, 1)
                for i in (0, 2, 1, 3):
                    if i == 1:
                        tiles_apart(last)
                    for hf, d, c in halves(s):
                        h = HB * hb + i
                        r = slice(64 * hf, 64 * hf + 64)
                        q = slice(64 * (h % 2), 64 * (h % 2) + 64)
                        mm(bank[r, i * 64:i * 64 + 64], wt[q, b, hf, i // 2, :], S[q, hb, d, i // 2, :], start=True, stop=True)
                        last = mm(bank[r, 256 + i * 64:320 + i * 64], qkT[q, h // 2, c * CHUNK:(c + 1) * CHUNK], S[q, hb, d, i // 2, :], start=True, stop=True)
                last.then_inc(d_full, 1)

            def scans(s, hb):
                f, u = D_FIRST[st], 2 * s + hb
                b = u % 2
                bank = d_claim(f)
                pe.wait_ge(vn_made, u + 1)
                for hf, d, c in halves(s):
                    for i in range(HB):
                        h = HB * hb + i
                        r = slice(64 * hf, 64 * hf + 64)
                        q = slice(64 * (h % 2), 64 * (h % 2) + 64)
                        mm(bank[r, i * 64:i * 64 + 64], at_[r, u % 4, i, :], vn[r, b, i, :], start=True, stop=True)
                        o = 256 + (d * 2 + i // 2) * 64
                        last = mm(bank[q, o:o + 64], ku[r, b, i, :], vn[r, b, i, :], start=True, stop=True)
                    if hf == 0:
                        tiles_apart(last)
                last.then_inc(d_full, 1)

            def by(b, c, part):
                u = U_FIRST[("by", b, c - c % 2)]
                y_hi, y_lo = (yM_hi, yM_lo) if b == 1 else (yA_hi, yA_lo)
                if c == 0 and part == 0:
                    evacuated((D_FIRST[("attn_o", RT - 1, AKV - 1)], D_FIRST[("mout", MH - 1)], D_FIRST[("oT",)] + 3)[b])
                columns_product(G_FIRST[("by", b, c)], u, P * (c % 2), y_hi, y_lo, 4, part, PARTS["by"])

            def in_parts(whole, part):
                if whole[0] == "by":
                    by(*whole[1:], part)
                elif whole[0] == "bg":
                    columns_product(G_FIRST[whole], U_FIRST[whole], 0, hT_hi, hT_lo, KT, part, PARTS["bg"])
                else:
                    rows_product(G_FIRST[whole], U_FIRST[whole], hT_hi, hT_lo, units=stage_units(whole), pieces=[part])

            for st in order:
                kind, a = st[0], st[1:]
                f, u = D_FIRST[st], U_FIRST[st]
                if kind == "small":
                    small()
                elif kind == "bias_a":
                    bias_a()
                elif kind == "bias_b":
                    bias_b(*a)
                elif kind == "small_b":
                    small_b()
                elif kind == "baproj":
                    baproj()
                elif kind == "part":
                    in_parts(*a)
                elif kind in PARTS:
                    in_parts(st, PARTS[kind] - 1)
                elif kind == "xT":
                    pe.wait_ge(x_scaled, 1)
                    transposes(f, [xt[:, rt, a[0] * P:(a[0] + 1) * P] for rt in range(RT)])
                elif kind == "mT":
                    pe.wait_ge(x_scaled, 2)
                    transposes(f, [mx[:, m, a[0] * P:(a[0] + 1) * P] for m in range(MT)])
                elif kind == "dnproj":
                    if a[0] == 0:
                        evacuated(D_FIRST[("xT", KT - 1)])
                    columns_product(G_FIRST[st], u, 0, hT_hi, hT_lo, KT)
                elif kind in ("aqproj", "akvproj"):
                    rows_product(G_FIRST[st], u, hT_hi, hT_lo)
                elif kind == "mkvproj":
                    evacuated(D_FIRST[("mT", KT - 1)])
                    rows_product(G_FIRST[st], u, memT_hi, memT_lo, MT)
                elif kind == "gates_b":
                    gates_b()
                elif kind == "dnnat":
                    rt, j = a
                    pe.wait_ge(dn_silu, 4 * j + 4)
                    transposes(f, [dnc[:, 4 * j + t, rt * P:(rt + 1) * P] for t in range(4)])
                elif kind == "aT":
                    pe.wait_ge(a_scaled, 2)
                    for t in range(4):
                        transposes(f + t, [anat[:, rt, t * P:(t + 1) * P] for rt in range(RT)])
                    for g in range(AKV):
                        bank = d_claim(f + 4 + g)
                        for rt in range(RT):
                            for side in range(2):
                                last = mm(bank[64 * side:64 * side + 64, rt * P:(rt + 1) * P], anat[:, rt, ATTN_Q + 64 * g:ATTN_Q + 64 * g + 64],
                                          const("ident"), start=True, stop=True)
                        last.then_inc(d_full, 1)
                elif kind == "attn_s":
                    attn_s(*a)
                elif kind == "attn_p":
                    attn_p(*a)
                elif kind == "attn_o":
                    attn_o(*a)
                elif kind == "mkT":
                    pe.wait_ge(mk_scaled, 1)
                    for j in range(MH // 2):
                        transposes(f + j, [mkn[:, m, (2 * j + i) * P:(2 * j + i + 1) * P] for i in range(2) for m in range(MT)])
                elif kind == "mqT":
                    pe.wait_ge(mq_scaled, 1)
                    for h in range(MH):
                        transposes(f + h, [mqn[:, rt, h * P:(h + 1) * P] for rt in range(RT)])
                elif kind == "mscore":
                    mscore(*a)
                elif kind == "mtrans":
                    mtrans(*a)
                elif kind == "mout":
                    mout(*a)
                elif kind == "dnT":
                    pe.wait_ge(dn_scaled, 2)
                    for j in range(2):
                        for t in range(4):
                            transposes(f + 4 * j + t, [dn_nat[:, j, rt, t * P:(t + 1) * P] for rt in range(RT)])
                elif kind == "decay":
                    decay(*a)
                elif kind == "levw":
                    levw(*a)
                elif kind == "levy":
                    levy(*a)
                elif kind == "uw":
                    uw(*a)
                elif kind == "scanv":
                    scanv(*a)
                elif kind == "scans":
                    scans(*a)
                elif kind == "oT":
                    pe.wait_ge(o_scaled, 1)
                    for t in range(4):
                        transposes(f + t, [o_nat[:, rt, t * P:(t + 1) * P] for rt in range(RT)])
                elif kind == "wout":
                    rows_product(G_FIRST[st], u, m_hi, m_lo, made=m_split)
                elif kind == "h2T":
                    pe.wait_ge(x2_scaled, 1)
                    transposes(f, [xn[:, rt, a[0] * P:(a[0] + 1) * P] for rt in range(RT)])
                elif kind == "up":
                    if a[0] == 0:
                        evacuated(D_FIRST[("h2T", KT - 1)])
                    columns_product(G_FIRST[st], u, 0, hT_hi, hT_lo, KT)
                    columns_product(G_FIRST[st] + 1, u + 1, 0, hT_hi, hT_lo, KT)
                elif kind == "down":
                    rows_product(G_FIRST[st], u, act_hi, act_lo, made=f_split)

        @block.scalar
        def _(act):
            steps = [0]

            def link(ins):
                steps[0] += 1
                ins.then_inc(act_step, 1)
                act.wait_ge(act_step, steps[0])

            def splits(place):
                for u in SPLITS_AT[place]:
                    if u >= len_units:
                        continue
                    act.wait_ge(raw_loaded[u % RAW_N], 16 * (u // RAW_N + 1))
                    if u >= HL_N:
                        name, value = UNIT_DONE[u - HL_N]
                        act.wait_ge(SIG[name], value)
                    nc.scalar.copy(unit_view(w_hi, u), unit_view(raw, u)).then_inc(hi_made, 1)

            def filled(f):
                act.wait_ge(d_full, f + 1)
                return db[f % 4]

            def g_filled(f):
                act.wait_ge(g_full, f + 1)
                return gb[f % 4]

            def root():
                act.wait_ge(var_made, NORM[st] + 1)
                v = {"xnorm": st_x[:, 0:RT], "mnorm": st_x[:, RT:], "anorm": st_a[:, :, AH:] if a == (1,) else st_a[:, :, 0:AH],
                     "mknorm": st_m[:, 16:24], "mqnorm": st_m[:, 0:16], "dnnorm": st_d[:, a[0]] if kind == "dnnorm" else None,
                     "osum": st_o[:], "x2norm": st_x[:, 0:RT]}[kind]
                nc.scalar.activation(v, v, ACT.Sqrt).then_inc(sqrt_made, 1)

            def col(i):
                return pcol[:, i:i + 1]

            def silu_of(c):
                f = G_FIRST[("dnproj", c)]
                act.wait_ge(g_free[f % 4], f // 4 + 1)
                nc.scalar.activation(dnc[:, c, :], dnc[:, c, :], ACT.Silu).then_inc(dn_silu, 1)

            def conv_start(c, half_, b):
                f = G_FIRST[st] + half_
                bank = g_filled(f)
                ct = half_ * FT + c
                if c >= 2:
                    act.wait_ge(f_split, c - 1)
                nc.scalar.activation(u_gv[:, b, half_, :], bank[:, :], ACT.Identity, bias=fcol[:, 3 * 2 * FT + ct:3 * 2 * FT + ct + 1],
                                     scale=fcol[:, 2 * FT + ct:2 * FT + ct + 1]).then_inc(ua_made, 1)

            for place_, st in enumerate(order):
                kind, a = st[0], st[1:]
                f, fg = D_FIRST[st], G_FIRST[st]
                if st == ("xT", 0):
                    splits(-1)
                if kind == "small":
                    nc.scalar.copy(pcol[:, 0:N_PC], filled(f)[:, 0:N_PC]).then_inc(d_free[f % 4], 1)
                elif kind == "small_b":
                    for i in range(2):
                        nc.scalar.copy(fcol[:, i * 2 * FH:(i + 1) * 2 * FH], filled(f + i)[:, 0:2 * FH]).then_inc(d_free[(f + i) % 4], 1)
                elif kind == "xnorm":
                    for t in range(RT):
                        act.wait_ge(x_in[t], 16)
                        ins = nc.scalar.activation(scr[:], xt[:, t, :], ACT.Square, accum_out=st_x[:, t:t + 1])
                        if t == RT - 1:
                            ins.then_inc(ss_made, 1)
                        else:
                            link(ins)
                    root()
                elif kind == "mnorm":
                    act.wait_ge(mem_in, 16)
                    for m in range(MT):
                        ins = nc.scalar.activation(scr[:], mx[:, m, :], ACT.Square, accum_out=st_x[:, RT + m:RT + m + 1])
                        if m == MT - 1:
                            ins.then_inc(ss_made, 1)
                        else:
                            link(ins)
                    root()
                elif kind == "xT":
                    act.wait_ge(d_free[D_FIRST[("small",)] % 4], D_FIRST[("small",)] // 4 + 1)
                    nc.scalar.activation(hT_hi[:, a[0], :], filled(f)[:, :], ACT.Identity, scale=col(PC_MIX + a[0])).then_inc(part_hi, 1)
                elif kind == "mT":
                    nc.scalar.activation(memT_hi[:, a[0], :], filled(f)[:, 0:N_MEM], ACT.Identity, scale=col(PC_MEM + a[0])).then_inc(part_hi, 1)
                elif kind == "bias_a":
                    nc.scalar.copy(bT[0:AH, :], filled(f)[0:AH, 0:BIAS_N + 1]).then_inc(d_free[f % 4], 1)
                elif kind == "bias_b":
                    nc.scalar.copy(bias[:, a[0], :], filled(f)[:, 0:3 * P]).then_inc(d_free[f % 4], 1)
                elif kind == "dnproj":
                    splits(place_)
                    c = a[0]
                    nc.scalar.activation(dnc[:, c, :], g_filled(fg)[:, :], ACT.Identity, scale=col((DN_TAPS // 2) * 12 + c)).then_inc(tap_made, 1)
                    if c:
                        silu_of(c - 1)
                    if c == 11:
                        silu_of(c)
                elif kind == "baproj":
                    nc.scalar.copy(ba[:].rearrange("p t c -> p (t c)"), g_filled(fg)[:, 0:32 * RT]).then_inc(g_free[fg % 4], 1)
                elif kind == "zproj":
                    splits(place_)
                    for rt in range(RT):
                        nc.scalar.activation(zs[:, rt, :], g_filled(fg + rt)[:, :], ACT.Silu).then_inc(g_free[(fg + rt) % 4], 1)
                elif kind == "gates_a":
                    act.wait_ge(sp_made, 1)
                    link(nc.scalar.activation(sp[:, 1], sp[:, 0], ACT.Abs))
                    link(nc.scalar.activation(sp[:, 1], sp[:, 1], ACT.Exp, scale=-1.0))
                    link(nc.scalar.activation(ealog[:], rowp[:, 0:16], ACT.Exp))
                    nc.scalar.activation(sp[:, 1], sp[:, 1], ACT.Ln, bias=1.0).then_inc(softplus_made, 1)
                    act.wait_ge(sp_made, 2)
                    nc.scalar.activation(sp[:, 1], ba[:, :, 0:16], ACT.Sigmoid).then_inc(beta_made, 1)
                elif kind == "gates_b":
                    nc.scalar.activation(e_slot[:], filled(f)[:, 0:192], ACT.Exp).then_inc(d_free[f % 4], 1)
                elif kind == "aqproj":
                    splits(place_)
                    for rt in range(RT):
                        nc.scalar.copy(anat[:, rt, 0:ATTN_Q], g_filled(fg + rt)[:, :]).then_inc(g_free[(fg + rt) % 4], 1)
                elif kind == "akvproj":
                    splits(place_)
                    for rt in range(RT):
                        bank = g_filled(fg + rt)
                        nc.scalar.copy(anat[:, rt, ATTN_Q:], bank[:, 0:ATTN_KV])
                        nc.scalar.copy(av[:, rt, :], bank[:, ATTN_KV:2 * ATTN_KV]).then_inc(g_free[(fg + rt) % 4], 1)
                elif kind in ("anorm", "mknorm", "mqnorm", "dnnorm", "osum"):
                    root()
                elif kind == "dnnat":
                    nc.scalar.copy(dn_nat[:, a[1], a[0], :], filled(f)[:, :]).then_inc(d_free[f % 4], 1)
                elif kind == "aT":
                    for t in range(4):
                        nc.scalar.activation(aqT[:, t, :], filled(f + t)[:, :], ACT.Identity, scale=col(PC_AQ)).then_inc(d_free[(f + t) % 4], 1)
                    for g in range(AKV):
                        nc.scalar.activation(akT[:, g, :], filled(f + 4 + g)[:, :], ACT.Identity, scale=col(PC_AK)).then_inc(d_free[(f + 4 + g) % 4], 1)
                elif kind == "attn_e":
                    n, g = a
                    kbs = key_blocks(n)
                    lo, hi = kbs[0] * P, (kbs[-1] + 1) * P
                    act.wait_ge(attn_max, NTH[st] + 1)
                    nc.scalar.activation(st_s[:, 5, :], st_s[:, 3, :], ACT.Exp)
                    for i in range(4):
                        ins = nc.scalar.activation(sc[:, i, lo:hi], sc[:, i, lo:hi], ACT.Exp, bias=st_s[:, 2, i:i + 1], accum_out=st_s[:, 4, i:i + 1])
                    ins.then_inc(attn_exp, 1)
                elif kind == "attn_p":
                    for j, kb in enumerate(key_blocks(a[0])):
                        nc.scalar.copy(pTs[kb].rearrange("p i q -> p (i q)"), filled(f + j)[:, :]).then_inc(d_free[(f + j) % 4], 1)
                elif kind == "attn_o":
                    n, g = a
                    nc.scalar.copy(yA_hi[:, 2 * g:2 * g + 2, n * P:(n + 1) * P], filled(f)[:, 0:2 * P].rearrange("p (i q) -> p i q", i=2)).then_inc(part_hi, 1)
                elif kind == "mqproj":
                    splits(place_)
                    for rt in range(RT):
                        nc.scalar.copy(mqn[:, rt, :], g_filled(fg + rt)[:, :]).then_inc(g_free[(fg + rt) % 4], 1)
                elif kind == "mkvproj":
                    splits(place_)
                    for m in range(MT):
                        dst = mv if a[0] else mkn
                        nc.scalar.copy(dst[:, m, :], g_filled(fg + m)[:, :]).then_inc(g_free[(fg + m) % 4], 1)
                elif kind == "mqT":
                    for h in range(MH):
                        nc.scalar.activation(mqT[:, h, :], filled(f + h)[:, :], ACT.Identity, scale=col(PC_MQ)).then_inc(d_free[(f + h) % 4], 1)
                elif kind == "mkT":
                    for j in range(MH // 2):
                        nc.scalar.activation(mkT[:, 2 * j:2 * j + 2, :], filled(f + j)[:, :].rearrange("p (h m) -> p h m", h=2), ACT.Identity, scale=col(PC_MK)).then_inc(d_free[(f + j) % 4], 1)
                elif kind == "mexp":
                    rt = a[0]
                    fs = D_FIRST[("mscore", rt)]
                    for j in range(2):
                        act.wait_ge(mem_max, 2 * rt + j + 1)
                        bank = filled(fs + j)
                        for i in range(2):
                            h = 2 * j + i
                            ins = nc.scalar.activation(msc[:, rt, h, :], bank[:, i * N_MEM:(i + 1) * N_MEM], ACT.Exp, bias=st_s[:, 6, h:h + 1], accum_out=st_s[:, 7, h:h + 1])
                        ins.then_inc(d_free[(fs + j) % 4], 1)
                elif kind == "mtrans":
                    for m in range(MT):
                        nc.scalar.copy(mpTs[m], filled(f + m)[:, :]).then_inc(d_free[(f + m) % 4], 1)
                elif kind == "mout":
                    nc.scalar.copy(yM_hi[:, a[0], :], filled(f)[:, :]).then_inc(part_hi, 1)
                elif kind == "dnT":
                    for j in range(8):
                        nc.scalar.copy(qkT[:, j, :], filled(f + j)[:, :]).then_inc(d_free[(f + j) % 4], 1)
                elif kind == "decay":
                    u = 2 * a[0] + a[1]
                    if u:
                        fu = D_FIRST[("decay",) + divmod(u - 1, 2)] + 1
                        act.wait_ge(d_free[fu % 4], fu // 4 + 1)
                    nc.scalar.activation(dec[:, 0].rearrange("p h c -> p (h c)"), filled(f)[:, 0:HB * CHUNK], ACT.Exp).then_inc(d_free[f % 4], 1)
                elif kind == "levw":
                    if a[2]:
                        nc.scalar.copy(wx[:, (2 * a[0] + a[1]) % 2].rearrange("p h c -> p (h c)"), filled(f)[:, 0:HB * CHUNK]).then_inc(d_free[f % 4], 1)
                elif kind in ("by", "part"):
                    splits(place_)
                elif kind == "bg":
                    splits(place_)
                    b, c = a
                    dst = merged[:, c, :] if b == 0 else tg[:]
                    if b and NTH[st] > KT:
                        act.wait_ge(gate_used, NTH[st] - KT)
                    nc.scalar.activation(dst, g_filled(fg)[:, :], ACT.Tanh, scale=0.5).then_inc(g_free[fg % 4], 1)
                    if b == 2:
                        act.wait_ge(gate_used, NTH[st] + 1 - KT)
                        nc.scalar.mul(m_hi[:, c, :], merged[:, c, :], 0.5).then_inc(mhi_made, 1)
                elif kind == "oT":
                    for t in range(4):
                        nc.scalar.activation(yA_hi[:, t, :], filled(f + t)[:, :], ACT.Identity, scale=col(PC_DO)).then_inc(part_hi, 1)
                elif kind == "wout":
                    splits(place_)
                elif kind == "x2norm":
                    fo = G_FIRST[("wout", 1)] + RT - 1
                    for b4 in range(4):
                        act.wait_ge(g_free[b4], (fo + 1 - b4 + 3) // 4)
                    for t in range(RT):
                        ins = nc.scalar.activation(scr2[:], x2[:, t, :], ACT.Square, accum_out=st_x[:, t:t + 1])
                        if t == RT - 1:
                            ins.then_inc(ss_made, 1)
                        else:
                            link(ins)
                    root()
                elif kind == "h2T":
                    nc.scalar.activation(hT_hi[:, a[0], :], filled(f)[:, :], ACT.Identity, scale=col(PC_FFN + a[0])).then_inc(part_hi, 1)
                elif kind == "up":
                    splits(place_)
                    c = a[0]
                    conv_start(c, 0, c % 2)
                    conv_start(c, 1, c % 2)
                    act.wait_ge(g_free[fg % 4], fg // 4 + 1)
                    nc.scalar.activation(u_gv[:, c % 2, 0, :], u_gv[:, c % 2, 0, :], ACT.Silu).then_inc(silu_made, 1)
                    act.wait_ge(glu_made, c + 1)
                    nc.scalar.copy(act_hi[:, c, :], u_gv[:, c % 2, 1, :]).then_inc(fhi_made, 1)
                elif kind == "down":
                    splits(place_)

        @block.vector
        def _(dve):
            v = nc.vector
            steps = [0]

            def link(ins):
                steps[0] += 1
                ins.then_inc(dve_step, 1)
                dve.wait_ge(dve_step, steps[0])

            def splits(place):
                for u in SPLITS_AT[place]:
                    if u >= len_units:
                        continue
                    dve.wait_ge(hi_made, u + 1)
                    v.tensor_tensor(unit_view(w_lo, u), unit_view(raw, u), unit_view(w_hi, u).bitcast(F), ALU.subtract).then_inc(lo_made, 1)

            def filled(f):
                dve.wait_ge(d_full, f + 1)
                return db[f % 4]

            def g_filled(f):
                dve.wait_ge(g_full, f + 1)
                return gb[f % 4]

            def inverse_root(stat, n_mean, after_squares=True):
                v.tensor_scalar(stat, stat, 1.0 / n_mean, EPS, ALU.mult, ALU.add).then_inc(var_made, 1)
                dve.wait_ge(sqrt_made, NORM[st] + 1)
                link(v.reciprocal(stat, stat))

            def squares(dst, src, width, d=64, room=None):
                room = tg if room is None else room
                link(v.tensor_tensor(room[:, 0:width], src, src, ALU.mult))
                link(v.tensor_reduce(dst, room[:, 0:width].rearrange("p (h d) -> p h d", d=d), X, ALU.add))

            def g_evacuated(f):
                dve.wait_ge(g_free[f % 4], f // 4 + 1)

            def low_part(dst, bank, hi, scale=None):
                if scale is None:
                    return v.tensor_tensor(dst, bank, hi.bitcast(F), ALU.subtract)
                return v.scalar_tensor_tensor(dst, bank, scale, hi.bitcast(F), ALU.mult, ALU.subtract)

            def col(i):
                return pcol[:, i:i + 1]

            def wide(ap, n=64):
                return ap.unsqueeze(len(ap.shape)).to_broadcast(list(ap.shape) + [n])

            his = [0]

            def hi_part():
                his[0] += 1
                dve.wait_ge(part_hi, his[0])

            v.memset(btab[BUCKETS:BUCKETS + 1, :], NEG).then_inc(table_ready, 1)
            for place_, st in enumerate(order):
                kind, a = st[0], st[1:]
                f, fg = D_FIRST[st], G_FIRST[st]
                if st == ("xT", 0):
                    splits(-1)
                if kind == "xnorm":
                    dve.wait_ge(ss_made, 1)
                    inverse_root(st_x[:, 0:RT], D)
                    for t in range(RT):
                        ins = v.tensor_scalar(xt[:, t, :], xt[:, t, :], st_x[:, t:t + 1], None, ALU.mult)
                    ins.then_inc(x_scaled, 1)
                elif kind == "mnorm":
                    dve.wait_ge(ss_made, 2)
                    inverse_root(st_x[:, RT:], D)
                    for m in range(MT):
                        ins = v.tensor_scalar(mx[:, m, :], mx[:, m, :], st_x[:, RT + m:RT + m + 1], None, ALU.mult)
                    ins.then_inc(x_scaled, 1)
                elif kind == "xT":
                    dve.wait_ge(d_free[D_FIRST[("small",)] % 4], D_FIRST[("small",)] // 4 + 1)
                    hi_part()
                    low_part(hT_lo[:, a[0], :], filled(f)[:, :], hT_hi[:, a[0], :], col(PC_MIX + a[0])).then_inc(d_free[f % 4], 1)
                elif kind == "mT":
                    hi_part()
                    low_part(memT_lo[:, a[0], :], filled(f)[:, 0:N_MEM], memT_hi[:, a[0], :], col(PC_MEM + a[0])).then_inc(d_free[f % 4], 1)
                elif kind == "dnproj":
                    splits(place_)
                    c = a[0]
                    bank = g_filled(fg)
                    dve.wait_ge(tap_made, c + 1)
                    for j in (0, 1, 3, 4):
                        d = j - DN_TAPS // 2
                        lo, hi = max(0, -d), SEQ - max(0, d)
                        y = dnc[:, c, lo:hi]
                        ins = v.scalar_tensor_tensor(y, bank[:, lo + d:hi + d], col(j * 12 + c), y, ALU.mult, ALU.add)
                        if j == 4:
                            ins.then_inc(g_free[fg % 4], 1)
                        else:
                            link(ins)
                elif kind in ("zproj", "aqproj", "akvproj", "mqproj", "mkvproj", "by", "part"):
                    splits(place_)
                elif kind == "gates_a":
                    g_evacuated(G_FIRST[("baproj",)])
                    dve.wait_ge(rows_in, 16 * 3)
                    dt = rowp[:, 16:32].unsqueeze(1).to_broadcast([P, RT, 16])
                    v.tensor_tensor(sp[:, 0], ba[:, :, 16:32], dt, ALU.add).then_inc(sp_made, 1)
                    dve.wait_ge(softplus_made, 1)
                    link(v.scalar_tensor_tensor(sp[:, 0], sp[:, 0], 0.0, sp[:, 1], ALU.max, ALU.add))
                    v.scalar_tensor_tensor(sp[:, 0], sp[:, 0], -1.0, ealog[:].unsqueeze(1).to_broadcast([P, RT, 16]), ALU.mult, ALU.mult).then_inc(sp_made, 1)
                    dve.wait_ge(sp_made, 2)
                    dve.wait_ge(beta_made, 1)
                    for src, dst in ((sp[:, 1], b_slot), (sp[:, 0], g_slot)):
                        for hf in range(2):
                            r = slice(64 * hf, 64 * hf + 64)
                            v.tensor_copy(dst[r, hf::2, :], src[r, :, 0:8])
                            for i in range(RT):
                                ins = v.tensor_copy(dst[r, 2 * i + 1 - hf, :], src[r, RT - 1 - i, 8:16])
                    ins.then_inc(slots_made, 1)
                elif kind == "anorm":
                    cols, hh = ((slice(0, ATTN_Q), slice(0, AH)), (slice(ATTN_Q, ATTN_Q + ATTN_KV), slice(AH, AH + AKV)))[a[0]]
                    for rt in range(RT):
                        g_evacuated(G_FIRST[("akvproj",) if a[0] else ("aqproj",)] + rt)
                    for rt in range(RT):
                        squares(st_a[:, rt, hh], anat[:, rt, cols], cols.stop - cols.start)
                    inverse_root(st_a[:, :, hh], AD)
                    if a[0] == 0:
                        link(v.tensor_scalar(st_a[:, :, hh], st_a[:, :, hh], AD ** -0.5, None, ALU.mult))
                    for rt in range(RT):
                        x3 = heads(anat[:, rt, cols])
                        ins = v.tensor_tensor(x3, x3, wide(st_a[:, rt, hh]), ALU.mult)
                    ins.then_inc(a_scaled, 1)
                elif kind == "attn_s":
                    n, g = a
                    kbs = key_blocks(n)
                    lo, hi = kbs[0] * P, (kbs[-1] + 1) * P
                    fb = D_FIRST[("bias_b", AH - 1)]
                    dve.wait_ge(d_free[fb % 4], fb // 4 + 1)
                    if NTH[st]:
                        prev = ("attn_p",) + divmod(NTH[st] - 1, AKV)
                        dve.wait_ge(d_full, D_FIRST[prev] + d_fills(prev))
                    for i in range(4):
                        bank = filled(f + i)
                        v.tensor_tensor(sc[:, i, lo:hi], bank[:, lo:hi], bias[:, 4 * g + i, lo:hi], ALU.add).then_inc(d_free[(f + i) % 4], 1)
                    for i in range(4):
                        dve.wait_ge(d_free[(f + i) % 4], (f + i) // 4 + 1)
                    sink = rowp[:, 32 + 4 * g:36 + 4 * g]
                    link(v.tensor_reduce(st_s[:, 0, :], sc[:, :, lo:hi], X, ALU.max))
                    link(v.tensor_tensor(st_s[:, 1, :], st_s[:, 0, :], sink, ALU.max))
                    link(v.tensor_scalar(st_s[:, 2, :], st_s[:, 1, :], -1.0, None, ALU.mult))
                    v.tensor_tensor(st_s[:, 3, :], sink, st_s[:, 2, :], ALU.add).then_inc(attn_max, 1)
                elif kind == "attn_t":
                    kbs = key_blocks(a[0])
                    lo, hi = kbs[0] * P, (kbs[-1] + 1) * P
                    dve.wait_ge(attn_exp, NTH[st] + 1)
                    link(v.tensor_tensor(st_s[:, 4, :], st_s[:, 4, :], st_s[:, 5, :], ALU.add))
                    link(v.reciprocal(st_s[:, 4, :], st_s[:, 4, :]))
                    for i in range(4):
                        ins = v.tensor_scalar(sc[:, i, lo:hi], sc[:, i, lo:hi], st_s[:, 4, i:i + 1], None, ALU.mult)
                    ins.then_inc(attn_scaled, 1)
                elif kind == "attn_o":
                    n, g = a
                    hi_part()
                    dst = slice(n * P, (n + 1) * P)
                    low_part(yA_lo[:, 2 * g:2 * g + 2, dst], filled(f)[:, 0:2 * P].rearrange("p (i q) -> p i q", i=2),
                             yA_hi[:, 2 * g:2 * g + 2, dst]).then_inc(d_free[f % 4], 1)
                elif kind == "mknorm":
                    for m in range(MT):
                        g_evacuated(G_FIRST[("mkvproj", 0)] + m)
                    for m in range(MT):
                        squares(st_m[:, 16 + 4 * m:20 + 4 * m], mkn[:, m, :], 512, MD)
                    inverse_root(st_m[:, 16:24], MD)
                    for m in range(MT):
                        x3 = mkn[:, m, :].rearrange("p (h d) -> p h d", d=MD)
                        ins = v.tensor_tensor(x3, x3, wide(st_m[:, 16 + 4 * m:20 + 4 * m], MD), ALU.mult)
                    ins.then_inc(mk_scaled, 1)
                elif kind == "mqnorm":
                    for rt in range(RT):
                        g_evacuated(G_FIRST[("mqproj",)] + rt)
                    for rt in range(RT):
                        squares(st_m[:, 4 * rt:4 * rt + 4], mqn[:, rt, :], 512, MD)
                    inverse_root(st_m[:, 0:16], MD)
                    link(v.tensor_scalar(st_m[:, 0:16], st_m[:, 0:16], MD ** -0.5, None, ALU.mult))
                    for rt in range(RT):
                        x3 = mqn[:, rt, :].rearrange("p (h d) -> p h d", d=MD)
                        ins = v.tensor_tensor(x3, x3, wide(st_m[:, 4 * rt:4 * rt + 4], MD), ALU.mult)
                    ins.then_inc(mq_scaled, 1)
                elif kind == "mscore":
                    for j in range(2):
                        h2 = slice(2 * j, 2 * j + 2)
                        link(v.tensor_reduce(st_s[:, 0, h2], filled(f + j)[:, :].rearrange("p (h m) -> p h m", h=2), X, ALU.max))
                        v.tensor_scalar(st_s[:, 6, h2], st_s[:, 0, h2], -1.0, None, ALU.mult).then_inc(mem_max, 1)
                elif kind == "mscale":
                    rt = a[0]
                    fs = D_FIRST[("mscore", rt)] + 1
                    dve.wait_ge(d_free[fs % 4], fs // 4 + 1)
                    link(v.reciprocal(st_s[:, 7, :], st_s[:, 7, :]))
                    for h in range(MH):
                        ins = v.tensor_scalar(msc[:, rt, h, :], msc[:, rt, h, :], st_s[:, 7, h:h + 1], None, ALU.mult)
                    ins.then_inc(mem_scaled, 1)
                elif kind == "mout":
                    hi_part()
                    low_part(yM_lo[:, a[0], :], filled(f)[:, :], yM_hi[:, a[0], :]).then_inc(d_free[f % 4], 1)
                elif kind == "dnnorm":
                    j = a[0]
                    fn = D_FIRST[("dnnat", RT - 1, j)]
                    for b4 in range(4):
                        dve.wait_ge(d_free[(fn - b4) % 4], (fn - b4) // 4 + 1)
                    for rt in range(RT):
                        squares(st_d[:, j, rt, :], dn_nat[:, j, rt, :], DN_W)
                    inverse_root(st_d[:, j], 1)
                    if j == 0:
                        link(v.tensor_scalar(st_d[:, 0], st_d[:, 0], DK ** -0.5, None, ALU.mult))
                    for rt in range(RT):
                        x3 = heads(dn_nat[:, j, rt, :])
                        ins = v.tensor_tensor(x3, x3, wide(st_d[:, j, rt, :]), ALU.mult)
                    ins.then_inc(dn_scaled, 1)
                elif kind == "dnT":
                    dve.wait_ge(d_full, f + 1)
                    v.memset(S[:].rearrange("p a b c d -> p (a b c d)"), 0.0).then_inc(state_zero, 1)
                elif kind == "decay":
                    s, hb = a
                    u = 2 * s + hb
                    bank = filled(f + 1)[:, :].rearrange("p (h j n) -> p h j n", h=HB, j=2)
                    dve.wait_ge(em_made, u + 1)
                    v.tensor_tensor(at_[:, u % 4], bank[:, :, 0, :], dec[:, 0], ALU.mult)
                    v.tensor_tensor(nn[:, u % 2], bank[:, :, 1, :], dec[:, 1], ALU.mult).then_inc(d_free[(f + 1) % 4], 1)
                elif kind == "levw":
                    s, hb, l = a
                    b = (2 * s + hb) % 2
                    if l == 0:
                        eye = const("ident64").unsqueeze(1).to_broadcast([P, HB, CHUNK])
                        dve.wait_ge(nm_made, level_no(s, hb, 0) + 1)
                        v.tensor_tensor(yx[:, b, 0], eye, nm[:, b, 0], ALU.subtract)
                        v.tensor_tensor(yx[:, b, 1], eye, heads(filled(f)[:, 0:HB * CHUNK]), ALU.subtract).then_inc(d_free[f % 4], 1)
                elif kind == "levy":
                    s, hb, l = a
                    b = (2 * s + hb) % 2
                    n = 2 if l < LEVELS - 1 else 1
                    y = yx[:, b].rearrange("p a h c -> p (a h c)")[:, 0:n * HB * CHUNK]
                    fl = f_level(s, hb, l - 1)
                    dve.wait_ge(d_free[fl % 4], fl // 4 + 1)
                    v.tensor_tensor(y, y, filled(f)[:, 0:n * HB * CHUNK], ALU.subtract).then_inc(d_free[f % 4], 1)
                elif kind == "uw":
                    s, hb = a
                    b = (2 * s + hb) % 2
                    bank = filled(f)
                    v.tensor_tensor(uu[:, b], heads(bank[:, 0:256]), wide(b_slot[:, s, HB * hb:HB * hb + HB]), ALU.mult)
                    v.tensor_copy(wt[:, b].rearrange("p a i c -> p (a i c)"), bank[:, 256:512]).then_inc(d_free[f % 4], 1)
                elif kind == "scanv":
                    s, hb = a
                    b = (2 * s + hb) % 2
                    bank = filled(f)
                    fu = D_FIRST[("uw", s, hb)]
                    dve.wait_ge(d_free[fu % 4], fu // 4 + 1)
                    link(v.tensor_tensor(vn[:, b], heads(bank[:, 0:256]), wide(b_slot[:, s, HB * hb:HB * hb + HB]), ALU.mult))
                    v.tensor_tensor(vn[:, b], uu[:, b], vn[:, b], ALU.subtract).then_inc(vn_made, 1)
                    if s:
                        dve.wait_ge(o_added, 2 * (s - 1) + hb + 1)
                    v.tensor_tensor(o1[:, b], heads(bank[:, 256:512]), wide(decay_of(0, s, hb)), ALU.mult).then_inc(d_free[f % 4], 1)
                elif kind == "scans":
                    s, hb = a
                    b = (2 * s + hb) % 2
                    fv = D_FIRST[("scanv", s, hb)]
                    dve.wait_ge(d_free[fv % 4], fv // 4 + 1)
                    egl = e_slot[:, 0:64].rearrange("p (q d i h) -> p q d i h", q=2, d=2, i=4)[:, s % 2, :, s // 2, 2 * hb:2 * hb + 2]
                    link(v.tensor_tensor(S[:, hb], S[:, hb], wide(egl), ALU.mult))
                    bank = filled(f)
                    link(v.tensor_tensor(o1[:, b], o1[:, b], heads(bank[:, 0:256]), ALU.add))
                    s_flat = S[:, hb].rearrange("p d i n -> p (d i n)")
                    v.tensor_tensor(s_flat, s_flat, bank[:, 256:512], ALU.add).then_inc(d_free[f % 4], 1)
                elif kind == "bg":
                    splits(place_)
                    b, c = a
                    fy = G_FIRST[("by", b, c)]
                    yb = g_filled(fy)
                    g_evacuated(fg)
                    if b == 0:
                        v.scalar_tensor_tensor(merged[:, c, :], merged[:, c, :], 1.0, yb[:, :], ALU.add, ALU.mult).then_inc(g_free[fy % 4], 1)
                    else:
                        v.scalar_tensor_tensor(tg[:], tg[:], 1.0, yb[:, :], ALU.add, ALU.mult).then_inc(g_free[fy % 4], 1)
                        g_evacuated(fy)
                        v.tensor_tensor(merged[:, c, :], merged[:, c, :], tg[:], ALU.add).then_inc(gate_used, 1)
                        if b == 2:
                            dve.wait_ge(mhi_made, c + 1)
                            v.scalar_tensor_tensor(m_lo[:, c, :], merged[:, c, :], 0.5, m_hi[:, c, :].bitcast(F), ALU.mult, ALU.subtract).then_inc(m_split, 1)
                elif kind == "osum":
                    dve.wait_ge(o_added, 2 * NSLOT)
                    for rt in range(RT):
                        squares(st_o[:, DH * rt:DH * rt + DH], o_nat[:, rt, :], DN_W, room=at_[:].rearrange("p a h c -> p (a h c)"))
                    inverse_root(st_o[:], DK)
                    for rt in range(RT):
                        x3 = heads(o_nat[:, rt, :])
                        link(v.tensor_tensor(x3, x3, wide(st_o[:, DH * rt:DH * rt + DH]), ALU.mult))
                        ins = v.tensor_tensor(o_nat[:, rt, :], o_nat[:, rt, :], zs[:, rt, :], ALU.mult)
                    ins.then_inc(o_scaled, 1)
                elif kind == "oT":
                    for t in range(4):
                        hi_part()
                        low_part(yA_lo[:, t, :], filled(f + t)[:, :], yA_hi[:, t, :], col(PC_DO)).then_inc(d_free[(f + t) % 4], 1)
                elif kind == "wout":
                    splits(place_)
                    dve.wait_ge(xr_in, 16)
                    cc = slice(512 * a[0], 512 * a[0] + 512)
                    for rt in range(RT):
                        v.tensor_tensor(x2[:, rt, cc], g_filled(fg + rt)[:, :], xr[:, rt, cc], ALU.add).then_inc(g_free[(fg + rt) % 4], 1)
                elif kind == "x2norm":
                    dve.wait_ge(ss_made, 3)
                    inverse_root(st_x[:, 0:RT], D)
                    for t in range(RT):
                        ins = v.tensor_scalar(xn[:, t, :], x2[:, t, :], st_x[:, t:t + 1], None, ALU.mult)
                    ins.then_inc(x2_scaled, 1)
                elif kind == "h2T":
                    hi_part()
                    low_part(hT_lo[:, a[0], :], filled(f)[:, :], hT_hi[:, a[0], :], col(PC_FFN + a[0])).then_inc(d_free[f % 4], 1)
                elif kind == "up":
                    splits(place_)
                    c = a[0]
                    for half_ in range(2):
                        ct = half_ * FT + c
                        bank = g_filled(fg + half_)
                        dve.wait_ge(ua_made, 2 * c + half_ + 1)
                        y = u_gv[:, c % 2, half_, :]
                        link(v.scalar_tensor_tensor(y[:, 1:SEQ], bank[:, 0:SEQ - 1], fcol[:, ct:ct + 1], y[:, 1:SEQ], ALU.mult, ALU.add))
                        v.scalar_tensor_tensor(y[:, 0:SEQ - 1], bank[:, 1:SEQ], fcol[:, 4 * FT + ct:4 * FT + ct + 1], y[:, 0:SEQ - 1], ALU.mult, ALU.add).then_inc(g_free[(fg + half_) % 4], 1)
                    dve.wait_ge(silu_made, c + 1)
                    dve.wait_ge(g_free[(fg + 1) % 4], (fg + 1) // 4 + 1)
                    uv = u_gv[:, c % 2, 1, :]
                    v.tensor_tensor(uv, uv, u_gv[:, c % 2, 0, :], ALU.mult).then_inc(glu_made, 1)
                    dve.wait_ge(fhi_made, c + 1)
                    v.tensor_tensor(act_lo[:, c, :], uv, act_hi[:, c, :].bitcast(F), ALU.subtract).then_inc(f_split, 1)
                elif kind == "down":
                    splits(place_)
                    cc = slice(512 * a[0], 512 * a[0] + 512)
                    for rt in range(RT):
                        v.tensor_tensor(x2[:, rt, cc], x2[:, rt, cc], g_filled(fg + rt)[:, :], ALU.add).then_inc(g_free[(fg + rt) % 4], 1)

        @block.gpsimd
        def _(pool):
            g_ = nc.gpsimd
            steps = [0]
            before = {}

            def link(ins):
                steps[0] += 1
                ins.then_inc(pool_step, 1)
                pool.wait_ge(pool_step, steps[0])

            def say(ins, made):
                before[made.name] = before.get(made.name, 0) + 1
                ins.then_inc(made, 1)
                pool.wait_ge(made, before[made.name])

            def wide(ap, n=64):
                return ap.unsqueeze(len(ap.shape)).to_broadcast(list(ap.shape) + [n])

            def four(ap):
                return ap.unsqueeze(1).to_broadcast([ap.shape[0], HB, CHUNK])

            def add_output(s, hb):
                b = (2 * s + hb) % 2
                f = D_FIRST[("scans", s, hb)]
                pool.wait_ge(d_free[f % 4], f // 4 + 1)
                for hf, _, c in halves(s):
                    r = slice(64 * hf, 64 * hf + 64)
                    dst = heads(o_nat[r, c // 2, 256 * hb:256 * hb + 256])
                    if s < NSLOT // 2:
                        ins = g_.tensor_copy(dst, o1[r, b])
                    else:
                        ins = g_.tensor_tensor(dst, dst, o1[r, b], ALU.add)
                    if hf == 0:
                        link(ins)
                say(ins, o_added)

            for st in order:
                kind, a = st[0], st[1:]
                f = D_FIRST[st]
                if kind == "levw" and a[0] > 0 and a[2] == 3:
                    add_output(a[0] - 1, a[1])
                if kind == "scans" and a[0] == NSLOT - 1:
                    add_output(*a)
                if kind == "decay":
                    s, hb = a
                    u = 2 * s + hb
                    mine = slice(HB * hb, HB * hb + HB)
                    if u == 0:
                        pool.wait_ge(slots_made, 1)
                        pool.wait_ge(d_full, D_FIRST[("dnT",)] + 1)
                    else:
                        fu = D_FIRST[("decay",) + divmod(u - 1, 2)] + 1
                        pool.wait_ge(d_free[fu % 4], fu // 4 + 1)
                    say(g_.tensor_tensor(dec[:, 0], wide(g_slot[:, s, mine]), four(const(f"incl{s % 2}")), ALU.mult), b_made)
                    link(g_.tensor_tensor(dec[:, 1], wide(b_slot[:, s, mine]), four(const(f"strict{s % 2}")), ALU.mult))
                    pool.wait_ge(d_free[f % 4], f // 4 + 1)
                    link(g_.tensor_tensor(dec[:, 0], dec[:, 0], four(const(f"incl{s % 2}")), ALU.mult))
                    say(g_.tensor_tensor(dec[:, 1], dec[:, 1], dec[:, 0], ALU.mult), em_made)
                elif kind == "levw":
                    s, hb, l = a
                    b = (2 * s + hb) % 2
                    fk = D_FIRST[("decay", s, hb)] + 1
                    pool.wait_ge(d_free[fk % 4], fk // 4 + 1)
                    if l == 2:
                        fl = f_level(s, hb, 0)
                        pool.wait_ge(d_free[fl % 4], fl // 4 + 1)
                    if l >= 2:
                        pool.wait_ge(d_full, D_FIRST[("levw", s, hb, l - 2)] + 1)
                    elif s:
                        pool.wait_ge(d_full, D_FIRST[("levw", s - 1, hb, LEVELS - 2 + l)] + 1)
                    say(g_.tensor_tensor(nm[:, b, l % 2], nn[:, b], four(const(f"pair{l}")), ALU.mult), nm_made)
                elif kind == "uw":
                    s, hb = a
                    u = 2 * s + hb
                    b = u % 2
                    if u >= 2:
                        pool.wait_ge(d_full, D_FIRST[("uw",) + divmod(u - 2, 2)] + 1)
                    if s:
                        pool.wait_ge(d_full, D_FIRST[("scans", s - 1, hb)] + 1)
                    for hf, _, c in halves(s):
                        r = slice(64 * hf, 64 * hf + 64)
                        k3 = heads(dn_nat[r, 1, c // 2, 256 * hb:256 * hb + 256])
                        link(g_.tensor_tensor(kk[r, b], k3, wide(decay_of(0, s, hb, r)), ALU.mult))
                        ins = g_.tensor_tensor(ku[r, b], k3, wide(decay_of(1, s, hb, r)), ALU.mult)
                        if hf == 0:
                            link(ins)
                    say(ins, kk_made)
_INS = ["x", "mem", "rel_bias_table", "norm_mix_g", "w_in", "attn_q_norm_g", "attn_k_norm_g", "attn_sink",
        "dn_conv_w", "dn_a_log", "dn_dt_bias", "dn_out_norm_g", "mem_norm_g", "mem_w_kv", "mem_q_norm_g",
        "mem_k_norm_g", "w_br_attn", "w_br_dn", "w_br_mem", "w_out", "norm_ffn_g", "ffn_w_up", "ffn_conv_w",
        "ffn_conv_b", "ffn_w_down"]


def kernel(**inputs):
    import concourse.bacc as _bacc
    from concourse.bass_utils import run_bass_kernel_spmd as _run

    nc = _bacc.Bacc("TRN2", target_bir_lowering=False, num_devices=1)
    arrays, args = {}, {}
    for name in _INS + ["consts"]:
        a = CONSTS if name == "consts" else np.ascontiguousarray(inputs[name])
        arrays[f"in_{name}"] = a
        args[name] = nc.dram_tensor(f"in_{name}", a.shape, mybir.dt.from_np(a.dtype), kind="ExternalInput").ap()
    out = nc.dram_tensor("out_x", (1, SEQ, D), mybir.dt.float32, kind="ExternalOutput").ap()
    encoder_layer(nc, args, out)
    r = _run(nc, [arrays], core_ids=[0])
    return r.results[0]["out_x"]
```

```python
import numpy as np
import concourse.bass as bass
from concourse import mybir
from contextlib import ExitStack

D, SEQ, P = 1024, 512, 128
KT = D // P
RT = SEQ // P
N_MEM = 256
MT = N_MEM // P
D_FF = 2816
FT = D_FF // P
EPS = 1e-6
AH, AKV, AD = 8, 2, 64
WINDOW, BUCKETS, MAX_DIST = 128, 32, 128
DH, DK = 8, 64
DN_TAPS, CHUNK = 5, 64
NSLOT = SEQ // CHUNK
HB = 4
MH, MD = 4, 128
FFN_TAPS = 3
ATTN_Q, ATTN_KV, DN_W, MEM_Q = AH * AD, AKV * AD, DH * DK, MH * MD
C_AQ = 0
C_AKV = C_AQ + ATTN_Q
C_DN = C_AKV + 2 * ATTN_KV
C_DZ = C_DN + 3 * DN_W
C_BA = C_DZ + DN_W
C_MQ = C_BA + 4 * DH
C_GATE = C_MQ + MEM_Q
D_IN = C_GATE + 3 * D
LEVELS = 6
NEG = -1e30
BIAS_N = 3 * P + P - 1
RAW_N, HL_N, UNIT = 2, 3, 1024

CONST_COLS = {}


def shape_constants():
    n = np.arange(P)
    same = (n[:, None] // CHUNK) == (n[None, :] // CHUNK)
    half = n // CHUNK
    c64 = np.arange(CHUNK)
    within = n % CHUNK
    parts = {"exchange": np.eye(P)[::-1], "pick": None, "ones64": np.ones((P, CHUNK))}
    for p in range(2):
        fwd = (half == p)[:, None]
        parts[f"upto{p}"] = same * np.where(fwd, n[:, None] <= n[None, :], n[:, None] >= n[None, :])
    parts["ident"] = np.eye(P)
    for p in range(2):
        fwd = (half == p)[:, None]
        parts[f"after{p}"] = same * np.where(fwd, n[:, None] > n[None, :], n[:, None] < n[None, :])
    for p in range(2):
        fwd = (half == p)[:, None]
        parts[f"incl{p}"] = np.where(fwd, within[:, None] <= c64[None], within[:, None] >= c64[None])
        parts[f"strict{p}"] = np.where(fwd, within[:, None] < c64[None], within[:, None] > c64[None])
    for l in range(LEVELS):
        parts[f"pair{l}"] = ((within[:, None] >> l) ^ (c64[None] >> l)) == 1
    parts["ident64"] = within[:, None] == c64[None]
    rel = np.arange(BIAS_N) - (2 * P - 1)
    nb = BUCKETS // 2
    exact = nb // 2
    dist = np.abs(rel)
    large = exact + (np.log(np.maximum(dist, 1) / exact) / np.log(MAX_DIST / exact) * (nb - exact)).astype(np.int32)
    bucket = (rel > 0) * nb + np.where(dist < exact, dist, np.minimum(large, nb - 1))
    pick = np.zeros((P, BIAS_N + 1))
    valid = dist <= WINDOW
    pick[bucket[valid], np.arange(BIAS_N)[valid]] = 1.0
    pick[BUCKETS, :BIAS_N] = ~valid
    parts["pick"] = pick
    at = 0
    for k, v in parts.items():
        CONST_COLS[k] = (at, v.shape[1])
        at += v.shape[1]
    return np.concatenate([np.asarray(v, np.float32) for v in parts.values()], axis=1)


CONSTS = shape_constants()
EARLY = ("exchange", "pick", "ones64", "upto0", "upto1")



PARTS = {"by": 2, "bg": 4, "mqproj": 16, "zproj": 16}
FILLER_ROOM = {"attn_s": 3.4, "attn_e": 3.92, "attn_t": 0.32, "attn_p": 1.53, "attn_o": 1.6, "mqT": 1.21, "mkT": 1.4,
               "mscore": 2.3, "mtrans": 1.72, "mout": 1.49, "part": 2.6, "by": 1.3, "bg": 2.6, "mqproj": 2.55,
               "mqnorm": 1.32, "mscale": 0.59, "mqsquare": 0.57, "anorm": 0.25}
BURST = 3
Q_AT, Q_EACH = 3, 2


def with_parts(st):
    return [("part", st, i) for i in range(PARTS[st[0]] - 1)] + [st]


def walk_order():
    order = [("xnorm",), ("small",)] + [("xT", k) for k in range(KT)]
    order += [("dnproj", 0), ("bias_a",), ("dnproj", 1), ("small_b",), ("mnorm",), ("dnproj", 2)]
    for c in range(3, 12):
        order += [("dnproj", c)]
        order += [("bias_b", c - 3), ("mT", c - 3)] if c - 3 < KT else []
        order += {4: [("bsplit",)], 5: [("baproj",)], 6: [("baT",)], 7: [("gates_a",)], 9: [("gates_b",)]}.get(c, [])
    order += [("mkvproj", 1)] + [("dnnat", rt, j) for j in range(3) for rt in range(RT)]
    order += [("dnnorm", 0), ("dnnorm", 1), ("aqproj",), ("anorm", 0), ("akvproj",), ("anorm", 1), ("mkvproj", 0), ("dnT",), ("mknorm",)]

    q_parts = with_parts(("mqproj",))
    fillers = [[("aT",)], [("mkT",)], q_parts[:BURST]]
    q_parts = q_parts[BURST:]
    for n in range(RT):
        for g in range(AKV):
            some, q_parts = q_parts[:Q_EACH], q_parts[Q_EACH:]
            if not q_parts:
                some, q_parts = some[:-1], some[-1:]
            chain = [[("attn_s", n, g)], [("attn_e", n, g)], [("attn_t", n, g)], [("attn_p", n, g)], [("attn_o", n, g)]]
            fillers += chain[:Q_AT] + [some] + chain[Q_AT:]
    branches = [with_parts((k, b, c)) for b in range(2) for c in range(KT) for k in ("by", "bg")]
    ahead = sum((branch[:-1] for branch in branches[:4]), [])
    branches = [branch[-1:] for branch in branches[:4]] + branches[4:]
    fillers += [[q] for q in q_parts]
    for rt in range(RT):
        fillers += [[("mqsquare", rt)]]
    fillers += [[("mqnorm",)], ahead[:4], [("mqT",)]]
    ahead = ahead[4:]
    for rt in range(RT):
        fillers += [[("mscore", rt), ("mexp", rt)], [("mscale", rt)]]
    for h in range(MH):
        fillers += [ahead[:1], [("mtrans", h)], [("mout", h)]]
        ahead = ahead[1:]
    assert not ahead
    held_back = sum(branches[-4:], [])
    fillers += [[st] for st in sum(branches[:-4], [])]

    lane = []
    for s in range(NSLOT + 1):
        here = []
        if s < NSLOT:
            here += [("decay", s, 0), ("decay", s, 1)]
        if s > 0:
            here += [("scanv", s - 1, 0), ("scanv", s - 1, 1)]
        if s < NSLOT:
            here += [("levw", s, 0, 0), ("levw", s, 1, 0)]
        if s > 0:
            here += [("scans", s - 1, 0), ("scans", s - 1, 1)]
        if s < NSLOT:
            for l in range(1, LEVELS):
                here += [("levw", s, 0, l), ("levw", s, 1, l), ("levy", s, 0, l), ("levy", s, 1, l)]
            here += [("uw", s, 0), ("uw", s, 1)]
        lane += here

    def room(group):
        return sum(FILLER_ROOM.get(st[0], 0.5) for st in group)

    per_stage = sum(room(group) for group in fillers) / (len(lane) - 4)
    z_parts = with_parts(("zproj",))
    spent = 0.0
    for i, st in enumerate(lane[:-2]):
        order.append(st)
        while fillers and spent < (i + 1) * per_stage:
            spent += room(fillers[0])
            order += fillers.pop(0)
    order += sum(fillers, []) + z_parts[:2] + lane[-2:-1] + z_parts[2:3] + lane[-1:] + z_parts[3:]
    order += [("osum",)] + held_back + [("oT",)]
    order += with_parts(("bg", 2, 0))[:-1] + with_parts(("bg", 2, 1))[:-1]
    for c in range(KT):
        order += with_parts(("by", 2, c)) + with_parts(("bg", 2, c))[-1 if c < 2 else 0:]
    order += [("wout", 0), ("wout", 1), ("x2norm",)]
    order += [("h2T", k) for k in range(KT)]
    order += [("up", c) for c in range(FT)]
    order += [("down", 0), ("down", 1)]
    return order


ORDER = walk_order()
G_FILLS = {"dnproj": 1, "baproj": 1, "zproj": RT, "aqproj": RT, "akvproj": RT, "mqproj": RT,
           "mkvproj": MT, "by": 1, "bg": 1, "wout": RT, "up": 2, "down": RT}
D_FILLS = {"small": 1, "small_b": 2, "bias_a": 1, "bias_b": 1, "xT": 1, "mT": 1, "gates_b": 1, "baT": 1, "aT": 4 + AKV, "dnnat": 1,
           "attn_s": 4, "attn_o": 1, "mqT": MH, "mkT": MH // 2, "mscore": 2, "mtrans": MT, "mout": 1, "dnT": 8,
           "decay": 2, "levw": 1, "levy": 1, "uw": 1, "scanv": 1, "scans": 1, "oT": 4, "h2T": 1}


def d_fills(st):
    return len(key_blocks(st[1])) if st[0] == "attn_p" else D_FILLS.get(st[0], 0)


def key_blocks(n):
    return [kb for kb in range(3) if 0 <= n - 1 + kb < RT]


def stage_units(st):
    kind = st[0]
    if kind == "dnproj":
        return [("w_in", 0, KT, C_DN + st[1] * P, P)]
    if kind in ("zproj", "aqproj", "mqproj"):
        c0 = {"zproj": C_DZ, "aqproj": C_AQ, "mqproj": C_MQ}[kind]
        return [("w_in", 2 * i, 2, c0, 512) for i in range(KT // 2)]
    if kind == "akvproj":
        return [("w_in", 4 * i, 4, C_AKV, 2 * ATTN_KV) for i in range(KT // 4)]
    if kind == "mkvproj":
        return [("mem_w_kv", 2 * i, 2, 512 * st[1], 512) for i in range(KT // 2)]
    if kind == "by":
        name = ("w_br_attn", "w_br_mem", "w_br_dn")[st[1]]
        return [(name, 0, 4, st[2] * P, 2 * P)] if st[2] % 2 == 0 else []
    if kind == "bg":
        gate = (0, 2, 1)[st[1]]
        return [("w_in", 0, KT, C_GATE + gate * D + st[2] * P, P)]
    if kind == "wout":
        return [("w_out", 2 * i, 2, 512 * st[1], 512) for i in range(KT // 2)]
    if kind == "up":
        return [("ffn_w_up", 0, KT, st[1] * P, P), ("ffn_w_up", 0, KT, D_FF + st[1] * P, P)]
    if kind == "down":
        return [("ffn_w_down", 2 * i, 2, 512 * st[1], 512) for i in range(FT // 2)]
    return []


G_FIRST, D_FIRST, U_FIRST, NTH, UNITS = {}, {}, {}, {}, []
LAST_USE = []
G_AT, D_AT = 0, 0
for PLACE, STAGE in enumerate(ORDER):
    G_FIRST[STAGE], D_FIRST[STAGE], U_FIRST[STAGE] = G_AT, D_AT, len(UNITS)
    NTH[STAGE] = sum(o[0] == STAGE[0] for o in ORDER[:PLACE])
    G_AT += G_FILLS.get(STAGE[0], 0)
    D_AT += d_fills(STAGE)
    for UNIT_OF in stage_units(STAGE):
        UNITS.append(UNIT_OF)
        NUMBER = len(UNITS) - U_FIRST[STAGE]
        if UNIT_OF[0].startswith("w_br"):
            LAST_USE.append(ORDER.index(STAGE[:2] + (STAGE[2] + 1,)))
        elif STAGE[0] in ("mqproj", "zproj") and NUMBER < KT // 2:
            LAST_USE.append(ORDER.index(("part", STAGE, RT * NUMBER - 1)))
        else:
            LAST_USE.append(PLACE)

UNIT_DONE, USED_AT = [], 0
for NUMBER, PLACE in enumerate(LAST_USE):
    STAGE = ORDER[PLACE][1] if ORDER[PLACE][0] == "part" else ORDER[PLACE]
    IN_STAGE = len(stage_units(STAGE))
    FIRST = G_FIRST[STAGE]
    if STAGE[0] in ("dnproj", "by", "bg"):
        UNIT_DONE.append(("g_full", FIRST + 1))
    elif STAGE[0] == "up":
        UNIT_DONE.append(("g_full", FIRST + NUMBER - U_FIRST[STAGE] + 1))
    elif NUMBER == U_FIRST[STAGE] + IN_STAGE - 1:
        UNIT_DONE.append(("g_full", FIRST + G_FILLS[STAGE[0]]))
    else:
        USED_AT += 1
        UNIT_DONE.append(("unit_used", USED_AT))

SPLITS_AT = {PLACE: [] for PLACE in range(-1, len(ORDER))}
SPLITS_AFTER = {PLACE: [] for PLACE in range(len(ORDER))}
ROWS = ("aqproj", "akvproj", "mqproj", "mkvproj", "zproj", "wout", "down")
SPLIT_PLACE = -1
for NUMBER in range(len(UNITS)):
    if NUMBER == RAW_N:
        SPLIT_PLACE = ORDER.index(("dnproj", 0))
    if NUMBER >= HL_N:
        SPLIT_PLACE = max(SPLIT_PLACE, LAST_USE[NUMBER - HL_N])
    LATE = NUMBER >= HL_N and ORDER[SPLIT_PLACE][0] in ROWS and (
        SPLITS_AFTER[SPLIT_PLACE] or (LAST_USE[NUMBER - HL_N] == SPLIT_PLACE and UNIT_DONE[NUMBER - HL_N][0] == "g_full"))
    (SPLITS_AFTER if LATE else SPLITS_AT)[SPLIT_PLACE].append(NUMBER)


def encoder_layer(nc, W, out, stop=None, dump=None):
    F, R = mybir.dt.float32, mybir.dt.float32r
    ALU, ACT, AX = mybir.AluOpType, mybir.ActivationFunctionType, mybir.AxisListType
    X = AX.X
    order = ORDER if stop is None else ORDER[:stop]

    ctx = ExitStack()
    with ctx:
        base = (nc.sbuf_base + 31) // 32 * 32
        end = nc.sbuf_usable_end
        at_end = [0]

        def place(name, shape, offset, dt=F):
            size = int(np.prod(shape[1:])) * 4
            at_end[0] = (offset + size + 31) // 32 * 32
            assert base + offset + size <= end, (name, base + offset + size, end)
            return nc.alloc_sbuf_tensor_at(name, shape, dt, offset=base + offset)

        def after(name, shape, dt=F):
            return place(name, shape, at_end[0], dt)

        def signal(name):
            return ctx.enter_context(nc.semaphore(name))

        kept = [k for k in CONST_COLS if k not in EARLY]
        n_const = sum(CONST_COLS[k][1] for k in kept)
        n_late = sum(CONST_COLS[k][1] for k in EARLY)
        cst = place("cst", [P, n_const], 0)
        raw = after("raw", [P, RAW_N, UNIT])
        w_hi = after("w_hi", [P, HL_N, UNIT], R)
        w_lo = after("w_lo", [P, HL_N, UNIT], R)
        pcol = after("pcol", [P, 96])
        fcol = after("fcol", [P, 4 * 2 * FT])
        rowp = after("rowp", [P, 2 * 16 + AH])
        st_x = after("st_x", [P, 2 * RT])
        st_a = after("st_a", [P, RT, 10])
        st_m = after("st_m", [P, 24])
        st_d = after("st_d", [P, 2, RT, DH])
        st_o = after("st_o", [P, RT * DH])
        st_s = after("st_s", [P, 8, 4])
        g_slot = after("g_slot", [P, NSLOT, DH])
        b_slot = after("b_slot", [P, NSLOT, DH])
        e_slot = after("e_slot", [P, 192])
        tg = after("tg", [P, SEQ])
        hT_hi = after("hT_hi", [P, KT, SEQ], R)
        hT_lo = after("hT_lo", [P, KT, SEQ], R)
        m0 = at_end[0]
        merged = after("merged", [P, KT, SEQ])
        y0 = at_end[0]
        yA_hi = after("yA_hi", [P, 4, SEQ], R)
        yA_lo = after("yA_lo", [P, 4, SEQ], R)
        yM_hi = after("yM_hi", [P, 4, SEQ], R)
        yM_lo = after("yM_lo", [P, 4, SEQ], R)
        a0 = at_end[0]
        xt = place("xt", [P, RT, D], m0)
        dnc = place("dnc", [P, 12, SEQ], m0)
        mkn = place("mkn", [P, MT, MEM_Q], m0 + 28672)
        aqT = place("aqT", [P, 4, SEQ], m0)
        sc = after("sc", [P, 4, 3 * P])
        pT1 = after("pT1", [P, 4, P])
        anat = place("anat", [P, RT, ATTN_Q + ATTN_KV], y0)
        bias = place("bias", [P, AH, 3 * P], y0 + 16384)
        akT = after("akT", [P, AKV, SEQ])
        msc = place("msc", [P, RT, MH, N_MEM], m0)
        mqn = place("mqn", [P, RT, MEM_Q], y0 + 16384)
        mqT = after("mqT", [P, MH, SEQ])
        mx = place("mx", [P, MT, D], a0)
        scr = after("scr", [P, D])
        rows = after("rows", [P, 3, P])
        late = after("late", [P, n_late])
        btab = after("btab", [P, AH])
        bT = after("bT", [P, BIAS_N + 1])
        brev = after("brev", [P, AH, 3 * P])
        w_ba = after("w_ba", [P, KT, 4 * DH])
        ba_hi = after("ba_hi", [P, KT, 4 * DH], R)
        ba_lo = after("ba_lo", [P, KT, 4 * DH], R)
        baT = after("baT", [4 * DH, SEQ])
        ba = after("ba", [P, RT, 32])
        sp = after("sp", [P, 2, RT, 16])
        ealog = after("ealog", [P, 16])
        dn_nat = place("dn_nat", [P, 3, RT, DN_W], a0)
        qkT = after("qkT", [P, 8, SEQ])
        o_nat = after("o_nat", [P, RT, DN_W])
        S = after("S", [P, 2, 2, 2, DK])
        dec = after("dec", [P, 2, 2, HB, CHUNK])
        nn = after("nn", [P, 2, HB, CHUNK])
        nm = after("nm", [P, 2, 2, HB, CHUNK])
        yx = after("yx", [P, 2, 2, HB, CHUNK])
        wx = after("wx", [P, 2, HB, CHUNK])
        kk = after("kk", [P, 2, HB, CHUNK])
        vn = after("vn", [P, 2, HB, CHUNK])
        at_ = after("at_", [P, 4, HB, CHUNK])
        mkT = after("mkT", [P, MH, N_MEM])
        mv = after("mv", [P, MT, MEM_Q])
        av = after("av", [P, RT, ATTN_KV])
        pT2 = after("pT2", [P, 4, P])
        memT_hi = place("memT_hi", [P, KT, N_MEM], a0 + 49152, R)
        memT_lo = after("memT_lo", [P, KT, N_MEM], R)
        uu = place("uu", [P, 2, HB, CHUNK], a0)
        wt = after("wt", [P, 2, 2, 2, CHUNK])
        ku = after("ku", [P, 2, HB, CHUNK])
        o1 = after("o1", [P, 2, HB, CHUNK])
        zs = place("zs", [P, RT, DN_W], a0 + 24576 + 8192)
        xr = place("xr", [P, RT, D], a0)
        xn = after("xn", [P, RT, D])
        m_hi = after("m_hi", [P, KT, SEQ], R)
        m_lo = after("m_lo", [P, KT, SEQ], R)
        x2 = place("x2", [P, RT, D], m0)
        act_hi = place("act_hi", [P, FT, SEQ], y0, R)
        act_lo = after("act_lo", [P, FT, SEQ], R)
        u_gv = after("u_gv", [P, 2, 2, SEQ])
        pTs = [tg[:].rearrange("p (i q) -> p i q", i=4), pT1, pT2]
        mpTs = [tg[:], pT2[:].rearrange("p i q -> p (i q)")]

        gb = [ctx.enter_context(nc.psum_tensor(f"g_bank{i}", [P, 512], F)) for i in range(4)]
        db = [ctx.enter_context(nc.psum_tensor(f"d_bank{i}", [P, 512], F)) for i in range(4)]
        bias_rows = nc.dram_tensor("bias_rows", (AH, BIAS_N + 1), F)

        def const(name, rows=slice(0, P)):
            if name in EARLY:
                first = CONST_COLS[EARLY[0]][0]
                return late[rows, CONST_COLS[name][0] - first:CONST_COLS[name][0] - first + CONST_COLS[name][1]]
            first = CONST_COLS[kept[0]][0]
            return cst[rows, CONST_COLS[name][0] - first:CONST_COLS[name][0] - first + CONST_COLS[name][1]]

        g_full, d_full = signal("g_full"), signal("d_full")
        g_free = [signal(f"g_free{i}") for i in range(4)]
        d_free = [signal(f"d_free{i}") for i in range(4)]
        raw_loaded = [signal(f"raw_loaded{i}") for i in range(RAW_N)]
        hi_made, lo_made, unit_used = signal("hi_made"), signal("lo_made"), signal("unit_used")
        act_step, dve_step, pool_step, pe_step = (signal(n) for n in ("act_step", "dve_step", "pool_step", "pe_step"))
        ident_in, consts_in, late_in, cols_in, fcols_in, rows_in, ba_in, mem_in = (signal(n) for n in (
            "ident_in", "consts_in", "late_in", "cols_in", "fcols_in", "rows_in", "ba_in", "mem_in"))
        x_in = [signal(f"x_in{t}") for t in range(RT)]
        table_in, bias_out, bias_in, xr_in = signal("table_in"), signal("bias_out"), signal("bias_in"), signal("xr_in")
        stored = signal("stored")
        table_ready, ss_made, sqrt_made, var_made = (signal(n) for n in ("table_ready", "ss_made", "sqrt_made", "var_made"))
        x_scaled, part_hi, tap_made = signal("x_scaled"), signal("part_hi"), signal("tap_made")
        ba_split, ba_rounded = signal("ba_split"), signal("ba_rounded")
        dn_silu, sp_made, softplus_made, beta_made = (signal(n) for n in ("dn_silu", "sp_made", "softplus_made", "beta_made"))
        slots_made, decays_made, a_scaled = signal("slots_made"), signal("decays_made"), signal("a_scaled")
        attn_max, attn_exp, attn_scaled = signal("attn_max"), signal("attn_exp"), signal("attn_scaled")
        mq_scaled, mk_scaled, mem_max, mem_scaled = signal("mq_scaled"), signal("mk_scaled"), signal("mem_max"), signal("mem_scaled")
        mq_inverse, o_inverse, o_scaled_too = signal("mq_inverse"), signal("o_inverse"), signal("o_scaled_too")
        aq_inverse, dn_inverse, aq_scaled = signal("aq_inverse"), signal("dn_inverse"), signal("aq_scaled")
        dn_scaled, state_zero = signal("dn_scaled"), signal("state_zero")
        b_made, em_made, nm_made, kk_made = signal("b_made"), signal("em_made"), signal("nm_made"), signal("kk_made")
        vn_made, o_added, o_scaled = signal("vn_made"), signal("o_added"), signal("o_scaled")
        gate_used, mhi_made, m_split = (signal(n) for n in ("gate_used", "mhi_made", "m_split"))
        x2_root, x2_last = signal("x2_root"), signal("x2_last")
        x2_scaled, ua_made, silu_made, glu_made, fhi_made, f_split = (signal(n) for n in ("x2_scaled", "ua_made", "silu_made", "glu_made", "fhi_made", "f_split"))
        SIG = {"g_full": g_full, "unit_used": unit_used}
        PC_MIX, PC_FFN, PC_MEM = DN_TAPS * 12, DN_TAPS * 12 + KT, DN_TAPS * 12 + 2 * KT
        PC_MQ, PC_MK, PC_AQ, PC_AK, PC_DO = (PC_MEM + KT + i for i in range(5))
        N_PC = PC_DO + 1
        FH = 2 * FT
        len_units = sum(len(stage_units(o)) for o in order)

        def level_no(s, hb, l):
            return NTH[("levw", s, hb, l)]

        def f_level(s, hb, l):
            return D_FIRST[("levy" if l else "levw", s, hb, l)]

        NORM = {st: i for i, st in enumerate([("xnorm", t) for t in range(RT)] + [st for st in ORDER if st[0] in (
            "mnorm", "dnnorm", "anorm", "mknorm", "mqnorm", "osum", "x2norm")])}

        def heads(ap):
            return ap.rearrange("p (h d) -> p h d", d=64)

        def halves(s):
            return [(hf, 0 if hf == s % 2 else 1, s if hf == s % 2 else NSLOT - 1 - s) for hf in range(2)]

        def decay_of(kind, s, hb, rows=slice(0, P)):
            v = e_slot[rows, 64:192].rearrange("p (k q i h) -> p k q i h", k=2, q=2, i=4)
            return v[:, kind, s % 2, s // 2, HB * hb:HB * hb + HB]

        def unit_view(ring, u):
            _, _, nk, _, nc_ = UNITS[u]
            n = RAW_N if ring is raw else HL_N
            return ring[:, u % n, 0:nk * nc_].rearrange("p (k c) -> p k c", k=nk)

        block = ctx.enter_context(nc.Block())

        @block.sync
        def _(sync):
            for t in range(RT):
                sync.dma_start(xt[:, t, :], W["x"][0, t * P:(t + 1) * P, :]).then_inc(x_in[t], 16)
            sync.dma_start(cst[:, 0:P], W["consts"][:, n_late:n_late + P]).then_inc(ident_in, 16)
            at = 0
            for src in ("dn_conv_w", "norm_mix_g", "norm_ffn_g", "mem_norm_g", "mem_q_norm_g", "mem_k_norm_g"):
                v = W[src].rearrange("l k (c p) -> (l k c) p", p=P) if src == "dn_conv_w" else W[src].rearrange("l (c p) -> (l c) p", p=P)
                sync.dma_start(rows[at:at + v.shape[0], 0, :], v).then_inc(cols_in, 16)
                at += v.shape[0]
            for src in ("attn_q_norm_g", "attn_k_norm_g", "dn_out_norm_g"):
                for side in range(2):
                    sync.dma_start(rows[at:at + 1, 0, 64 * side:64 * side + 64], W[src]).then_inc(cols_in, 16)
                at += 1
            def load_units(first, last):
                for u in range(first, last):
                    name, k0, nk, c0, n = UNITS[u]
                    if u >= RAW_N:
                        sync.wait_ge(lo_made, u - RAW_N + 1)
                    src = W[name][0, k0 * P:(k0 + nk) * P, c0:c0 + n].rearrange("(k p) c -> p k c", p=P)
                    sync.dma_start(unit_view(raw, u), src).then_inc(raw_loaded[u % RAW_N], 16)

            done = min(RAW_N, len_units)
            load_units(0, done)
            sync.dma_start(btab[0:BUCKETS, :], W["rel_bias_table"]).then_inc(table_in, 16)
            sync.dma_start(late[:], W["consts"][:, 0:n_late]).then_inc(late_in, 16)
            for i, st in enumerate(order):
                if st == ("wout", 0):
                    f = D_FIRST[("oT",)] + 3
                    sync.wait_ge(d_free[f % 4], f // 4 + 1)
                    sync.dma_start(xr[:], W["x"][0].rearrange("(t p) d -> p t d", p=P)).then_inc(xr_in, 16)
                ahead = min(len_units, U_FIRST[st] + len(stage_units(st)) + HL_N)
                if ahead > done:
                    load_units(done, ahead)
                    done = ahead
                if st == ("dnproj", 0):
                    sync.dma_start(cst[:, P:], W["consts"][:, n_late + P:]).then_inc(consts_in, 16)
                    fw = W["ffn_conv_w"].rearrange("l k (c p) -> (l k c) p", p=P)
                    fb = W["ffn_conv_b"].rearrange("l (c p) -> (l c) p", p=P)
                    sync.dma_start(rows[0:2 * FH, 1, :], fw[0:2 * FH, :]).then_inc(fcols_in, 16)
                    sync.dma_start(rows[0:FH, 2, :], fw[2 * FH:3 * FH, :]).then_inc(fcols_in, 16)
                    sync.dma_start(rows[FH:2 * FH, 2, :], fb).then_inc(fcols_in, 16)
                    small = (("dn_a_log", 0, 16, "l t h -> l (t h)"), ("dn_dt_bias", 16, 16, "l t h -> l (t h)"), ("attn_sink", 32, AH, None))
                    for src, c0, n, how in small:
                        v = W[src].rearrange(how) if how else W[src]
                        sync.dma_start(rowp[:, c0:c0 + n], v.to_broadcast([P, n])).then_inc(rows_in, 16)
                    sync.dma_start(w_ba[:], W["w_in"][0, :, C_BA:C_BA + 4 * DH].rearrange("(k p) c -> p k c", p=P)).then_inc(ba_in, 16)
                    sync.dma_start(mx[:], W["mem"][0].rearrange("(t p) d -> p t d", p=P)).then_inc(mem_in, 16)
                if st[0] == "bias_a":
                    f = D_FIRST[st]
                    sync.wait_ge(d_free[f % 4], f // 4 + 1)
                    sync.dma_start(bias_rows.ap(), bT[0:AH, :]).then_inc(bias_out, 16)
                if st == ("dnproj", 2):
                    sync.wait_ge(bias_out, 16)
                    band = bass.AP(tensor=bias_rows, offset=0, ap=[[1, P], [BIAS_N + 1, AH], [1, 3 * P]])
                    sync.dma_start(brev[:], band).then_inc(bias_in, 16)
                if st[0] == "down":
                    for rt in range(RT):
                        f = G_FIRST[st] + rt
                        sync.wait_ge(g_free[f % 4], f // 4 + 1)
                        c0 = 512 * st[1]
                        sync.dma_start(out[0, rt * P:(rt + 1) * P, c0:c0 + 512], x2[:, rt, c0:c0 + 512]).then_inc(stored, 16)
                    if st[1] == 1:
                        sync.wait_ge(stored, 16 * 2 * RT)

        @block.tensor
        def _(pe):
            mm = nc.tensor.matmul
            steps = [0]

            def tiles_apart(ins):
                steps[0] += 1
                ins.then_inc(pe_step, 1)
                pe.wait_ge(pe_step, steps[0])

            def d_claim(f):
                if f >= 4:
                    pe.wait_ge(d_free[f % 4], f // 4)
                return db[f % 4]

            def g_claim(f):
                if f >= 4:
                    pe.wait_ge(g_free[f % 4], f // 4)
                return gb[f % 4]

            def evacuated(f):
                pe.wait_ge(d_free[f % 4], f // 4 + 1)

            def arrived(u):
                pe.wait_ge(hi_made, u + 1)
                pe.wait_ge(lo_made, u + 1)

            def transposes(f, sources, width=P):
                bank = d_claim(f)
                for i, src in enumerate(sources):
                    last = nc.tensor.transpose(bank[:, i * width:(i + 1) * width], src, const("ident"))
                last.then_inc(d_full, 1)

            def columns_product(f, u, col, act_hi_, act_lo_, nk, part=0, parts=1, made_by=None):
                bank = g_claim(f) if part == 0 else gb[f % 4]
                if part == 0:
                    arrived(u)
                hi, lo = unit_view(w_hi, u), unit_view(w_lo, u)
                for k in range(nk * part // parts, nk * (part + 1) // parts):
                    if made_by:
                        evacuated(D_FIRST[(made_by, k)])
                    for w, a in ((hi, act_hi_), (hi, act_lo_), (lo, act_hi_)):
                        last = mm(bank[:, :], w[:, k, col:col + P], a[:, k, :], start=(k == 0 and w is hi and a is act_hi_),
                                  stop=(k == nk - 1 and w is lo))
                if part == parts - 1:
                    last.then_inc(g_full, 1)

            def rows_product(f, first, act_hi_, act_lo_, tiles=RT, units=None, pieces=None, made=None):
                units = stage_units(st) if units is None else units
                for piece in range(len(units) * tiles) if pieces is None else pieces:
                    j, t = divmod(piece, tiles)
                    _, k0, nk, _, n = units[j]
                    u = first + j
                    bank = g_claim(f + t) if j == 0 else gb[(f + t) % 4]
                    if t == 0:
                        arrived(u)
                        if made is not None:
                            pe.wait_ge(made, k0 + nk)
                    hi, lo = unit_view(w_hi, u), unit_view(w_lo, u)
                    final = j == len(units) - 1
                    for k in range(nk):
                        for a, w in ((act_hi_, hi), (act_hi_, lo), (act_lo_, hi)):
                            last = mm(bank[:, 0:n], a[:, k0 + k, t * P:(t + 1) * P], w[:, k, :],
                                      start=(k0 + k == 0 and a is act_hi_ and w is hi),
                                      stop=(final and k == nk - 1 and a is act_lo_))
                    if final:
                        last.then_inc(g_full, 1)
                    elif t == tiles - 1:
                        last.then_inc(unit_used, 1)

            def small():
                pe.wait_ge(ident_in, 16)
                pe.wait_ge(cols_in, 16 * 12)
                bank = d_claim(D_FIRST[st])
                nc.tensor.transpose(bank[:, 0:N_PC], rows[0:N_PC, 0, :], const("ident", slice(0, N_PC))[:, 0:N_PC]).then_inc(d_full, 1)

            def small_b():
                pe.wait_ge(fcols_in, 16 * 3)
                for i in range(2):
                    bank = d_claim(D_FIRST[st] + i)
                    nc.tensor.transpose(bank[:, 0:2 * FH], rows[0:2 * FH, 1 + i, :], const("ident", slice(0, 2 * FH))[:, 0:2 * FH]).then_inc(d_full, 1)

            def bias_a():
                bank = d_claim(D_FIRST[st])
                pe.wait_ge(table_in, 16)
                pe.wait_ge(late_in, 16)
                pe.wait_ge(table_ready, 1)
                mm(bank[0:AH, 0:BIAS_N + 1], btab[0:BUCKETS + 1, :], const("pick", slice(0, BUCKETS + 1)), start=True, stop=True).then_inc(d_full, 1)

            def bias_b(h):
                pe.wait_ge(bias_in, 16)
                bank = d_claim(D_FIRST[st])
                mm(bank[:, 0:3 * P], const("exchange"), brev[:, h, :], start=True, stop=True).then_inc(d_full, 1)

            def baproj():
                pe.wait_ge(ba_split, 1)
                bank = g_claim(G_FIRST[st])
                for k in range(KT):
                    for w, x_ in ((ba_hi, hT_hi), (ba_hi, hT_lo), (ba_lo, hT_hi)):
                        last = mm(bank[0:4 * DH, :], w[:, k, :], x_[:, k, :], start=(k == 0 and w is ba_hi and x_ is hT_hi),
                                  stop=(k == KT - 1 and w is ba_lo))
                last.then_inc(g_full, 1)

            def baT_():
                bank = d_claim(D_FIRST[st])
                fb = G_FIRST[("baproj",)]
                pe.wait_ge(g_free[fb % 4], fb // 4 + 1)
                for t in range(RT):
                    last = nc.tensor.transpose(bank[:, 32 * t:32 * t + 32], baT[:, t * P:(t + 1) * P], const("ident", slice(0, 4 * DH))[:, 0:4 * DH])
                last.then_inc(d_full, 1)

            def gates_b():
                bank = d_claim(D_FIRST[st])
                pe.wait_ge(slots_made, 1)
                for hf in range(2):
                    rr = slice(64 * hf, 64 * hf + 64)
                    for p in range(2):
                        d = 0 if hf == p else 1
                        for par in range(2):
                            o = (p * 2 + d) * 16
                            last = mm(bank[64 * par:64 * par + 64, o:o + 16].rearrange("p (i h) -> p i h", i=4), const("ones64", rr),
                                      g_slot[rr, p::2, par::2], start=True, stop=True)
                    tiles_apart(last)
                for kind, mask in enumerate(("upto", "after")):
                    for p in range(2):
                        o = 64 + (kind * 2 + p) * 32
                        last = mm(bank[:, o:o + 32].rearrange("p (i h) -> p i h", i=4), const(f"{mask}{p}"), g_slot[:, p::2, :], start=True, stop=True)
                last.then_inc(d_full, 1)

            def attn_s(n, g):
                f, kbs = D_FIRST[st], key_blocks(n)
                lo, hi = kbs[0], kbs[-1] + 1
                evacuated(D_FIRST[("aT",)] + 5)
                for i in range(4):
                    h = 4 * g + i
                    r = slice(64 * (h % 2), 64 * (h % 2) + 64)
                    bank = d_claim(f + i)
                    mm(bank[:, lo * P:hi * P], aqT[r, h // 2, n * P:(n + 1) * P], akT[r, g, (n - 1 + lo) * P:(n - 1 + hi) * P],
                       start=True, stop=True).then_inc(d_full, 1)

            def attn_p(n, g):
                pe.wait_ge(attn_scaled, NTH[st] + 1)
                for j, kb in enumerate(key_blocks(n)):
                    transposes(D_FIRST[st] + j, [sc[:, i, kb * P:(kb + 1) * P] for i in range(4)])

            def attn_o(n, g):
                fo, kbs = D_FIRST[st], key_blocks(n)
                bank = d_claim(fo)
                evacuated(D_FIRST[("attn_p", n, g)] + len(kbs) - 1)
                for par in range(2):
                    for kb in kbs:
                        last = mm(bank[64 * par:64 * par + 64, 0:2 * P].rearrange("p (i q) -> p i q", i=2), av[:, n - 1 + kb, 64 * g:64 * g + 64],
                                  pTs[kb][:, par::2, :], start=(kb == kbs[0]), stop=(kb == kbs[-1]))
                last.then_inc(d_full, 1)

            def mscore(rt):
                evacuated(D_FIRST[("mqT",)] + MH - 1)
                evacuated(D_FIRST[("mkT",)] + 1)
                for j in range(2):
                    bank = d_claim(D_FIRST[st] + j)
                    for i in range(2):
                        h = 2 * j + i
                        last = mm(bank[:, i * N_MEM:(i + 1) * N_MEM], mqT[:, h, rt * P:(rt + 1) * P], mkT[:, h, :], start=True, stop=True)
                    last.then_inc(d_full, 1)

            def mtrans(h):
                pe.wait_ge(mem_scaled, RT)
                for m in range(MT):
                    transposes(D_FIRST[st] + m, [msc[:, rt, h, m * P:(m + 1) * P] for rt in range(RT)])

            def mout(h):
                bank = d_claim(D_FIRST[st])
                evacuated(D_FIRST[("mtrans", h)] + MT - 1)
                for m in range(MT):
                    last = mm(bank[:, :], mv[:, m, h * P:(h + 1) * P], mpTs[m], start=(m == 0), stop=(m == MT - 1))
                last.then_inc(d_full, 1)

            def decay(s, hb):
                f, u = D_FIRST[st], 2 * s + hb
                bank = d_claim(f)
                pe.wait_ge(consts_in, 16)
                pe.wait_ge(b_made, u + 1)
                mm(bank[:, 0:HB * CHUNK], const(f"after{s % 2}"), dec[:, u % 2, 0].rearrange("p h c -> p (h c)"), start=True, stop=True).then_inc(d_full, 1)
                bank = d_claim(f + 1)
                evacuated(D_FIRST[("dnT",)] + 7)
                for i in (0, 2, 1, 3):
                    if i == 1:
                        tiles_apart(last)
                    for hf, _, c in halves(s):
                        h = HB * hb + i
                        r = slice(64 * (h % 2), 64 * (h % 2) + 64)
                        both = qkT[r, :, c * CHUNK:(c + 1) * CHUNK].rearrange("p (j t) n -> p t j n", j=2)[:, h // 2]
                        last = mm(bank[64 * hf:64 * hf + 64, i * 128:(i + 1) * 128].rearrange("p (j n) -> p j n", j=2),
                                  qkT[r, 4 + h // 2, c * CHUNK:(c + 1) * CHUNK], both, start=True, stop=True)
                last.then_inc(d_full, 1)

            def levw(s, hb, l):
                f, b = D_FIRST[st], (2 * s + hb) % 2
                bank = d_claim(f)
                pe.wait_ge(nm_made, level_no(s, hb, l) + 1)
                if l > 0:
                    evacuated(f_level(s, hb, l - 1))
                for i in range(HB):
                    for hf in range(2):
                        r = slice(64 * hf, 64 * hf + 64)
                        rhs = const("ident64", r) if l == 0 else yx[r, b, 1, i, :]
                        last = mm(bank[r, i * CHUNK:(i + 1) * CHUNK], nm[r, b, l % 2, i, :], rhs, start=True, stop=True)
                last.then_inc(d_full, 1)

            def levy(s, hb, l):
                f, b = D_FIRST[st], (2 * s + hb) % 2
                bank = d_claim(f)
                evacuated(D_FIRST[("levw", s, hb, l)])
                for i in range(HB):
                    for hf in range(2):
                        r = slice(64 * hf, 64 * hf + 64)
                        last = mm(bank[r, i * CHUNK:(i + 1) * CHUNK], wx[r, b, i, :], yx[r, b, 0, i, :], start=True, stop=True)
                        if l < LEVELS - 1:
                            last = mm(bank[r, 256 + i * CHUNK:256 + (i + 1) * CHUNK], yx[r, b, 0, i, :], wx[r, b, i, :], start=True, stop=True)
                last.then_inc(d_full, 1)

            def uw(s, hb):
                f, u = D_FIRST[st], 2 * s + hb
                b = u % 2
                bank = d_claim(f)
                evacuated(f_level(s, hb, LEVELS - 1))
                pe.wait_ge(kk_made, u + 1)
                for hf, _, c in halves(s):
                    for i in range(HB):
                        h = HB * hb + i
                        r = slice(64 * hf, 64 * hf + 64)
                        q = slice(64 * (h % 2), 64 * (h % 2) + 64)
                        mm(bank[r, i * CHUNK:(i + 1) * CHUNK], yx[r, b, 0, i, :], dn_nat[r, 2, c // 2, h * 64:h * 64 + 64], start=True, stop=True)
                        o = 256 + (hf * 2 + i // 2) * 64
                        last = mm(bank[q, o:o + 64], kk[r, b, i, :], yx[r, b, 0, i, :], start=True, stop=True)
                    if hf == 0:
                        tiles_apart(last)
                last.then_inc(d_full, 1)

            def scanv(s, hb):
                f, u = D_FIRST[st], 2 * s + hb
                b = u % 2
                bank = d_claim(f)
                evacuated(D_FIRST[("uw", s, hb)])
                if s:
                    evacuated(D_FIRST[("scans", s - 1, hb)])
                else:
                    pe.wait_ge(state_zero, 1)
                for i in (0, 2, 1, 3):
                    if i == 1:
                        tiles_apart(last)
                    for hf, d, c in halves(s):
                        h = HB * hb + i
                        r = slice(64 * hf, 64 * hf + 64)
                        q = slice(64 * (h % 2), 64 * (h % 2) + 64)
                        mm(bank[r, i * 64:i * 64 + 64], wt[q, b, hf, i // 2, :], S[q, hb, d, i // 2, :], start=True, stop=True)
                        last = mm(bank[r, 256 + i * 64:320 + i * 64], qkT[q, h // 2, c * CHUNK:(c + 1) * CHUNK], S[q, hb, d, i // 2, :], start=True, stop=True)
                last.then_inc(d_full, 1)

            def scans(s, hb):
                f, u = D_FIRST[st], 2 * s + hb
                b = u % 2
                bank = d_claim(f)
                pe.wait_ge(vn_made, u + 1)
                for hf, d, c in halves(s):
                    for i in range(HB):
                        h = HB * hb + i
                        r = slice(64 * hf, 64 * hf + 64)
                        q = slice(64 * (h % 2), 64 * (h % 2) + 64)
                        mm(bank[r, i * 64:i * 64 + 64], at_[r, u % 4, i, :], vn[r, b, i, :], start=True, stop=True)
                        o = 256 + (d * 2 + i // 2) * 64
                        last = mm(bank[q, o:o + 64], ku[r, b, i, :], vn[r, b, i, :], start=True, stop=True)
                    if hf == 0:
                        tiles_apart(last)
                last.then_inc(d_full, 1)

            def by(b, c, part):
                u = U_FIRST[("by", b, c - c % 2)]
                y_hi, y_lo = (yM_hi, yM_lo) if b == 1 else (yA_hi, yA_lo)
                if c == 0 and part == 0:
                    evacuated((D_FIRST[("attn_o", RT - 1, AKV - 1)], D_FIRST[("mout", MH - 1)], D_FIRST[("oT",)] + 3)[b])
                columns_product(G_FIRST[("by", b, c)], u, P * (c % 2), y_hi, y_lo, 4, part, PARTS["by"])

            def in_parts(whole, part):
                if whole[0] == "by":
                    by(*whole[1:], part)
                elif whole[0] == "bg":
                    columns_product(G_FIRST[whole], U_FIRST[whole], 0, hT_hi, hT_lo, KT, part, PARTS["bg"])
                else:
                    rows_product(G_FIRST[whole], U_FIRST[whole], hT_hi, hT_lo, units=stage_units(whole), pieces=[part])

            for st in order:
                kind, a = st[0], st[1:]
                f, u = D_FIRST[st], U_FIRST[st]
                if kind == "small":
                    small()
                elif kind == "bias_a":
                    bias_a()
                elif kind == "bias_b":
                    bias_b(*a)
                elif kind == "small_b":
                    small_b()
                elif kind == "baproj":
                    baproj()
                elif kind == "baT":
                    baT_()
                elif kind == "part":
                    in_parts(*a)
                elif kind in PARTS:
                    in_parts(st, PARTS[kind] - 1)
                elif kind == "xT":
                    pe.wait_ge(x_scaled, 1)
                    transposes(f, [xt[:, rt, a[0] * P:(a[0] + 1) * P] for rt in range(RT)])
                    if a[0] >= 4:
                        first = ("dnproj", 0)
                        columns_product(G_FIRST[first], U_FIRST[first], 0, hT_hi, hT_lo, KT, a[0] - 4, KT, "xT")
                elif kind == "mT":
                    pe.wait_ge(x_scaled, 2)
                    transposes(f, [mx[:, m, a[0] * P:(a[0] + 1) * P] for m in range(MT)])
                elif kind == "dnproj":
                    if a[0] == 0:
                        for k in range(4, KT):
                            columns_product(G_FIRST[st], u, 0, hT_hi, hT_lo, KT, k, KT, "xT")
                    else:
                        columns_product(G_FIRST[st], u, 0, hT_hi, hT_lo, KT)
                elif kind in ("aqproj", "akvproj"):
                    rows_product(G_FIRST[st], u, hT_hi, hT_lo)
                elif kind == "mkvproj":
                    evacuated(D_FIRST[("mT", KT - 1)])
                    rows_product(G_FIRST[st], u, memT_hi, memT_lo, MT)
                elif kind == "gates_b":
                    gates_b()
                elif kind == "dnnat":
                    rt, j = a
                    pe.wait_ge(dn_silu, 4 * j + 4)
                    transposes(f, [dnc[:, 4 * j + t, rt * P:(rt + 1) * P] for t in range(4)])
                elif kind == "aT":
                    pe.wait_ge(aq_scaled, 1)
                    pe.wait_ge(a_scaled, 1)
                    for t in range(4):
                        transposes(f + t, [anat[:, rt, t * P:(t + 1) * P] for rt in range(RT)])
                    for g in range(AKV):
                        bank = d_claim(f + 4 + g)
                        for rt in range(RT):
                            for side in range(2):
                                last = mm(bank[64 * side:64 * side + 64, rt * P:(rt + 1) * P], anat[:, rt, ATTN_Q + 64 * g:ATTN_Q + 64 * g + 64],
                                          const("ident"), start=True, stop=True)
                        last.then_inc(d_full, 1)
                elif kind == "attn_s":
                    attn_s(*a)
                elif kind == "attn_p":
                    attn_p(*a)
                elif kind == "attn_o":
                    attn_o(*a)
                elif kind == "mkT":
                    pe.wait_ge(mk_scaled, 1)
                    for j in range(MH // 2):
                        transposes(f + j, [mkn[:, m, (2 * j + i) * P:(2 * j + i + 1) * P] for i in range(2) for m in range(MT)])
                elif kind == "mqT":
                    pe.wait_ge(mq_scaled, 1)
                    for h in range(MH):
                        transposes(f + h, [mqn[:, rt, h * P:(h + 1) * P] for rt in range(RT)])
                elif kind == "mscore":
                    mscore(*a)
                elif kind == "mtrans":
                    mtrans(*a)
                elif kind == "mout":
                    mout(*a)
                elif kind == "dnT":
                    pe.wait_ge(dn_scaled, 2)
                    for j in range(2):
                        for t in range(4):
                            transposes(f + 4 * j + t, [dn_nat[:, j, rt, t * P:(t + 1) * P] for rt in range(RT)])
                elif kind == "decay":
                    decay(*a)
                elif kind == "levw":
                    levw(*a)
                elif kind == "levy":
                    levy(*a)
                elif kind == "uw":
                    uw(*a)
                elif kind == "scanv":
                    scanv(*a)
                elif kind == "scans":
                    scans(*a)
                elif kind == "oT":
                    pe.wait_ge(o_scaled, 1)
                    pe.wait_ge(o_scaled_too, 1)
                    for t in range(4):
                        transposes(f + t, [o_nat[:, rt, t * P:(t + 1) * P] for rt in range(RT)])
                elif kind == "wout":
                    rows_product(G_FIRST[st], u, m_hi, m_lo, made=m_split)
                elif kind == "h2T":
                    pe.wait_ge(x2_scaled, 1 + a[0] // 4)
                    pe.wait_ge(x2_last, 1 + a[0] // 4)
                    transposes(f, [xn[:, rt, a[0] * P:(a[0] + 1) * P] for rt in range(RT)])
                    if a[0] >= 4:
                        for i in range(2):
                            columns_product(G_FIRST[("up", 0)] + i, U_FIRST[("up", 0)] + i, 0, hT_hi, hT_lo, KT, a[0] - 4, KT, "h2T")
                elif kind == "up":
                    if a[0] == 0:
                        for k in range(4, KT):
                            for i in range(2):
                                columns_product(G_FIRST[st] + i, u + i, 0, hT_hi, hT_lo, KT, k, KT, "h2T")
                    else:
                        columns_product(G_FIRST[st], u, 0, hT_hi, hT_lo, KT)
                        columns_product(G_FIRST[st] + 1, u + 1, 0, hT_hi, hT_lo, KT)
                elif kind == "down":
                    rows_product(G_FIRST[st], u, act_hi, act_lo, made=f_split)

        @block.scalar
        def _(act):
            steps = [0]

            def link(ins):
                steps[0] += 1
                ins.then_inc(act_step, 1)
                act.wait_ge(act_step, steps[0])

            def splits(place, table=SPLITS_AT):
                for u in table[place]:
                    if u >= len_units:
                        continue
                    act.wait_ge(raw_loaded[u % RAW_N], 16 * (u // RAW_N + 1))
                    if u >= HL_N:
                        name, value = UNIT_DONE[u - HL_N]
                        act.wait_ge(SIG[name], value)
                    nc.scalar.copy(unit_view(w_hi, u), unit_view(raw, u)).then_inc(hi_made, 1)

            def filled(f):
                act.wait_ge(d_full, f + 1)
                return db[f % 4]

            def g_filled(f):
                act.wait_ge(g_full, f + 1)
                return gb[f % 4]

            def root():
                act.wait_ge(var_made, NORM[st] + 1)
                v = {"mnorm": st_x[:, RT:RT + MT], "anorm": st_a[:, :, AH:] if a == (1,) else st_a[:, :, 0:AH],
                     "mknorm": st_m[:, 16:24], "mqnorm": st_m[:, 0:16], "dnnorm": st_d[:, a[0]] if kind == "dnnorm" else None,
                     "osum": st_o[:], "x2norm": st_x[:, 0:RT]}[kind]
                nc.scalar.activation(v, v, ACT.Sqrt).then_inc(sqrt_made, 1)

            def col(i):
                return pcol[:, i:i + 1]

            def silu_of(c):
                f = G_FIRST[("dnproj", c)]
                act.wait_ge(g_free[f % 4], f // 4 + 1)
                nc.scalar.activation(dnc[:, c, :], dnc[:, c, :], ACT.Silu).then_inc(dn_silu, 1)

            def conv_start(c, half_, b):
                f = G_FIRST[st] + half_
                bank = g_filled(f)
                ct = half_ * FT + c
                if c >= 2:
                    act.wait_ge(f_split, c - 1)
                nc.scalar.activation(u_gv[:, b, half_, :], bank[:, :], ACT.Identity, bias=fcol[:, 3 * 2 * FT + ct:3 * 2 * FT + ct + 1],
                                     scale=fcol[:, 2 * FT + ct:2 * FT + ct + 1]).then_inc(ua_made, 1)

            for place_, st in enumerate(order):
                kind, a = st[0], st[1:]
                f, fg = D_FIRST[st], G_FIRST[st]
                if st == ("xT", 4):
                    splits(-1)
                if kind == "small":
                    nc.scalar.copy(pcol[:, 0:N_PC], filled(f)[:, 0:N_PC]).then_inc(d_free[f % 4], 1)
                elif kind == "small_b":
                    for i in range(2):
                        nc.scalar.copy(fcol[:, i * 2 * FH:(i + 1) * 2 * FH], filled(f + i)[:, 0:2 * FH]).then_inc(d_free[(f + i) % 4], 1)
                elif kind == "xnorm":
                    for t in range(RT):
                        act.wait_ge(x_in[t], 16)
                        nc.scalar.activation(scr[:], xt[:, t, :], ACT.Square, accum_out=st_x[:, t:t + 1]).then_inc(ss_made, 1)
                        act.wait_ge(var_made, t + 1)
                        nc.scalar.activation(st_x[:, t:t + 1], st_x[:, t:t + 1], ACT.Sqrt).then_inc(sqrt_made, 1)
                elif kind == "mnorm":
                    act.wait_ge(mem_in, 16)
                    for m in range(MT):
                        ins = nc.scalar.activation(scr[:], mx[:, m, :], ACT.Square, accum_out=st_x[:, RT + m:RT + m + 1])
                        if m == MT - 1:
                            ins.then_inc(ss_made, 1)
                        else:
                            link(ins)
                    root()
                elif kind == "xT":
                    act.wait_ge(d_free[D_FIRST[("small",)] % 4], D_FIRST[("small",)] // 4 + 1)
                    nc.scalar.activation(hT_hi[:, a[0], :], filled(f)[:, :], ACT.Identity, scale=col(PC_MIX + a[0])).then_inc(part_hi, 1)
                elif kind == "mT":
                    nc.scalar.activation(memT_hi[:, a[0], :], filled(f)[:, 0:N_MEM], ACT.Identity, scale=col(PC_MEM + a[0])).then_inc(part_hi, 1)
                elif kind == "bias_a":
                    nc.scalar.copy(bT[0:AH, :], filled(f)[0:AH, 0:BIAS_N + 1]).then_inc(d_free[f % 4], 1)
                elif kind == "bias_b":
                    nc.scalar.copy(bias[:, a[0], :], filled(f)[:, 0:3 * P]).then_inc(d_free[f % 4], 1)
                elif kind == "dnproj":
                    splits(place_)
                    c = a[0]
                    nc.scalar.activation(dnc[:, c, :], g_filled(fg)[:, :], ACT.Identity, scale=col((DN_TAPS // 2) * 12 + c)).then_inc(tap_made, 1)
                    if c:
                        silu_of(c - 1)
                    if c == 11:
                        silu_of(c)
                elif kind == "baproj":
                    nc.scalar.copy(baT[:], g_filled(fg)[0:4 * DH, :]).then_inc(g_free[fg % 4], 1)
                elif kind == "bsplit":
                    act.wait_ge(ba_in, 16)
                    nc.scalar.copy(ba_hi[:], w_ba[:]).then_inc(ba_rounded, 1)
                elif kind == "baT":
                    nc.scalar.copy(ba[:].rearrange("p t c -> p (t c)"), filled(f)[:, 0:32 * RT]).then_inc(d_free[f % 4], 1)
                elif kind == "zproj":
                    splits(place_)
                    for rt in range(RT):
                        nc.scalar.activation(zs[:, rt, :], g_filled(fg + rt)[:, :], ACT.Silu).then_inc(g_free[(fg + rt) % 4], 1)
                elif kind == "gates_a":
                    act.wait_ge(sp_made, 1)
                    link(nc.scalar.activation(sp[:, 1], sp[:, 0], ACT.Abs))
                    link(nc.scalar.activation(sp[:, 1], sp[:, 1], ACT.Exp, scale=-1.0))
                    link(nc.scalar.activation(ealog[:], rowp[:, 0:16], ACT.Exp))
                    nc.scalar.activation(sp[:, 1], sp[:, 1], ACT.Ln, bias=1.0).then_inc(softplus_made, 1)
                    act.wait_ge(sp_made, 2)
                    nc.scalar.activation(sp[:, 1], ba[:, :, 0:16], ACT.Sigmoid).then_inc(beta_made, 1)
                elif kind == "gates_b":
                    nc.scalar.activation(e_slot[:], filled(f)[:, 0:192], ACT.Exp).then_inc(d_free[f % 4], 1)
                elif kind == "aqproj":
                    splits(place_)
                    for rt in range(RT):
                        nc.scalar.copy(anat[:, rt, 0:ATTN_Q], g_filled(fg + rt)[:, :]).then_inc(g_free[(fg + rt) % 4], 1)
                elif kind == "akvproj":
                    splits(place_)
                    for rt in range(RT):
                        bank = g_filled(fg + rt)
                        nc.scalar.copy(anat[:, rt, ATTN_Q:], bank[:, 0:ATTN_KV])
                        nc.scalar.copy(av[:, rt, :], bank[:, ATTN_KV:2 * ATTN_KV]).then_inc(g_free[(fg + rt) % 4], 1)
                elif kind in ("anorm", "mknorm", "mqnorm", "dnnorm", "osum"):
                    root()
                elif kind == "dnnat":
                    nc.scalar.copy(dn_nat[:, a[1], a[0], :], filled(f)[:, :]).then_inc(d_free[f % 4], 1)
                elif kind == "aT":
                    for t in range(4):
                        nc.scalar.activation(aqT[:, t, :], filled(f + t)[:, :], ACT.Identity, scale=col(PC_AQ)).then_inc(d_free[(f + t) % 4], 1)
                    for g in range(AKV):
                        nc.scalar.activation(akT[:, g, :], filled(f + 4 + g)[:, :], ACT.Identity, scale=col(PC_AK)).then_inc(d_free[(f + 4 + g) % 4], 1)
                elif kind == "attn_e":
                    n, g = a
                    kbs = key_blocks(n)
                    lo, hi = kbs[0] * P, (kbs[-1] + 1) * P
                    for j in range(2):
                        h2 = slice(2 * j, 2 * j + 2)
                        act.wait_ge(attn_max, 2 * NTH[st] + j + 1)
                        nc.scalar.activation(st_s[:, 5, h2], st_s[:, 3, h2], ACT.Exp)
                        for i in range(2 * j, 2 * j + 2):
                            ins = nc.scalar.activation(sc[:, i, lo:hi], sc[:, i, lo:hi], ACT.Exp, bias=st_s[:, 2, i:i + 1], accum_out=st_s[:, 4, i:i + 1])
                        ins.then_inc(attn_exp, 1)
                elif kind == "attn_p":
                    for j, kb in enumerate(key_blocks(a[0])):
                        nc.scalar.copy(pTs[kb].rearrange("p i q -> p (i q)"), filled(f + j)[:, :]).then_inc(d_free[(f + j) % 4], 1)
                elif kind == "attn_o":
                    n, g = a
                    nc.scalar.copy(yA_hi[:, 2 * g:2 * g + 2, n * P:(n + 1) * P], filled(f)[:, 0:2 * P].rearrange("p (i q) -> p i q", i=2)).then_inc(part_hi, 1)
                elif kind == "mqproj":
                    splits(place_)
                    for rt in range(RT):
                        nc.scalar.copy(mqn[:, rt, :], g_filled(fg + rt)[:, :]).then_inc(g_free[(fg + rt) % 4], 1)
                elif kind == "mkvproj":
                    splits(place_)
                    for m in range(MT):
                        dst = mv if a[0] else mkn
                        nc.scalar.copy(dst[:, m, :], g_filled(fg + m)[:, :]).then_inc(g_free[(fg + m) % 4], 1)
                elif kind == "mqT":
                    for h in range(MH):
                        nc.scalar.activation(mqT[:, h, :], filled(f + h)[:, :], ACT.Identity, scale=col(PC_MQ)).then_inc(d_free[(f + h) % 4], 1)
                elif kind == "mkT":
                    for j in range(MH // 2):
                        nc.scalar.activation(mkT[:, 2 * j:2 * j + 2, :], filled(f + j)[:, :].rearrange("p (h m) -> p h m", h=2), ACT.Identity, scale=col(PC_MK)).then_inc(d_free[(f + j) % 4], 1)
                elif kind == "mexp":
                    rt = a[0]
                    fs = D_FIRST[("mscore", rt)]
                    for j in range(2):
                        act.wait_ge(mem_max, 2 * rt + j + 1)
                        bank = filled(fs + j)
                        for i in range(2):
                            h = 2 * j + i
                            ins = nc.scalar.activation(msc[:, rt, h, :], bank[:, i * N_MEM:(i + 1) * N_MEM], ACT.Exp, bias=st_s[:, 6, h:h + 1], accum_out=st_s[:, 7, h:h + 1])
                        ins.then_inc(d_free[(fs + j) % 4], 1)
                elif kind == "mtrans":
                    for m in range(MT):
                        nc.scalar.copy(mpTs[m], filled(f + m)[:, :]).then_inc(d_free[(f + m) % 4], 1)
                elif kind == "mout":
                    nc.scalar.copy(yM_hi[:, a[0], :], filled(f)[:, :]).then_inc(part_hi, 1)
                elif kind == "dnT":
                    for j in range(8):
                        nc.scalar.copy(qkT[:, j, :], filled(f + j)[:, :]).then_inc(d_free[(f + j) % 4], 1)
                elif kind == "decay":
                    u = 2 * a[0] + a[1]
                    nc.scalar.activation(dec[:, u % 2, 0].rearrange("p h c -> p (h c)"), filled(f)[:, 0:HB * CHUNK], ACT.Exp).then_inc(d_free[f % 4], 1)
                elif kind == "levw":
                    if a[2]:
                        nc.scalar.copy(wx[:, (2 * a[0] + a[1]) % 2].rearrange("p h c -> p (h c)"), filled(f)[:, 0:HB * CHUNK]).then_inc(d_free[f % 4], 1)
                elif kind in ("by", "part"):
                    splits(place_)
                elif kind == "bg":
                    splits(place_)
                    b, c = a
                    dst = merged[:, c, :] if b == 0 else tg[:]
                    if b and NTH[st] > KT:
                        act.wait_ge(gate_used, NTH[st] - KT)
                    nc.scalar.activation(dst, g_filled(fg)[:, :], ACT.Tanh, scale=0.5).then_inc(g_free[fg % 4], 1)
                    if b == 2:
                        act.wait_ge(gate_used, NTH[st] + 1 - KT)
                        nc.scalar.mul(m_hi[:, c, :], merged[:, c, :], 0.5).then_inc(mhi_made, 1)
                elif kind == "oT":
                    for t in range(4):
                        nc.scalar.activation(yA_hi[:, t, :], filled(f + t)[:, :], ACT.Identity, scale=col(PC_DO)).then_inc(part_hi, 1)
                elif kind == "wout":
                    splits(place_)
                    act.wait_ge(m_split, KT)
                    for rt in range(RT):
                        act.wait_ge(g_free[(fg + rt) % 4], (fg + rt) // 4 + 1)
                        stat = RT * a[0] + rt
                        ins = nc.scalar.activation(tg[:], x2[:, rt, 512 * a[0]:512 * a[0] + 512], ACT.Square, accum_out=st_x[:, stat:stat + 1])
                        if stat == 2 * RT - 1:
                            ins.then_inc(ss_made, 1)
                        else:
                            link(ins)
                elif kind == "x2norm":
                    root()
                    act.wait_ge(x2_root, 1)
                    for cc in (slice(0, D // 2), slice(D // 2, D)):
                        nc.scalar.mul(xn[:, RT - 1, cc], x2[:, RT - 1, cc], st_x[:, RT - 1:RT]).then_inc(x2_last, 1)
                elif kind == "h2T":
                    nc.scalar.activation(hT_hi[:, a[0], :], filled(f)[:, :], ACT.Identity, scale=col(PC_FFN + a[0])).then_inc(part_hi, 1)
                elif kind == "up":
                    splits(place_)
                    c = a[0]
                    conv_start(c, 0, c % 2)
                    conv_start(c, 1, c % 2)
                    act.wait_ge(g_free[fg % 4], fg // 4 + 1)
                    nc.scalar.activation(u_gv[:, c % 2, 0, :], u_gv[:, c % 2, 0, :], ACT.Silu).then_inc(silu_made, 1)
                    act.wait_ge(glu_made, c + 1)
                    nc.scalar.copy(act_hi[:, c, :], u_gv[:, c % 2, 1, :]).then_inc(fhi_made, 1)
                elif kind == "down":
                    splits(place_)
                if kind in ROWS:
                    splits(place_, SPLITS_AFTER)

        @block.vector
        def _(dve):
            v = nc.vector
            steps = [0]

            def link(ins):
                steps[0] += 1
                ins.then_inc(dve_step, 1)
                dve.wait_ge(dve_step, steps[0])

            def splits(place, table=SPLITS_AT):
                for u in table[place]:
                    if u >= len_units:
                        continue
                    dve.wait_ge(hi_made, u + 1)
                    v.tensor_tensor(unit_view(w_lo, u), unit_view(raw, u), unit_view(w_hi, u).bitcast(F), ALU.subtract).then_inc(lo_made, 1)

            def filled(f):
                dve.wait_ge(d_full, f + 1)
                return db[f % 4]

            def g_filled(f):
                dve.wait_ge(g_full, f + 1)
                return gb[f % 4]

            def inverse_root(stat, n_mean, made=None):
                v.tensor_scalar(stat, stat, 1.0 / n_mean, EPS, ALU.mult, ALU.add).then_inc(var_made, 1)
                dve.wait_ge(sqrt_made, NORM[st] + 1)
                if made is None:
                    link(v.reciprocal(stat, stat))
                else:
                    v.reciprocal(stat, stat).then_inc(made, 1)
                    dve.wait_ge(made, 1)

            def squares(dst, src, width, d=64, room=None):
                room = tg if room is None else room
                link(v.tensor_tensor(room[:, 0:width], src, src, ALU.mult))
                link(v.tensor_reduce(dst, room[:, 0:width].rearrange("p (h d) -> p h d", d=d), X, ALU.add))

            def g_evacuated(f):
                dve.wait_ge(g_free[f % 4], f // 4 + 1)

            def low_part(dst, bank, hi, scale=None):
                if scale is None:
                    return v.tensor_tensor(dst, bank, hi.bitcast(F), ALU.subtract)
                return v.scalar_tensor_tensor(dst, bank, scale, hi.bitcast(F), ALU.mult, ALU.subtract)

            def col(i):
                return pcol[:, i:i + 1]

            def wide(ap, n=64):
                return ap.unsqueeze(len(ap.shape)).to_broadcast(list(ap.shape) + [n])

            his = [0]

            def hi_part():
                his[0] += 1
                dve.wait_ge(part_hi, his[0])

            v.memset(btab[BUCKETS:BUCKETS + 1, :], NEG).then_inc(table_ready, 1)
            for place_, st in enumerate(order):
                kind, a = st[0], st[1:]
                f, fg = D_FIRST[st], G_FIRST[st]
                if st == ("xT", 4):
                    splits(-1)
                if kind == "xnorm":
                    for t in range(RT):
                        rms = st_x[:, t:t + 1]
                        dve.wait_ge(ss_made, t + 1)
                        v.tensor_scalar(rms, rms, 1.0 / D, EPS, ALU.mult, ALU.add).then_inc(var_made, 1)
                        dve.wait_ge(sqrt_made, t + 1)
                        link(v.reciprocal(rms, rms))
                        ins = v.tensor_scalar(xt[:, t, :], xt[:, t, :], rms, None, ALU.mult)
                    ins.then_inc(x_scaled, 1)
                elif kind == "mnorm":
                    dve.wait_ge(ss_made, RT + 1)
                    inverse_root(st_x[:, RT:RT + MT], D)
                    for m in range(MT):
                        ins = v.tensor_scalar(mx[:, m, :], mx[:, m, :], st_x[:, RT + m:RT + m + 1], None, ALU.mult)
                    ins.then_inc(x_scaled, 1)
                elif kind == "xT":
                    dve.wait_ge(d_free[D_FIRST[("small",)] % 4], D_FIRST[("small",)] // 4 + 1)
                    hi_part()
                    low_part(hT_lo[:, a[0], :], filled(f)[:, :], hT_hi[:, a[0], :], col(PC_MIX + a[0])).then_inc(d_free[f % 4], 1)
                elif kind == "mT":
                    hi_part()
                    low_part(memT_lo[:, a[0], :], filled(f)[:, 0:N_MEM], memT_hi[:, a[0], :], col(PC_MEM + a[0])).then_inc(d_free[f % 4], 1)
                elif kind == "dnproj":
                    splits(place_)
                    c = a[0]
                    bank = g_filled(fg)
                    dve.wait_ge(tap_made, c + 1)
                    for j in (0, 1, 3, 4):
                        d = j - DN_TAPS // 2
                        lo, hi = max(0, -d), SEQ - max(0, d)
                        y = dnc[:, c, lo:hi]
                        ins = v.scalar_tensor_tensor(y, bank[:, lo + d:hi + d], col(j * 12 + c), y, ALU.mult, ALU.add)
                        if j == 4:
                            ins.then_inc(g_free[fg % 4], 1)
                        else:
                            link(ins)
                elif kind in ("zproj", "aqproj", "akvproj", "mqproj", "mkvproj", "by", "part"):
                    splits(place_)
                elif kind == "bsplit":
                    dve.wait_ge(ba_rounded, 1)
                    v.tensor_tensor(ba_lo[:], w_ba[:], ba_hi[:].bitcast(F), ALU.subtract).then_inc(ba_split, 1)
                elif kind == "gates_a":
                    fb = D_FIRST[("baT",)]
                    dve.wait_ge(d_free[fb % 4], fb // 4 + 1)
                    dve.wait_ge(rows_in, 16 * 3)
                    dt = rowp[:, 16:32].unsqueeze(1).to_broadcast([P, RT, 16])
                    v.tensor_tensor(sp[:, 0], ba[:, :, 16:32], dt, ALU.add).then_inc(sp_made, 1)
                    dve.wait_ge(softplus_made, 1)
                    link(v.scalar_tensor_tensor(sp[:, 0], sp[:, 0], 0.0, sp[:, 1], ALU.max, ALU.add))
                    v.scalar_tensor_tensor(sp[:, 0], sp[:, 0], -1.0, ealog[:].unsqueeze(1).to_broadcast([P, RT, 16]), ALU.mult, ALU.mult).then_inc(sp_made, 1)
                    dve.wait_ge(sp_made, 2)
                    dve.wait_ge(beta_made, 1)
                    for src, dst in ((sp[:, 1], b_slot), (sp[:, 0], g_slot)):
                        for hf in range(2):
                            r = slice(64 * hf, 64 * hf + 64)
                            v.tensor_copy(dst[r, hf::2, :], src[r, :, 0:8])
                            for i in range(RT):
                                ins = v.tensor_copy(dst[r, 2 * i + 1 - hf, :], src[r, RT - 1 - i, 8:16])
                    ins.then_inc(slots_made, 1)
                elif kind == "anorm":
                    cols, hh = ((slice(0, ATTN_Q), slice(0, AH)), (slice(ATTN_Q, ATTN_Q + ATTN_KV), slice(AH, AH + AKV)))[a[0]]
                    for rt in range(RT):
                        g_evacuated(G_FIRST[("akvproj",) if a[0] else ("aqproj",)] + rt)
                    for rt in range(RT):
                        squares(st_a[:, rt, hh], anat[:, rt, cols], cols.stop - cols.start)
                    inverse_root(st_a[:, :, hh], AD)
                    if a[0] == 0:
                        v.tensor_scalar(st_a[:, :, hh], st_a[:, :, hh], AD ** -0.5, None, ALU.mult).then_inc(aq_inverse, 1)
                        continue
                    for rt in range(RT):
                        x3 = heads(anat[:, rt, cols])
                        ins = v.tensor_tensor(x3, x3, wide(st_a[:, rt, hh]), ALU.mult)
                    ins.then_inc(a_scaled, 1)
                elif kind == "attn_s":
                    n, g = a
                    kbs = key_blocks(n)
                    lo, hi = kbs[0] * P, (kbs[-1] + 1) * P
                    fb = D_FIRST[("bias_b", AH - 1)]
                    dve.wait_ge(d_free[fb % 4], fb // 4 + 1)
                    if NTH[st]:
                        prev = ("attn_p",) + divmod(NTH[st] - 1, AKV)
                        dve.wait_ge(d_full, D_FIRST[prev] + d_fills(prev))
                    sink = rowp[:, 32 + 4 * g:36 + 4 * g]
                    for j in range(2):
                        h2 = slice(2 * j, 2 * j + 2)
                        for i in range(2 * j, 2 * j + 2):
                            bank = filled(f + i)
                            v.tensor_tensor(sc[:, i, lo:hi], bank[:, lo:hi], bias[:, 4 * g + i, lo:hi], ALU.add).then_inc(d_free[(f + i) % 4], 1)
                        for i in range(2 * j, 2 * j + 2):
                            dve.wait_ge(d_free[(f + i) % 4], (f + i) // 4 + 1)
                        link(v.tensor_reduce(st_s[:, 0, h2], sc[:, h2, lo:hi], X, ALU.max))
                        link(v.tensor_tensor(st_s[:, 1, h2], st_s[:, 0, h2], sink[:, h2], ALU.max))
                        link(v.tensor_scalar(st_s[:, 2, h2], st_s[:, 1, h2], -1.0, None, ALU.mult))
                        v.tensor_tensor(st_s[:, 3, h2], sink[:, h2], st_s[:, 2, h2], ALU.add).then_inc(attn_max, 1)
                elif kind == "attn_t":
                    kbs = key_blocks(a[0])
                    lo, hi = kbs[0] * P, (kbs[-1] + 1) * P
                    for j in range(2):
                        h2 = slice(2 * j, 2 * j + 2)
                        dve.wait_ge(attn_exp, 2 * NTH[st] + j + 1)
                        link(v.tensor_tensor(st_s[:, 4, h2], st_s[:, 4, h2], st_s[:, 5, h2], ALU.add))
                        link(v.reciprocal(st_s[:, 4, h2], st_s[:, 4, h2]))
                        for i in range(2 * j, 2 * j + 2):
                            ins = v.tensor_scalar(sc[:, i, lo:hi], sc[:, i, lo:hi], st_s[:, 4, i:i + 1], None, ALU.mult)
                    ins.then_inc(attn_scaled, 1)
                elif kind == "attn_o":
                    n, g = a
                    hi_part()
                    dst = slice(n * P, (n + 1) * P)
                    low_part(yA_lo[:, 2 * g:2 * g + 2, dst], filled(f)[:, 0:2 * P].rearrange("p (i q) -> p i q", i=2),
                             yA_hi[:, 2 * g:2 * g + 2, dst]).then_inc(d_free[f % 4], 1)
                elif kind == "mknorm":
                    for m in range(MT):
                        g_evacuated(G_FIRST[("mkvproj", 0)] + m)
                    for m in range(MT):
                        squares(st_m[:, 16 + 4 * m:20 + 4 * m], mkn[:, m, :], 512, MD)
                    inverse_root(st_m[:, 16:24], MD)
                    for m in range(MT):
                        x3 = mkn[:, m, :].rearrange("p (h d) -> p h d", d=MD)
                        ins = v.tensor_tensor(x3, x3, wide(st_m[:, 16 + 4 * m:20 + 4 * m], MD), ALU.mult)
                    ins.then_inc(mk_scaled, 1)
                elif kind == "mqnorm":
                    inverse_root(st_m[:, 0:16], MD)
                    v.tensor_scalar(st_m[:, 0:16], st_m[:, 0:16], MD ** -0.5, None, ALU.mult).then_inc(mq_inverse, 1)
                elif kind == "mqsquare":
                    g_evacuated(G_FIRST[("mqproj",)] + a[0])
                    squares(st_m[:, 4 * a[0]:4 * a[0] + 4], mqn[:, a[0], :], 512, MD)
                elif kind == "mscore":
                    for j in range(2):
                        h2 = slice(2 * j, 2 * j + 2)
                        link(v.tensor_reduce(st_s[:, 0, h2], filled(f + j)[:, :].rearrange("p (h m) -> p h m", h=2), X, ALU.max))
                        v.tensor_scalar(st_s[:, 6, h2], st_s[:, 0, h2], -1.0, None, ALU.mult).then_inc(mem_max, 1)
                elif kind == "mscale":
                    rt = a[0]
                    fs = D_FIRST[("mscore", rt)] + 1
                    dve.wait_ge(d_free[fs % 4], fs // 4 + 1)
                    link(v.reciprocal(st_s[:, 7, :], st_s[:, 7, :]))
                    for h in range(MH):
                        ins = v.tensor_scalar(msc[:, rt, h, :], msc[:, rt, h, :], st_s[:, 7, h:h + 1], None, ALU.mult)
                    ins.then_inc(mem_scaled, 1)
                elif kind == "mout":
                    hi_part()
                    low_part(yM_lo[:, a[0], :], filled(f)[:, :], yM_hi[:, a[0], :]).then_inc(d_free[f % 4], 1)
                elif kind == "dnnorm":
                    j = a[0]
                    fn = D_FIRST[("dnnat", RT - 1, j)]
                    for b4 in range(4):
                        dve.wait_ge(d_free[(fn - b4) % 4], (fn - b4) // 4 + 1)
                    for rt in range(RT):
                        squares(st_d[:, j, rt, :], dn_nat[:, j, rt, :], DN_W)
                    inverse_root(st_d[:, j], 1)
                    v.tensor_scalar(st_d[:, j], st_d[:, j], 1.0 if j else DK ** -0.5, None, ALU.mult).then_inc(dn_inverse, 1)
                elif kind == "dnT":
                    dve.wait_ge(d_full, f + 1)
                    v.memset(S[:].rearrange("p a b c d -> p (a b c d)"), 0.0).then_inc(state_zero, 1)
                elif kind == "decay":
                    s, hb = a
                    u = 2 * s + hb
                    bank = filled(f + 1)[:, :].rearrange("p (h j n) -> p h j n", h=HB, j=2)
                    dve.wait_ge(em_made, u + 1)
                    v.tensor_tensor(at_[:, u % 4], bank[:, :, 0, :], dec[:, u % 2, 0], ALU.mult)
                    v.tensor_tensor(nn[:, u % 2], bank[:, :, 1, :], dec[:, u % 2, 1], ALU.mult).then_inc(d_free[(f + 1) % 4], 1)
                elif kind == "levw":
                    s, hb, l = a
                    b = (2 * s + hb) % 2
                    if l == 0:
                        eye = const("ident64").unsqueeze(1).to_broadcast([P, HB, CHUNK])
                        dve.wait_ge(consts_in, 16)
                        dve.wait_ge(nm_made, level_no(s, hb, 0) + 1)
                        v.tensor_tensor(yx[:, b, 0], eye, nm[:, b, 0], ALU.subtract)
                        v.tensor_tensor(yx[:, b, 1], eye, heads(filled(f)[:, 0:HB * CHUNK]), ALU.subtract).then_inc(d_free[f % 4], 1)
                elif kind == "levy":
                    s, hb, l = a
                    b = (2 * s + hb) % 2
                    n = 2 if l < LEVELS - 1 else 1
                    y = yx[:, b].rearrange("p a h c -> p (a h c)")[:, 0:n * HB * CHUNK]
                    fl = f_level(s, hb, l - 1)
                    dve.wait_ge(d_free[fl % 4], fl // 4 + 1)
                    v.tensor_tensor(y, y, filled(f)[:, 0:n * HB * CHUNK], ALU.subtract).then_inc(d_free[f % 4], 1)
                elif kind == "uw":
                    s, hb = a
                    b = (2 * s + hb) % 2
                    bank = filled(f)
                    v.tensor_tensor(uu[:, b], heads(bank[:, 0:256]), wide(b_slot[:, s, HB * hb:HB * hb + HB]), ALU.mult)
                    v.tensor_copy(wt[:, b].rearrange("p a i c -> p (a i c)"), bank[:, 256:512]).then_inc(d_free[f % 4], 1)
                elif kind == "scanv":
                    s, hb = a
                    b = (2 * s + hb) % 2
                    bank = filled(f)
                    fu = D_FIRST[("uw", s, hb)]
                    dve.wait_ge(d_free[fu % 4], fu // 4 + 1)
                    link(v.tensor_tensor(vn[:, b], heads(bank[:, 0:256]), wide(b_slot[:, s, HB * hb:HB * hb + HB]), ALU.mult))
                    v.tensor_tensor(vn[:, b], uu[:, b], vn[:, b], ALU.subtract).then_inc(vn_made, 1)
                    if s:
                        dve.wait_ge(o_added, 2 * (s - 1) + hb + 1)
                    v.tensor_tensor(o1[:, b], heads(bank[:, 256:512]), wide(decay_of(0, s, hb)), ALU.mult).then_inc(d_free[f % 4], 1)
                elif kind == "scans":
                    s, hb = a
                    b = (2 * s + hb) % 2
                    fv = D_FIRST[("scanv", s, hb)]
                    dve.wait_ge(d_free[fv % 4], fv // 4 + 1)
                    egl = e_slot[:, 0:64].rearrange("p (q d i h) -> p q d i h", q=2, d=2, i=4)[:, s % 2, :, s // 2, 2 * hb:2 * hb + 2]
                    link(v.tensor_tensor(S[:, hb], S[:, hb], wide(egl), ALU.mult))
                    bank = filled(f)
                    link(v.tensor_tensor(o1[:, b], o1[:, b], heads(bank[:, 0:256]), ALU.add))
                    s_flat = S[:, hb].rearrange("p d i n -> p (d i n)")
                    v.tensor_tensor(s_flat, s_flat, bank[:, 256:512], ALU.add).then_inc(d_free[f % 4], 1)
                elif kind == "bg":
                    splits(place_)
                    b, c = a
                    fy = G_FIRST[("by", b, c)]
                    yb = g_filled(fy)
                    g_evacuated(fg)
                    if b == 0:
                        v.scalar_tensor_tensor(merged[:, c, :], merged[:, c, :], 1.0, yb[:, :], ALU.add, ALU.mult).then_inc(g_free[fy % 4], 1)
                    else:
                        v.scalar_tensor_tensor(tg[:], tg[:], 1.0, yb[:, :], ALU.add, ALU.mult).then_inc(g_free[fy % 4], 1)
                        g_evacuated(fy)
                        v.tensor_tensor(merged[:, c, :], merged[:, c, :], tg[:], ALU.add).then_inc(gate_used, 1)
                        if b == 2:
                            dve.wait_ge(mhi_made, c + 1)
                            v.scalar_tensor_tensor(m_lo[:, c, :], merged[:, c, :], 0.5, m_hi[:, c, :].bitcast(F), ALU.mult, ALU.subtract).then_inc(m_split, 1)
                elif kind == "osum":
                    dve.wait_ge(o_added, 2 * NSLOT)
                    for rt in range(RT):
                        squares(st_o[:, DH * rt:DH * rt + DH], o_nat[:, rt, :], DN_W, room=at_[:].rearrange("p a h c -> p (a h c)"))
                    inverse_root(st_o[:], DK, o_inverse)
                    for rt in range(RT // 2):
                        x3 = heads(o_nat[:, rt, :])
                        link(v.tensor_tensor(x3, x3, wide(st_o[:, DH * rt:DH * rt + DH]), ALU.mult))
                        ins = v.tensor_tensor(o_nat[:, rt, :], o_nat[:, rt, :], zs[:, rt, :], ALU.mult)
                    ins.then_inc(o_scaled, 1)
                elif kind == "oT":
                    for t in range(4):
                        hi_part()
                        low_part(yA_lo[:, t, :], filled(f + t)[:, :], yA_hi[:, t, :], col(PC_DO)).then_inc(d_free[(f + t) % 4], 1)
                elif kind == "wout":
                    splits(place_)
                    dve.wait_ge(xr_in, 16)
                    cc = slice(512 * a[0], 512 * a[0] + 512)
                    for rt in range(RT):
                        v.tensor_tensor(x2[:, rt, cc], g_filled(fg + rt)[:, :], xr[:, rt, cc], ALU.add).then_inc(g_free[(fg + rt) % 4], 1)
                elif kind == "x2norm":
                    dve.wait_ge(ss_made, RT + 2)
                    link(v.tensor_tensor(st_x[:, 0:RT], st_x[:, 0:RT], st_x[:, RT:], ALU.add))
                    v.tensor_scalar(st_x[:, 0:RT], st_x[:, 0:RT], 1.0 / D, EPS, ALU.mult, ALU.add).then_inc(var_made, 1)
                    dve.wait_ge(sqrt_made, NORM[st] + 1)
                    v.reciprocal(st_x[:, 0:RT], st_x[:, 0:RT]).then_inc(x2_root, 1)
                    dve.wait_ge(x2_root, 1)
                    for cc in (slice(0, D // 2), slice(D // 2, D)):
                        for t in range(RT - 1):
                            ins = v.tensor_scalar(xn[:, t, cc], x2[:, t, cc], st_x[:, t:t + 1], None, ALU.mult)
                        ins.then_inc(x2_scaled, 1)
                elif kind == "h2T":
                    hi_part()
                    low_part(hT_lo[:, a[0], :], filled(f)[:, :], hT_hi[:, a[0], :], col(PC_FFN + a[0])).then_inc(d_free[f % 4], 1)
                elif kind == "up":
                    splits(place_)
                    c = a[0]
                    for half_ in range(2):
                        ct = half_ * FT + c
                        bank = g_filled(fg + half_)
                        dve.wait_ge(ua_made, 2 * c + half_ + 1)
                        y = u_gv[:, c % 2, half_, :]
                        link(v.scalar_tensor_tensor(y[:, 1:SEQ], bank[:, 0:SEQ - 1], fcol[:, ct:ct + 1], y[:, 1:SEQ], ALU.mult, ALU.add))
                        v.scalar_tensor_tensor(y[:, 0:SEQ - 1], bank[:, 1:SEQ], fcol[:, 4 * FT + ct:4 * FT + ct + 1], y[:, 0:SEQ - 1], ALU.mult, ALU.add).then_inc(g_free[(fg + half_) % 4], 1)
                    dve.wait_ge(silu_made, c + 1)
                    dve.wait_ge(g_free[(fg + 1) % 4], (fg + 1) // 4 + 1)
                    uv = u_gv[:, c % 2, 1, :]
                    v.tensor_tensor(uv, uv, u_gv[:, c % 2, 0, :], ALU.mult).then_inc(glu_made, 1)
                    dve.wait_ge(fhi_made, c + 1)
                    v.tensor_tensor(act_lo[:, c, :], uv, act_hi[:, c, :].bitcast(F), ALU.subtract).then_inc(f_split, 1)
                elif kind == "down":
                    splits(place_)
                    cc = slice(512 * a[0], 512 * a[0] + 512)
                    for rt in range(RT):
                        v.tensor_tensor(x2[:, rt, cc], x2[:, rt, cc], g_filled(fg + rt)[:, :], ALU.add).then_inc(g_free[(fg + rt) % 4], 1)
                if kind in ROWS:
                    splits(place_, SPLITS_AFTER)

        @block.gpsimd
        def _(pool):
            g_ = nc.gpsimd
            steps = [0]
            before = {}

            def link(ins):
                steps[0] += 1
                ins.then_inc(pool_step, 1)
                pool.wait_ge(pool_step, steps[0])

            def say(ins, made):
                before[made.name] = before.get(made.name, 0) + 1
                ins.then_inc(made, 1)
                pool.wait_ge(made, before[made.name])

            def wide(ap, n=64):
                return ap.unsqueeze(len(ap.shape)).to_broadcast(list(ap.shape) + [n])

            def four(ap):
                return ap.unsqueeze(1).to_broadcast([ap.shape[0], HB, CHUNK])

            def add_output(s, hb):
                b = (2 * s + hb) % 2
                f = D_FIRST[("scans", s, hb)]
                pool.wait_ge(d_free[f % 4], f // 4 + 1)
                for hf, _, c in halves(s):
                    r = slice(64 * hf, 64 * hf + 64)
                    dst = heads(o_nat[r, c // 2, 256 * hb:256 * hb + 256])
                    if s < NSLOT // 2:
                        ins = g_.tensor_copy(dst, o1[r, b])
                    else:
                        ins = g_.tensor_tensor(dst, dst, o1[r, b], ALU.add)
                    if hf == 0:
                        link(ins)
                say(ins, o_added)

            for st in order:
                kind, a = st[0], st[1:]
                f = D_FIRST[st]
                if kind == "dnnorm":
                    pool.wait_ge(dn_inverse, a[0] + 1)
                    for rt in range(RT):
                        x3 = heads(dn_nat[:, a[0], rt, :])
                        ins = g_.tensor_tensor(x3, x3, wide(st_d[:, a[0], rt, :]), ALU.mult)
                        if rt < RT - 1:
                            link(ins)
                    say(ins, dn_scaled)
                if kind == "osum":
                    pool.wait_ge(o_inverse, 1)
                    fz = G_FIRST[("zproj",)]
                    for rt in range(RT // 2, RT):
                        pool.wait_ge(g_free[(fz + rt) % 4], (fz + rt) // 4 + 1)
                        x3 = heads(o_nat[:, rt, :])
                        link(g_.tensor_tensor(x3, x3, wide(st_o[:, DH * rt:DH * rt + DH]), ALU.mult))
                        ins = g_.tensor_tensor(o_nat[:, rt, :], o_nat[:, rt, :], zs[:, rt, :], ALU.mult)
                        if rt < RT - 1:
                            link(ins)
                    say(ins, o_scaled_too)
                if kind == "mqnorm":
                    pool.wait_ge(mq_inverse, 1)
                    for rt in range(RT):
                        x3 = mqn[:, rt, :].rearrange("p (h d) -> p h d", d=MD)
                        ins = g_.tensor_tensor(x3, x3, wide(st_m[:, 4 * rt:4 * rt + 4], MD), ALU.mult)
                        if rt < RT - 1:
                            link(ins)
                    say(ins, mq_scaled)
                if st == ("anorm", 0):
                    pool.wait_ge(aq_inverse, 1)
                    for rt in range(RT):
                        x3 = heads(anat[:, rt, 0:ATTN_Q])
                        ins = g_.tensor_tensor(x3, x3, wide(st_a[:, rt, 0:AH]), ALU.mult)
                        if rt < RT - 1:
                            link(ins)
                    say(ins, aq_scaled)
                if kind == "levw" and a[0] > 0 and a[2] == 3:
                    add_output(a[0] - 1, a[1])
                if kind == "scans" and a[0] == NSLOT - 1:
                    add_output(*a)
                if kind == "decay":
                    s, hb = a
                    if s == hb == 0:
                        pool.wait_ge(consts_in, 16)
                        pool.wait_ge(slots_made, 1)
                        pool.wait_ge(d_full, D_FIRST[("dnT",)] + 1)
                    if hb == 0:
                        for n in range(2):
                            mine = slice(HB * n, HB * n + HB)
                            if s:
                                fu = D_FIRST[("decay", s - 1, n)] + 1
                                pool.wait_ge(d_free[fu % 4], fu // 4 + 1)
                            say(g_.tensor_tensor(dec[:, n, 0], wide(g_slot[:, s, mine]), four(const(f"incl{s % 2}")), ALU.mult), b_made)
                            link(g_.tensor_tensor(dec[:, n, 1], wide(b_slot[:, s, mine]), four(const(f"strict{s % 2}")), ALU.mult))
                    pool.wait_ge(d_free[f % 4], f // 4 + 1)
                    link(g_.tensor_tensor(dec[:, hb, 0], dec[:, hb, 0], four(const(f"incl{s % 2}")), ALU.mult))
                    say(g_.tensor_tensor(dec[:, hb, 1], dec[:, hb, 1], dec[:, hb, 0], ALU.mult), em_made)
                elif kind == "levw":
                    s, hb, l = a
                    b = (2 * s + hb) % 2
                    fk = D_FIRST[("decay", s, hb)] + 1
                    pool.wait_ge(d_free[fk % 4], fk // 4 + 1)
                    if l == 2:
                        fl = f_level(s, hb, 0)
                        pool.wait_ge(d_free[fl % 4], fl // 4 + 1)
                    if l >= 2:
                        pool.wait_ge(d_full, D_FIRST[("levw", s, hb, l - 2)] + 1)
                    elif s:
                        pool.wait_ge(d_full, D_FIRST[("levw", s - 1, hb, LEVELS - 2 + l)] + 1)
                    say(g_.tensor_tensor(nm[:, b, l % 2], nn[:, b], four(const(f"pair{l}")), ALU.mult), nm_made)
                elif kind == "uw":
                    s, hb = a
                    u = 2 * s + hb
                    b = u % 2
                    if u >= 2:
                        pool.wait_ge(d_full, D_FIRST[("uw",) + divmod(u - 2, 2)] + 1)
                    if s:
                        pool.wait_ge(d_full, D_FIRST[("scans", s - 1, hb)] + 1)
                    for hf, _, c in halves(s):
                        r = slice(64 * hf, 64 * hf + 64)
                        k3 = heads(dn_nat[r, 1, c // 2, 256 * hb:256 * hb + 256])
                        link(g_.tensor_tensor(kk[r, b], k3, wide(decay_of(0, s, hb, r)), ALU.mult))
                        ins = g_.tensor_tensor(ku[r, b], k3, wide(decay_of(1, s, hb, r)), ALU.mult)
                        if hf == 0:
                            link(ins)
                    say(ins, kk_made)
_INS = ["x", "mem", "rel_bias_table", "norm_mix_g", "w_in", "attn_q_norm_g", "attn_k_norm_g", "attn_sink",
        "dn_conv_w", "dn_a_log", "dn_dt_bias", "dn_out_norm_g", "mem_norm_g", "mem_w_kv", "mem_q_norm_g",
        "mem_k_norm_g", "w_br_attn", "w_br_dn", "w_br_mem", "w_out", "norm_ffn_g", "ffn_w_up", "ffn_conv_w",
        "ffn_conv_b", "ffn_w_down"]


def kernel(**inputs):
    import concourse.bacc as _bacc
    from concourse.bass_utils import run_bass_kernel_spmd as _run

    nc = _bacc.Bacc("TRN2", target_bir_lowering=False, num_devices=1)
    arrays, args = {}, {}
    for name in _INS + ["consts"]:
        a = CONSTS if name == "consts" else np.ascontiguousarray(inputs[name])
        arrays[f"in_{name}"] = a
        args[name] = nc.dram_tensor(f"in_{name}", a.shape, mybir.dt.from_np(a.dtype), kind="ExternalInput").ap()
    out = nc.dram_tensor("out_x", (1, SEQ, D), mybir.dt.float32, kind="ExternalOutput").ap()
    encoder_layer(nc, args, out)
    r = _run(nc, [arrays], core_ids=[0])
    return r.results[0]["out_x"]
```
